# Optimizing a Trainium2 kernel written in Bass

```python
import math
import jax, jax.numpy as jnp
from jax import lax
import numpy as np

D_MODEL = 1024
BATCH = 1
SEQ = 512
DEPTH = 2

HEAD_DIM = 64
A_GROUPS = ((128, 1), (512, 4), (2048, 16))
A_HEADS_PER_GROUP = 4
A_HEADS = A_HEADS_PER_GROUP * len(A_GROUPS)
A_WIDTH = A_HEADS * HEAD_DIM
B_HEADS = D_MODEL // HEAD_DIM
B_WIDTH = B_HEADS * HEAD_DIM
N_A = DEPTH // 2
N_B = DEPTH - N_A
D_FF = 2816
CONV_W = 3
ROPE_DIM = HEAD_DIM // 4
ROPE_THETA = 500000.0
BLK = 128
EPS = 1e-6
NEG = -1e30


def rms_norm(x, g):
    x32 = x.astype(jnp.float32)
    y = x32 * lax.rsqrt(jnp.mean(x32 * x32, axis=-1, keepdims=True) + EPS)
    return (y * g.astype(jnp.float32)).astype(x.dtype)

def rope_tables(T):
    pos = jnp.arange(T, dtype=jnp.float32)
    inv = ROPE_THETA ** (-jnp.arange(0, ROPE_DIM, 2, dtype=jnp.float32) / ROPE_DIM)
    ang = pos[:, None] * inv[None, :]
    return jnp.cos(ang), jnp.sin(ang)

def apply_rope(t, cos, sin):
    half = ROPE_DIM // 2
    c = cos[None, :, None, :].astype(t.dtype)
    s = sin[None, :, None, :].astype(t.dtype)
    x1 = t[..., :half]
    x2 = t[..., half:ROPE_DIM]
    return jnp.concatenate([x1 * c - x2 * s, x2 * c + x1 * s, t[..., ROPE_DIM:]], axis=-1)

def banded_attention(q, k, v, n_back):
    N, L, H, D = q.shape
    nb = L // BLK
    qb = q.reshape(N, nb, BLK, H, D)
    kb = k.reshape(N, nb, BLK, H, D)
    vb = v.reshape(N, nb, BLK, H, D)

    def with_prev(t):
        prev = jnp.pad(t[:, :-1], ((0, 0), (1, 0), (0, 0), (0, 0), (0, 0)))
        return jnp.concatenate([prev, t], axis=2)

    kc, vc = with_prev(kb), with_prev(vb)
    s = jnp.einsum('nbqhd,nbkhd->nbhqk', qb, kc).astype(jnp.float32) * (D ** -0.5)
    rel = (jnp.arange(BLK)[:, None] + BLK) - jnp.arange(2 * BLK)[None, :]
    band = (rel >= 0) & (rel <= n_back)
    has_prev = (jnp.arange(nb)[:, None, None] > 0) | (jnp.arange(2 * BLK)[None, None, :] >= BLK)
    mask = band[None] & has_prev
    s = jnp.where(mask[None, :, None], s, NEG)
    m = jnp.max(s, axis=-1, keepdims=True)
    p = jnp.exp(s - m)
    l = jnp.sum(p, axis=-1, keepdims=True)
    o = jnp.einsum('nbhqk,nbkhd->nbqhd', (p / l).astype(v.dtype), vc)
    lse = (m + jnp.log(l))[..., 0]
    return o.reshape(N, L, H, D), lse.transpose(0, 1, 3, 2).reshape(N, L, H)

def dilated_mixer(xn, w_qkv, w_o, cos, sin):
    B, T, _ = xn.shape
    qkv = xn @ w_qkv
    q, k, v = jnp.split(qkv, 3, axis=-1)
    q = apply_rope(q.reshape(B, T, A_HEADS, HEAD_DIM), cos, sin)
    k = apply_rope(k.reshape(B, T, A_HEADS, HEAD_DIM), cos, sin)
    v = v.reshape(B, T, A_HEADS, HEAD_DIM)
    G = A_HEADS_PER_GROUP
    outs, lses = [], []
    for g, (window, r) in enumerate(A_GROUPS):
        L = T // r
        Lp = -(-L // BLK) * BLK

        def gather(t):
            t = t[:, :, g * G:(g + 1) * G].reshape(B, L, r, G, HEAD_DIM)
            t = t.transpose(0, 2, 1, 3, 4).reshape(B * r, L, G, HEAD_DIM)
            return jnp.pad(t, ((0, 0), (0, Lp - L), (0, 0), (0, 0)))

        o, lse = banded_attention(gather(q), gather(k), gather(v), window // r)
        o = o[:, :L].reshape(B, r, L, G, HEAD_DIM).transpose(0, 2, 1, 3, 4).reshape(B, T, G, HEAD_DIM)
        lse = lse[:, :L].reshape(B, r, L, G).transpose(0, 2, 1, 3).reshape(B, T, G)
        outs.append(o)
        lses.append(lse)
    alpha = jax.nn.softmax(jnp.stack(lses, axis=0), axis=0)
    o = jnp.concatenate([outs[g] * alpha[g][..., None].astype(outs[g].dtype)
                         for g in range(len(A_GROUPS))], axis=2)
    return o.reshape(B, T, A_WIDTH) @ w_o

def fox_mixer(xn, w_q, w_o, k, v, c):
    B, T, _ = xn.shape
    q = (xn @ w_q).reshape(B, T, B_HEADS, HEAD_DIM)
    c_t = c.transpose(0, 2, 1)
    scale = HEAD_DIM ** -0.5
    outs = []
    for i in range(T // BLK):
        q0, q1 = i * BLK, (i + 1) * BLK
        s = jnp.einsum('bqhd,bkhd->bhqk', q[:, q0:q1], k[:, :q1]).astype(jnp.float32) * scale
        s = s + (c_t[:, :, q0:q1, None] - c_t[:, :, None, :q1])
        causal = jnp.arange(q0, q1)[:, None] >= jnp.arange(q1)[None, :]
        s = jnp.where(causal, s, NEG)
        p = jax.nn.softmax(s, axis=-1).astype(v.dtype)
        outs.append(jnp.einsum('bhqk,bkhd->bqhd', p, v[:, :q1]))
    o = jnp.concatenate(outs, axis=1)
    return o.reshape(B, T, B_WIDTH) @ w_o

def conv_ffn(xn, w_up, cw, cb, w_down):
    a = xn @ w_up
    T = a.shape[1]
    ap = jnp.pad(a, ((0, 0), (CONV_W - 1, 0), (0, 0)))
    a = sum(ap[:, j:j + T] * cw[j] for j in range(CONV_W)) + cb
    gate, val = jnp.split(a, 2, axis=-1)
    return (jax.nn.gelu(gate, approximate=True) * val) @ w_down

def first_inputs(seed: int = 0) -> dict:
    key = jax.random.key(seed)
    ks = jax.random.split(key, 14)

    def nrm(k, shape, fan_in):
        return jax.random.normal(k, shape, jnp.float32) * fan_in ** -0.5

    return {
        "x": jax.random.normal(ks[0], (BATCH, SEQ, D_MODEL), jnp.float32),
        "norm_gains": 1.0 + 0.05 * jax.random.normal(ks[1], (DEPTH, 4, D_MODEL), jnp.float32),
        "w_qkv_a": nrm(ks[2], (N_A, D_MODEL, 3 * A_WIDTH), D_MODEL),
        "w_o_a": nrm(ks[3], (N_A, A_WIDTH, D_MODEL), A_WIDTH),
        "w_q_b": nrm(ks[4], (N_B, D_MODEL, B_WIDTH), D_MODEL),
        "w_o_b": nrm(ks[5], (N_B, B_WIDTH, D_MODEL), B_WIDTH),
        "kv_norm": 1.0 + 0.05 * jax.random.normal(ks[6], (D_MODEL,), jnp.float32),
        "w_kvf": nrm(ks[7], (D_MODEL, 2 * B_WIDTH + B_HEADS), D_MODEL),
        "b_f": 3.0 + 0.5 * jax.random.normal(ks[8], (B_HEADS,), jnp.float32),
        "w_up": nrm(ks[9], (DEPTH, D_MODEL, 2 * D_FF), D_MODEL),
        "conv_w": nrm(ks[10], (DEPTH, CONV_W, 2 * D_FF), CONV_W),
        "conv_b": 0.01 * jax.random.normal(ks[11], (DEPTH, 2 * D_FF), jnp.float32),
        "w_down": nrm(ks[12], (DEPTH, D_FF, D_MODEL), D_FF),
    }

def first_block(x, norm_gains, w_qkv_a, w_o_a, w_q_b, w_o_b, kv_norm, w_kvf, b_f,
              w_up, conv_w, conv_b, w_down):
    B, T, _ = x.shape
    cos, sin = rope_tables(T)
    h = x
    k_sh = v_sh = c_sh = None
    for l in range(DEPTH):
        g = norm_gains[l]
        if l < N_A:
            mix = dilated_mixer(rms_norm(h, g[0]), w_qkv_a[l], w_o_a[l], cos, sin)
        else:
            if l == N_A:
                kvf = rms_norm(h, kv_norm) @ w_kvf
                k_sh = kvf[..., :B_WIDTH].reshape(B, T, B_HEADS, HEAD_DIM)
                v_sh = kvf[..., B_WIDTH:2 * B_WIDTH].reshape(B, T, B_HEADS, HEAD_DIM)
                log_f = jax.nn.log_sigmoid((kvf[..., 2 * B_WIDTH:] + b_f).astype(jnp.float32))
                c_sh = jnp.cumsum(log_f, axis=1)
            j = l - N_A
            mix = fox_mixer(rms_norm(h, g[0]), w_q_b[j], w_o_b[j], k_sh, v_sh, c_sh)
        h = h + rms_norm(mix, g[1])
        f = conv_ffn(rms_norm(h, g[2]), w_up[l], conv_w[l], conv_b[l], w_down[l])
        h = h + rms_norm(f, g[3])
    return h


DEPTH_2 = 1

CTX_LEN = 256
GRID_W = 64
N_MOD = 6
D_FF_2 = 4 * D_MODEL
CHUNK = 64
NORM_EPS = 1e-6

HY_C = D_MODEL // 4
HY_ORDER = 2
HY_SHORT = 3
HY_EMB = 33
HY_FH = 64
HY_DECAY_TARGET = 1e-2
HY_FAST_PCT = 0.3
HY_SLOW_PCT = 1.5

GLA_H = 4
GLA_VW = 3 * D_MODEL // 8
GLA_KW = GLA_VW // 2
GLA_DK = GLA_KW // GLA_H
GLA_DV = GLA_VW // GLA_H
GLA_RANK = 16
GLA_TAU = 16.0

GDN_H = 4
GDN_W = 3 * D_MODEL // 8
GDN_D = GDN_W // GDN_H
GDN_SHORT = 7

D_MIX = HY_C + GLA_VW + GDN_W
HY_IN = 3 * HY_C
GLA_IN = 2 * GLA_KW + 2 * GLA_VW + 2 * GLA_RANK
GDN_IN = 4 * GDN_W + 4 * GDN_H
IN_SIZES = (HY_IN, GLA_IN, GDN_IN)
N_IN = HY_IN + GLA_IN + GDN_IN


F32 = jnp.float32

def split_last(t, sizes):
    return jnp.split(t, np.cumsum(sizes)[:-1].tolist(), axis=-1)

def rmsnorm(x, g):
    xf = x.astype(F32)
    y = xf * lax.rsqrt(jnp.mean(xf * xf, axis=-1, keepdims=True) + NORM_EPS)
    return (y * g.astype(F32)).astype(x.dtype)

def modulate(x, g, shift, scale):
    return rmsnorm(x, g) * (1 + scale) + shift

def to_heads(t, n_heads):
    b, l, _ = t.shape
    return t.reshape(b, l, n_heads, -1).transpose(0, 2, 1, 3)

def from_heads(t):
    b, h, l, d = t.shape
    return t.transpose(0, 2, 1, 3).reshape(b, l, h * d)

def l2norm(t):
    return t * lax.rsqrt(jnp.sum(t * t, axis=-1, keepdims=True) + NORM_EPS)

def short_conv(u, w, n_seg, seg_len):
    b, l, ch = u.shape
    k = w.shape[0]
    us = u.reshape(b * n_seg, seg_len, ch)
    out = lax.conv_general_dilated(us, w[:, None, :].astype(u.dtype), window_strides=(1,),
                                   padding=[(k // 2, k // 2)], dimension_numbers=('NWC', 'WIO', 'NWC'),
                                   feature_group_count=ch)
    return out.reshape(b, l, ch)

def hyena_filters(length, w1, b1, w2, b2, w3, sin_freq):
    t = jnp.linspace(0.0, 1.0, length, dtype=F32)[:, None]
    bands = (HY_EMB - 1) // 2
    f = jnp.linspace(1e-4, bands - 1, bands, dtype=F32)
    w = 2 * math.pi * jnp.arange(length, dtype=F32) / length
    ang = w[:, None] * f[None, :]
    z = jnp.concatenate([t, jnp.cos(ang), -jnp.sin(ang)], axis=-1)
    h = jnp.sin(sin_freq[0].astype(F32) * (z @ w1.astype(F32) + b1.astype(F32)))
    h = jnp.sin(sin_freq[1].astype(F32) * (h @ w2.astype(F32) + b2.astype(F32)))
    h = (h @ w3.astype(F32)).reshape(length, HY_ORDER, 2, HY_C)
    deltas = jnp.abs(jnp.linspace(math.log(HY_DECAY_TARGET) / HY_SLOW_PCT,
                                  math.log(HY_DECAY_TARGET) / HY_FAST_PCT, HY_C, dtype=F32))
    h = h * jnp.exp(-t * deltas[None, :])[:, None, None, :]
    h_fwd, h_bwd = h[:, :, 0], h[:, :, 1]
    return jnp.concatenate([h_fwd, jnp.zeros_like(h_fwd[:1]), h_bwd[:0:-1]], axis=0)

def hyena_mix(z, n_seg, seg_len, conv_w, conv_b, filt, d_skip):
    u = (short_conv(z, conv_w, n_seg, seg_len) + conv_b).astype(F32)
    v, x1, x2 = jnp.split(u, 3, axis=-1)
    l = u.shape[1]
    filt_f = jnp.fft.rfft(filt, axis=0)
    y = v
    for o, gate in enumerate((x1, x2)):
        conv = jnp.fft.irfft(jnp.fft.rfft(y, n=2 * l, axis=1) * filt_f[None, :, o], n=2 * l, axis=1)[:, :l]
        y = gate * (conv + d_skip[o].astype(F32) * y)
    return y.astype(z.dtype)

def to_chunks(t, n):
    return jnp.moveaxis(t.reshape(t.shape[:2] + (n, CHUNK) + t.shape[3:]), 2, 0)

def from_chunks(t):
    t = jnp.moveaxis(t, 0, 2)
    return t.reshape(t.shape[:2] + (-1,) + t.shape[4:])

def gla_chunk_scan(q, k, v, log_a, s0):
    n = q.shape[2] // CHUNK
    mask = jnp.tril(jnp.ones((CHUNK, CHUNK), bool))[:, :, None]

    def step(s, xs):
        qc, kc, vc, ac = xs
        b = jnp.cumsum(ac, axis=2)
        diff = b[:, :, :, None, :] - b[:, :, None, :, :]
        decay = jnp.exp(jnp.where(mask, diff, -jnp.inf))
        attn = jnp.einsum('bhid,bhjd,bhijd->bhij', qc, kc, decay)
        o = jnp.einsum('bhid,bhde->bhie', qc * jnp.exp(b), s) + jnp.einsum('bhij,bhje->bhie', attn, vc)
        b_last = b[:, :, -1:, :]
        s_new = jnp.exp(b_last[:, :, 0, :])[..., None] * s + jnp.einsum(
            'bhjd,bhje->bhde', kc * jnp.exp(b_last - b), vc)
        return s_new, o

    s_fin, o = lax.scan(step, s0, (to_chunks(q, n), to_chunks(k, n), to_chunks(v, n), to_chunks(log_a, n)))
    return from_chunks(o), s_fin

def gdn_chunk_scan(q, k, v, g, beta, s0):
    n = q.shape[2] // CHUNK
    dk = q.shape[-1]
    strict = jnp.tril(jnp.ones((CHUNK, CHUNK), bool), -1)
    incl = jnp.tril(jnp.ones((CHUNK, CHUNK), bool))
    eye = jnp.eye(CHUNK, dtype=F32)

    def step(s, xs):
        qc, kc, vc, gc, bc = xs
        gcum = jnp.cumsum(gc, axis=-1)
        diff = gcum[..., :, None] - gcum[..., None, :]
        kb = kc * bc[..., None]
        a = -jnp.einsum('bhid,bhjd->bhij', kb, kc) * jnp.exp(jnp.where(strict, diff, -jnp.inf))
        rhs = jnp.concatenate([kb * jnp.exp(gcum)[..., None], vc * bc[..., None]], axis=-1)
        sol = lax.linalg.triangular_solve(eye - a, rhs, left_side=True, lower=True, unit_diagonal=True)
        w, u = sol[..., :dk], sol[..., dk:]
        v_new = u - w @ s
        attn = jnp.einsum('bhid,bhjd->bhij', qc, kc) * jnp.exp(jnp.where(incl, diff, -jnp.inf))
        o = (qc * jnp.exp(gcum)[..., None]) @ s + attn @ v_new
        g_last = gcum[..., -1:]
        s_new = jnp.exp(g_last)[..., None] * s + jnp.einsum(
            'bhjd,bhje->bhde', kc * jnp.exp(g_last - gcum)[..., None], v_new)
        return s_new, o

    s_fin, o = lax.scan(step, s0, (to_chunks(q, n), to_chunks(k, n), to_chunks(v, n),
                                   to_chunks(g, n), to_chunks(beta, n)))
    return from_chunks(o), s_fin

def bidir_scan(scan_fn, shared, fwd, bwd, s0_f, s0_b):
    o_f, s_f = scan_fn(*shared, *fwd, s0_f)
    flip = lambda a: jnp.flip(a, axis=2)
    o_b, s_b = scan_fn(*[flip(a) for a in shared], *[flip(a) for a in bwd], s0_b)
    return o_f + flip(o_b), s_f, s_b

def gated_head_norm(o, gate, g_norm):
    y = o * lax.rsqrt(jnp.mean(o * o, axis=-1, keepdims=True) + NORM_EPS) * g_norm.astype(F32)
    return from_heads(y) * jax.nn.silu(gate.astype(F32))

def gla_prep(z, w_a2, b_a):
    zf = z.astype(F32)
    q, k, v, gate, a_f, a_b = split_last(zf, (GLA_KW, GLA_KW, GLA_VW, GLA_VW, GLA_RANK, GLA_RANK))
    log_a = [to_heads(jax.nn.log_sigmoid(a @ w_a2[d].astype(F32) + b_a[d].astype(F32)) / GLA_TAU, GLA_H)
             for d, a in enumerate((a_f, a_b))]
    shared = (to_heads(q, GLA_H) * GLA_DK ** -0.5, to_heads(k, GLA_H), to_heads(v, GLA_H))
    return shared, (log_a[0],), (log_a[1],), gate

def gla_branch(z_lat, z_ctx, with_ctx_out, w_a2, b_a, norm_g):
    sh_c, fw_c, bw_c, gate_c = gla_prep(z_ctx, w_a2, b_a)
    s0 = jnp.zeros((z_ctx.shape[0], GLA_H, GLA_DK, GLA_DV), F32)
    o_c, s_f, s_b = bidir_scan(gla_chunk_scan, sh_c, fw_c, bw_c, s0, s0)
    sh_l, fw_l, bw_l, gate_l = gla_prep(z_lat, w_a2, b_a)
    o_l, _, _ = bidir_scan(gla_chunk_scan, sh_l, fw_l, bw_l, s_f, s_b)
    out_lat = gated_head_norm(o_l, gate_l, norm_g).astype(z_lat.dtype)
    out_ctx = gated_head_norm(o_c, gate_c, norm_g).astype(z_ctx.dtype) if with_ctx_out else None
    return out_lat, out_ctx

def gdn_prep(z, conv_w, a_log, dt_bias, n_seg, seg_len):
    qkv, gate, a_f, a_b, b_f, b_b = split_last(z, (3 * GDN_W, GDN_W, GDN_H, GDN_H, GDN_H, GDN_H))
    qkv = jax.nn.silu(short_conv(qkv, conv_w, n_seg, seg_len)).astype(F32)
    q, k, v = jnp.split(qkv, 3, axis=-1)
    shared = (l2norm(to_heads(q, GDN_H)) * GDN_D ** -0.5, l2norm(to_heads(k, GDN_H)), to_heads(v, GDN_H))

    def log_decay(a, d):
        return (-jnp.exp(a_log[d].astype(F32)) *
                jax.nn.softplus(a.astype(F32) + dt_bias[d].astype(F32))).transpose(0, 2, 1)

    def write_gate(b):
        return jax.nn.sigmoid(b.astype(F32)).transpose(0, 2, 1)

    return shared, (log_decay(a_f, 0), write_gate(b_f)), (log_decay(a_b, 1), write_gate(b_b)), gate

def gdn_branch(z_lat, z_ctx, rows, with_ctx_out, conv_w, a_log, dt_bias, norm_g):
    sh_c, fw_c, bw_c, gate_c = gdn_prep(z_ctx, conv_w, a_log, dt_bias, 1, z_ctx.shape[1])
    s0 = jnp.zeros((z_ctx.shape[0], GDN_H, GDN_D, GDN_D), F32)
    o_c, s_f, s_b = bidir_scan(gdn_chunk_scan, sh_c, fw_c, bw_c, s0, s0)
    sh_l, fw_l, bw_l, gate_l = gdn_prep(z_lat, conv_w, a_log, dt_bias, rows, GRID_W)
    o_l, _, _ = bidir_scan(gdn_chunk_scan, sh_l, fw_l, bw_l, s_f, s_b)
    out_lat = gated_head_norm(o_l, gate_l, norm_g).astype(z_lat.dtype)
    out_ctx = gated_head_norm(o_c, gate_c, norm_g).astype(z_ctx.dtype) if with_ctx_out else None
    return out_lat, out_ctx

def mixer(h, hc, rows, with_ctx_out, w_in, w_out, hy_conv_w, hy_conv_b, hy_filter, hy_d,
          gla_w_a2, gla_b_a, gla_norm_g, gdn_conv_w, gdn_a_log, gdn_dt_bias, gdn_norm_g):
    zl_hy, zl_gla, zl_gdn = split_last(h @ w_in, IN_SIZES)
    zc_hy, zc_gla, zc_gdn = split_last(hc @ w_in, IN_SIZES)
    hy_lat = hyena_mix(zl_hy, rows, GRID_W, hy_conv_w, hy_conv_b, hyena_filters(h.shape[1], *hy_filter), hy_d)
    gla_lat, gla_ctx = gla_branch(zl_gla, zc_gla, with_ctx_out, gla_w_a2, gla_b_a, gla_norm_g)
    gdn_lat, gdn_ctx = gdn_branch(zl_gdn, zc_gdn, rows, with_ctx_out, gdn_conv_w, gdn_a_log, gdn_dt_bias, gdn_norm_g)
    y_lat = jnp.concatenate([hy_lat, gla_lat, gdn_lat], axis=-1) @ w_out
    if not with_ctx_out:
        return y_lat, None
    hy_ctx = hyena_mix(zc_hy, 1, hc.shape[1], hy_conv_w, hy_conv_b, hyena_filters(hc.shape[1], *hy_filter), hy_d)
    y_ctx = jnp.concatenate([hy_ctx, gla_ctx, gdn_ctx], axis=-1) @ w_out
    return y_lat, y_ctx

def sq_relu_mlp(h, w1, w2):
    return jnp.square(jax.nn.relu(h @ w1)) @ w2

def second_inputs(seed: int = 0) -> dict:
    key = jax.random.key(seed)
    ks = iter(jax.random.split(key, 32))
    nrm = lambda shape, std: std * jax.random.normal(next(ks), shape, F32)
    dt = jnp.exp(jax.random.uniform(next(ks), (DEPTH_2, 2, GDN_H), F32, math.log(1e-3), math.log(1e-1)))
    return {
        'x': nrm((BATCH, SEQ, D_MODEL), 1.0),
        'c': nrm((BATCH, D_MODEL), 1.0),
        'ctx': nrm((BATCH, CTX_LEN, D_MODEL), 1.0),
        'c_ctx': nrm((D_MODEL,), 1.0),
        'norm1_g': 1.0 + nrm((DEPTH_2, D_MODEL), 0.05),
        'norm2_g': 1.0 + nrm((DEPTH_2, D_MODEL), 0.05),
        'w_mod': nrm((DEPTH_2, D_MODEL, N_MOD * D_MODEL), D_MODEL ** -0.5),
        'b_mod': nrm((DEPTH_2, N_MOD * D_MODEL), 0.02),
        'w_in': nrm((DEPTH_2, D_MODEL, N_IN), D_MODEL ** -0.5),
        'w_out': nrm((DEPTH_2, D_MIX, D_MODEL), D_MIX ** -0.5),
        'hy_conv_w': nrm((DEPTH_2, HY_SHORT, HY_IN), HY_SHORT ** -0.5),
        'hy_conv_b': nrm((DEPTH_2, HY_IN), 0.02),
        'hy_f_w1': nrm((DEPTH_2, HY_EMB, HY_FH), HY_EMB ** -0.5),
        'hy_f_b1': nrm((DEPTH_2, HY_FH), 0.02),
        'hy_f_w2': nrm((DEPTH_2, HY_FH, HY_FH), HY_FH ** -0.5),
        'hy_f_b2': nrm((DEPTH_2, HY_FH), 0.02),
        'hy_f_w3': nrm((DEPTH_2, HY_FH, HY_ORDER * 2 * HY_C), 0.05 * HY_FH ** -0.5),
        'hy_sin_freq': 1.0 + nrm((DEPTH_2, 2, HY_FH), 0.05),
        'hy_d': nrm((DEPTH_2, HY_ORDER, HY_C), 1.0),
        'gla_w_a2': nrm((DEPTH_2, 2, GLA_RANK, GLA_KW), GLA_RANK ** -0.5),
        'gla_b_a': nrm((DEPTH_2, 2, GLA_KW), 0.02),
        'gla_norm_g': 1.0 + nrm((DEPTH_2, GLA_DV), 0.05),
        'gdn_conv_w': nrm((DEPTH_2, GDN_SHORT, 3 * GDN_W), GDN_SHORT ** -0.5),
        'gdn_a_log': jnp.log(jax.random.uniform(next(ks), (DEPTH_2, 2, GDN_H), F32, 1.0, 16.0)),
        'gdn_dt_bias': dt + jnp.log(-jnp.expm1(-dt)),
        'gdn_norm_g': 1.0 + nrm((DEPTH_2, GDN_D), 0.05),
        'w_mlp1': nrm((DEPTH_2, D_MODEL, D_FF_2), D_MODEL ** -0.5),
        'w_mlp2': nrm((DEPTH_2, D_FF_2, D_MODEL), D_FF_2 ** -0.5),
        'final_norm_g': 1.0 + nrm((D_MODEL,), 0.05),
    }

def second_block(x, c, ctx, c_ctx, norm1_g, norm2_g, w_mod, b_mod, w_in, w_out, hy_conv_w, hy_conv_b,
              hy_f_w1, hy_f_b1, hy_f_w2, hy_f_b2, hy_f_w3, hy_sin_freq, hy_d, gla_w_a2, gla_b_a, gla_norm_g,
              gdn_conv_w, gdn_a_log, gdn_dt_bias, gdn_norm_g, w_mlp1, w_mlp2, final_norm_g):
    rows = x.shape[1] // GRID_W
    silu_c = jax.nn.silu(c)
    silu_cc = jax.nn.silu(c_ctx)
    for l in range(DEPTH_2):
        with_ctx_out = l < DEPTH_2 - 1
        sh1, sc1, g1, sh2, sc2, g2 = jnp.split((silu_c @ w_mod[l] + b_mod[l])[:, None, :], N_MOD, axis=-1)
        csh1, csc1, cg1, csh2, csc2, cg2 = jnp.split(silu_cc @ w_mod[l] + b_mod[l], N_MOD, axis=-1)
        h = modulate(x, norm1_g[l], sh1, sc1)
        hc = modulate(ctx, norm1_g[l], csh1, csc1)
        hy_filter = (hy_f_w1[l], hy_f_b1[l], hy_f_w2[l], hy_f_b2[l], hy_f_w3[l], hy_sin_freq[l])
        y, yc = mixer(h, hc, rows, with_ctx_out, w_in[l], w_out[l], hy_conv_w[l], hy_conv_b[l], hy_filter,
                      hy_d[l], gla_w_a2[l], gla_b_a[l], gla_norm_g[l], gdn_conv_w[l], gdn_a_log[l],
                      gdn_dt_bias[l], gdn_norm_g[l])
        x = x + g1 * y
        x = x + g2 * sq_relu_mlp(modulate(x, norm2_g[l], sh2, sc2), w_mlp1[l], w_mlp2[l])
        if with_ctx_out:
            ctx = ctx + cg1 * yc
            ctx = ctx + cg2 * sq_relu_mlp(modulate(ctx, norm2_g[l], csh2, csc2), w_mlp1[l], w_mlp2[l])
    return rmsnorm(x, final_norm_g)


def setup_inputs(seed=0):
    out = dict(first_inputs(seed))
    for name, value in second_inputs(seed + 1).items():
        if name != "x":
            out[name + "_2"] = value
    return out


def reference(
    x, norm_gains, w_qkv_a, w_o_a, w_q_b, w_o_b, kv_norm, w_kvf, b_f, w_up, conv_w, conv_b,
    w_down, c_2, ctx_2, c_ctx_2, norm1_g_2, norm2_g_2, w_mod_2, b_mod_2, w_in_2, w_out_2,
    hy_conv_w_2, hy_conv_b_2, hy_f_w1_2, hy_f_b1_2, hy_f_w2_2, hy_f_b2_2, hy_f_w3_2,
    hy_sin_freq_2, hy_d_2, gla_w_a2_2, gla_b_a_2, gla_norm_g_2, gdn_conv_w_2, gdn_a_log_2,
    gdn_dt_bias_2, gdn_norm_g_2, w_mlp1_2, w_mlp2_2, final_norm_g_2,
):
    x = first_block(
        x, norm_gains, w_qkv_a, w_o_a, w_q_b, w_o_b, kv_norm, w_kvf, b_f, w_up, conv_w, conv_b,
        w_down,
    )
    return second_block(
        x, c_2, ctx_2, c_ctx_2, norm1_g_2, norm2_g_2, w_mod_2, b_mod_2, w_in_2, w_out_2,
        hy_conv_w_2, hy_conv_b_2, hy_f_w1_2, hy_f_b1_2, hy_f_w2_2, hy_f_b2_2, hy_f_w3_2,
        hy_sin_freq_2, hy_d_2, gla_w_a2_2, gla_b_a_2, gla_norm_g_2, gdn_conv_w_2, gdn_a_log_2,
        gdn_dt_bias_2, gdn_norm_g_2, w_mlp1_2, w_mlp2_2, final_norm_g_2,
    )


_drawn_inputs = setup_inputs


def setup_inputs(seed=0):
    import zlib

    import numpy as np

    out = dict(_drawn_inputs(seed))
    spreads = {}
    factors = {'conv_b': 4.275,
     'norm2_g_2': 2.671,
     'hy_conv_b_2': 7.139,
     'hy_f_b1_2': 4.528,
     'hy_f_b2_2': 3.827,
     'hy_sin_freq_2': 5.667,
     'gla_b_a_2': 8.0,
     'gla_norm_g_2': 8.0,
     'gdn_norm_g_2': 7.644}
    for name, (base, spread) in spreads.items():
        noise = np.random.default_rng([zlib.crc32(name.encode()), seed]).standard_normal(out[name].shape)
        drawn = base * np.exp(spread * noise) if base else spread * noise
        out[name] = __import__('jax').numpy.asarray(drawn.astype(out[name].dtype))
    for name, factor in factors.items():
        out[name] = (out[name] * factor).astype(out[name].dtype)
    return out
```

```python
from contextlib import ExitStack
import math

import concourse.bass as bass
from concourse import mybir
import numpy as np

F32 = mybir.dt.float32
ALU = mybir.AluOpType
ACT = mybir.ActivationFunctionType
AX = mybir.AxisListType

P = 128
T = 512
TB = T // P
D = 1024
KD = D // P
HD = 64
A_GROUPS = 3
A_SLOTS = 4
A_W = A_GROUPS * A_SLOTS * HD
B_HEADS = 16
D_FF = 2816
KF = D_FF // P
EPS = 1e-6
NEG = -8e30
ROPE_DIM = 16
ROPE_THETA = 500000.0
CTX = 256
CB = CTX // P
TA = T + CTX
NBLK = TA // P
D_FF2 = 4096
KF2 = D_FF2 // P
N_MOD = 6
CH = 64
NCH, CCH = TA // CH, CTX // CH
HY_C = 256
HY_EMB, HY_FH = 33, 64
GH = 4
GLA_DK, GLA_DV, GLA_RANK = 48, 96, 16
GLA_TAU = 16.0
GDN_D = 96
GW = GH * GDN_D
GDN_TAPS = 7
NFREQ = T
AG = {"gla_f": 0, "gla_b": 32, "decay": 64, "beta": 96}
RING = 10
UNIT = 1024


def fm_units(w):
    k, f = w.shape
    blocks = w.reshape(k // P, P, f // P, P).transpose(2, 0, 1, 3).reshape(-1, 8, P, P)
    return blocks.transpose(0, 2, 1, 3).reshape(-1, P, UNIT)


def tm_units(w):
    n = w.shape[1]
    u = w.reshape(4, 2, P, n).transpose(0, 2, 1, 3).reshape(4, P, 2 * n)
    return np.concatenate([u, np.zeros((4, P, UNIT - 2 * n), w.dtype)], axis=2)


def pad_cols(w, groups, size):
    parts = []
    for n, width in enumerate(groups):
        parts += [w[:, n * size:(n + 1) * size], np.zeros((w.shape[0], width - size), w.dtype)]
    return np.concatenate(parts, axis=1)


def vec(v):
    return v.reshape(-1, P).T


def weight_list(i):
    wq = i["w_qkv_a"][0]
    wf = i["w_kvf"]
    out = [("a_qk", fm_units(wq[:, :2 * A_W])),
           ("a_v0", tm_units(wq[:, 2 * A_W:2 * A_W + 384])), ("a_v1", tm_units(wq[:, 2 * A_W + 384:])),
           ("a_o", fm_units(i["w_o_a"][0]))]

    def ffn(l):
        up = i["w_up"][l]
        pairs = np.concatenate([up[:, :D_FF].reshape(D, KF, 1, P), up[:, D_FF:].reshape(D, KF, 1, P)], axis=2)
        return [(f"up{l}", fm_units(pairs.reshape(D, 2 * D_FF))), (f"down{l}", fm_units(i["w_down"][l]))]

    out += ffn(0)
    out += [("b_q", fm_units(i["w_q_b"][0])), ("b_k", fm_units(wf[:, :D])),
            ("b_f", fm_units(pad_cols(wf[:, 2 * D:], [P], B_HEADS))),
            ("b_v0", tm_units(wf[:, D:D + 512])), ("b_v1", tm_units(wf[:, D + 512:2 * D])),
            ("b_o", fm_units(i["w_o_b"][0]))]
    out += ffn(1)
    out += [("mod", fm_units(i["w_mod_2"][0]))]
    w = i["w_in_2"][0]
    gl, gd = w[:, 3 * HY_C:3 * HY_C + 1184], w[:, 3 * HY_C + 1184:]
    kw = GH * GLA_DK
    ranks = gl[:, 2 * kw + 2 * GW:]
    gates = gd[:, 4 * GW:]
    ag = np.concatenate([pad_cols(ranks, [32, 32], GLA_RANK), pad_cols(gates, [32, 32], 2 * GH)], axis=1)
    out += [("hy", fm_units(w[:, :3 * HY_C])),
            ("ag", fm_units(ag)),
            ("gl_q", fm_units(pad_cols(gl[:, :kw], [64] * GH, GLA_DK))),
            ("gl_k", fm_units(pad_cols(gl[:, kw:2 * kw], [64] * GH, GLA_DK))),
            ("gl_v", tm_units(gl[:, 2 * kw:2 * kw + GW])),
            ("gl_g", tm_units(gl[:, 2 * kw + GW:2 * kw + 2 * GW])),
            ("gd_q", fm_units(pad_cols(gd[:, :GW], [P] * GH, GDN_D))),
            ("gd_k", fm_units(pad_cols(gd[:, GW:2 * GW], [P] * GH, GDN_D))),
            ("gd_v", fm_units(gd[:, 2 * GW:3 * GW])),
            ("gd_g", tm_units(gd[:, 3 * GW:4 * GW])),
            ("out2", fm_units(i["w_out_2"][0])),
            ("mlp1", fm_units(i["w_mlp1_2"][0])), ("mlp2", fm_units(i["w_mlp2_2"][0]))]
    return out


def small_list(i):
    g = i["norm_gains"]
    out = [(f"g{l}{n}", vec(g[l, n])) for l in range(2) for n in range(4)]
    out += [("kvg", vec(i["kv_norm"]))]
    for l in range(2):
        cw = i["conv_w"][l]
        pair = lambda v: v.reshape(2, KF, P).transpose(2, 1, 0).reshape(P, 2 * KF)
        out += [(f"cw{l}{j}", pair(cw[j])) for j in range(3)] + [(f"cb{l}", pair(i["conv_b"][l]))]
    out += [("b_f", np.concatenate([i["b_f"], np.zeros(P - B_HEADS, np.float32)]).reshape(P, 1))]
    both = lambda a, b: np.stack([a, b], axis=2).reshape(P, -1)
    bm = vec(i["b_mod_2"][0])
    out += [("c", both(vec(i["c_2"]), vec(i["c_ctx_2"]))), ("b_mod", both(bm, bm)),
            ("n1", vec(i["norm1_g_2"])), ("n2", vec(i["norm2_g_2"])), ("nf", vec(i["final_norm_g_2"]))]
    out += [(f"hyw{j}", vec(i["hy_conv_w_2"][0, j])) for j in range(3)]
    out += [("hyb", vec(i["hy_conv_b_2"])), ("hyd", vec(i["hy_d_2"]))]

    def rows(parts):
        col = np.zeros((P, 1), np.float32)
        for at, v in parts:
            col[at:at + v.size, 0] = v.ravel()
        return col
    out += [("gla_b", vec(pad_cols(i["gla_b_a_2"].reshape(1, -1), [64] * 8, GLA_DK)))]
    cw = i["gdn_conv_w_2"][0]
    for j in range(GDN_TAPS):
        qk = pad_cols(cw[j:j + 1, :2 * GW], [P] * 8, GDN_D)
        out.append((f"gdw{j}", vec(np.concatenate([qk, cw[j:j + 1, 2 * GW:]], axis=1))))
    out += [("a_log", rows([(AG["decay"], i["gdn_a_log_2"])])), ("dt", rows([(AG["decay"], i["gdn_dt_bias_2"])])),
            ("gla_ng", np.broadcast_to(i["gla_norm_g_2"], (P, GLA_DV))),
            ("gdn_ng", np.broadcast_to(i["gdn_norm_g_2"], (P, GDN_D))),
            ("fb1", rows([(0, i["hy_f_b1_2"])])), ("fb2", rows([(0, i["hy_f_b2_2"])])),
            ("fq1", rows([(0, i["hy_sin_freq_2"][0, 0])])), ("fq2", rows([(0, i["hy_sin_freq_2"][0, 1])]))]
    return out


def filter_weights(i):
    a = np.zeros((P, HY_FH + HY_FH + 4 * HY_C), np.float32)
    a[:HY_EMB, :HY_FH] = i["hy_f_w1_2"][0]
    a[:HY_FH, HY_FH:2 * HY_FH] = i["hy_f_w2_2"][0]
    a[:HY_FH, 2 * HY_FH:] = i["hy_f_w3_2"][0]
    g = np.zeros((P, 2 * P), np.float32)
    for d in range(2):
        g[32 * d:32 * d + GLA_RANK] = pad_cols(i["gla_w_a2_2"][0, d], [64] * GH, GLA_DK)
    return np.concatenate([a, g], axis=1)


def const_list():
    f = np.float32
    eye = np.eye(P, dtype=f)
    inv = f(ROPE_THETA) ** (-np.arange(0, ROPE_DIM, 2, dtype=f) / f(ROPE_DIM))
    ang = (np.arange(T, dtype=f)[:, None] * inv[None, :]).astype(np.float64).T
    c, s = np.ones((P, T)), np.zeros((P, T))
    perm = np.zeros((P, P), f)
    for h in (0, HD):
        c[h:h + 8], c[h + 8:h + 16] = np.cos(ang), np.cos(ang)
        s[h:h + 8], s[h + 8:h + 16] = -np.sin(ang), np.sin(ang)
        for d in range(8):
            perm[h + d, h + 8 + d] = perm[h + 8 + d, h + d] = 1.0
    q, k = np.arange(P)[:, None], np.arange(P)[None, :]
    causal = np.where(q >= k, 0.0, NEG)
    zero = np.zeros((P, P))
    window = np.concatenate([np.full((P, P), NEG)] * 2 + [np.where(k >= q, 0.0, NEG), causal], axis=1)
    masks = [window]
    for r in (4, 16):
        same = (q - k) % r == 0
        masks.append(np.concatenate([np.where(same, 0.0, NEG)] * 3 + [np.where(same & (q >= k), 0.0, NEG)], axis=1))
    fox = np.concatenate([zero] * 3 + [causal], axis=1)
    sel = np.zeros((P, B_HEADS, P))
    for h in range(B_HEADS):
        sel[h, h] = -8.0
    out = [("base", np.concatenate([eye, np.ones((P, P)), perm], axis=1)),
           ("mix_a", np.concatenate([c, s] + masks, axis=1)),
           ("mix_b", np.concatenate([fox, sel.reshape(P, -1)], axis=1))]
    n = np.arange(T)
    w = np.outer(n, 2 * np.arange(NFREQ) + 1) % (4 * T) * (np.pi / (2 * T))
    tiles = lambda a: a.reshape(-1, P, a.shape[1]).transpose(1, 0, 2).reshape(P, -1)
    out += [("dft", np.concatenate([tiles(m) for m in (np.cos(w), np.sin(w), np.cos(w).T / T, np.sin(w).T / T)], axis=1))]
    t = np.linspace(0.0, 1.0, T).astype(f)[:, None]
    bands = (HY_EMB - 1) // 2
    fr = np.linspace(1e-4, bands - 1, bands).astype(f)
    ang = ((f(2 * math.pi) * np.arange(T, dtype=f) / f(T))[:, None] * fr[None, :]).astype(f).astype(np.float64)
    z = np.concatenate([t, np.cos(ang), -np.sin(ang)], axis=1).T
    z = np.concatenate([z, np.zeros((P - HY_EMB, T))], axis=0)
    deltas = np.abs(np.linspace(math.log(1e-2) / 1.5, math.log(1e-2) / 0.3, HY_C)).astype(f)
    dec = np.exp(-(t * deltas[None, :]).astype(np.float64))
    back = dec.copy()
    back[0] = 0.0
    out += [("filt", np.concatenate([z, tiles(np.concatenate([dec, back], axis=1))], axis=1))]
    j, i = np.arange(P)[:, None], np.arange(P)[None, :]
    same = j // CH == i // CH
    m0 = [same & (i >= j), same & (i <= j)]
    reset = np.broadcast_to((np.arange(TA) % CH != 0).astype(f), (P, TA))
    fwd = np.zeros((P, 2))
    fwd[AG["decay"]:AG["decay"] + GH, 0] = 1
    fwd[AG["decay"] + GH:AG["decay"] + 2 * GH, 1] = 1
    sign = np.ones((P, 1))
    sign[AG["beta"]:] = -1
    out += [("gla", np.concatenate([m * 1.0 for m in m0] + [reset, fwd, sign], axis=1))]
    add = lambda m: np.where(m, 0.0, NEG)
    dm = []
    for d in range(2):
        later = (i > j) if d == 0 else (i < j)
        dm += [add(same & later), add(m0[d])]
    for d in range(2):
        m = 1
        while m < CH:
            pair = (i // (2 * m) == j // (2 * m)) & (i // m != j // m)
            dm.append((pair & ((i > j) if d == 0 else (i < j))) * 1.0)
            m *= 2
    sela, sell = np.zeros((P, 8, P)), np.zeros((P, 8, P))
    for r in range(8):
        sela[AG["decay"] + r, r] = 1
        sell[AG["decay"] + r, r] = sell[AG["beta"] + r, r] = 1
    out += [("gdn_m", np.concatenate(dm, axis=1)), ("gdn_s", np.concatenate([sela.reshape(P, -1), sell.reshape(P, -1)], axis=1))]
    return [(n, a.astype(f)) for n, a in out]


SHAPES = {
    "norm_gains": (2, 4, D), "w_qkv_a": (1, D, 3 * A_W), "w_o_a": (1, A_W, D), "w_q_b": (1, D, D),
    "w_o_b": (1, D, D), "kv_norm": (D,), "w_kvf": (D, 2 * D + B_HEADS), "b_f": (B_HEADS,),
    "w_up": (2, D, 2 * D_FF), "conv_w": (2, 3, 2 * D_FF), "conv_b": (2, 2 * D_FF), "w_down": (2, D_FF, D),
    "c_2": (1, D), "c_ctx_2": (D,), "norm1_g_2": (1, D), "norm2_g_2": (1, D), "w_mod_2": (1, D, N_MOD * D),
    "b_mod_2": (1, N_MOD * D), "w_in_2": (1, D, 3504), "w_out_2": (1, D, D), "hy_conv_w_2": (1, 3, 3 * HY_C),
    "hy_conv_b_2": (1, 3 * HY_C), "hy_f_b1_2": (1, HY_FH), "hy_f_b2_2": (1, HY_FH), "hy_sin_freq_2": (1, 2, HY_FH),
    "hy_d_2": (1, 2, HY_C), "gla_b_a_2": (1, 2, GH * GLA_DK), "gla_norm_g_2": (1, GLA_DV),
    "gdn_conv_w_2": (1, GDN_TAPS, 3 * GW), "gdn_a_log_2": (1, 2, GH), "gdn_dt_bias_2": (1, 2, GH),
    "gdn_norm_g_2": (1, GDN_D), "w_mlp1_2": (1, D, D_FF2), "w_mlp2_2": (1, D_FF2, D), "final_norm_g_2": (D,),
}


def starts(pairs, axis):
    at, out = 0, {}
    for name, a in pairs:
        out[name] = at
        at += a.shape[axis]
    return out, at


def places():
    z = {k: np.broadcast_to(np.float32(0), s) for k, s in SHAPES.items()}
    return starts(weight_list(z), 0), starts(small_list(z), 1), starts(const_list(), 1)


KA_ = A_W // P
SHARED = {
    "projected": [("a_qk", 2 * KA_), ("a_v", 2 * TB), ("a_ps", KD), ("ffn0_up", 2 * KF), ("ffn0_ps", KD), ("b_qk", 2 * KD),
                  ("b_f", 1), ("b_v", 2 * TB), ("b_ps", KD), ("ffn1_up", 2 * KF), ("ffn1_ps", KD), ("mod_ps", N_MOD * KD),
                  ("hy_ps", 6), ("ag_ps", 2), ("glq_ps", 2), ("glk_ps", 4), ("glv_ps", NBLK), ("glz_ps", 8),
                  ("gla_gps", TB), ("gd_ps", 18), ("gd_gps", TB), ("out2_ps", KD), ("mlp_up", KF2), ("mlp_ps", KD)],
    "turned": [("a_turned", 48), ("a_flip", KA_), ("b_turned", 64), ("b_flip", KD), ("y_turn", 2 * TB),
               ("gl_turn", NBLK), ("gla_flip", 3), ("gd_turn", 2 * NBLK), ("gd_gT", 1), ("gdh_flip", 3)],
    "scored": [("a_scores", 48), ("b_scores", 64), ("fl", 2), ("f_pos", 2 * TB), ("H_ps", 2 * TB), ("gl_s", 2 * TB),
               ("gd_ss", 12)],
    "weighted": [("a_values", 16), ("b_values", 64), ("U", 2 * TB), ("gl_o", TB)],
    "rotated": [("a_rot", 2 * KA_), ("conv", 4), ("gl_U", NCH)],
    "crossed": [("cx_sq_used", KD), ("gl_x", 2 * (NCH - CCH))],
    "copied": [("a_raw", 2 * KA_), ("a_vt", 2 * TB), ("a_fm", KA_), ("b_qkt", 2 * KD), ("b_vt", 2 * TB), ("b_fm", KD),
               ("H", 2 * TB), ("yT", 2 * TB), ("ag", 2), ("glq", 2), ("glk", 4), ("glv", NBLK), ("glkT", NBLK),
               ("gla_gate", TB), ("gla_cat", 3), ("gd_gate", TB), ("gd_tm", 2 * NBLK), ("gdh_cat", 3), ("mlp_relu", KF2)],
    "probs": [("a_probs", 48), ("b_probs", 64), ("fs", 2)],
    "pt_act": [("a_pt_act", 24), ("b_pt_act", 32)],
    "gelu": [("ffn0_gelu", KF), ("ffn1_gelu", KF)],
    "tap": [("ffn0_tap", 2 * KF), ("ffn1_tap", 2 * KF), ("hy_tap", 6), ("gd_tap", 18), ("mlp_x", KD)],
    "looked_up": [("b_ln", 1), ("exp_c", 1), ("cx_sd", 1), ("ea0", 1), ("ea", 1), ("gt_ln", 1), ("gla_ln", 1),
                  ("gla_esc", 1), ("gla_ep", 1), ("gla_en", 1), ("gla_sd", 1), ("gd_sd", 12), ("gd_es", 3), ("gdh_sd", 1)],
    "squared": [("cx_sq", KD), ("x2_lat", KD), ("x2_ctx", KD), ("gd_sq", 12)],
    "mixed": [("a_mix", KD), ("ffn0_mix", KD), ("b_mix", KD), ("ffn1_mix", KD)],
    "tmp": [("a_tmp", KD), ("ffn0_tmp", KD), ("b_tmp", KD), ("ffn1_tmp", KD)],
    "residual": [(st + "_h", KD) for st in ("a", "ffn0", "b", "ffn1", "out2", "mlp")],
    "masked": [("a_masked", 48), ("b_masked", 64), ("f_used", 2 * TB)],
    "pt_dve": [("a_pt_dve", 24), ("b_pt_dve", 32)],
    "rows": [("a_rows", 16), ("b_rows", 64), ("spec", 2 * TB), ("gl_in", TB)],
    "max": [("a_max", 16), ("b_max", 64), ("Y", 2 * TB), ("gl_A", TB)],
    "convolved": [("ffn0_conv", 2 * KF), ("ffn1_conv", 2 * KF), ("hy_u", 6), ("gd_conv", 18)],
    "ff": [("ffn0_ff", KF), ("ffn1_ff", KF), ("mlp_ff", KF2)],
    "normed": [(n, KD) for n in ("a_xn", "ffn0_xn", "b_xn", "b_xkv", "ffn1_xn", "x2a", "x2b", "mlp_a", "y")],
    "stepped": [("b_z", 1), ("b_absz", 1), ("b_c", 1), ("silu_c", 1), ("mod", 1), ("cx_var", 1), ("cx_rstd", 1),
                ("gt_abs", 1), ("gt", 1), ("gla_abs", 1), ("gla_diff", 1), ("gla_qk", 4), ("gla_ss", 1), ("gla_normed", 1),
                ("gd_tg", 1), ("gd_gl", 1), ("gdh_ss", 1), ("gdh_normed", 1)],
    "roped": [("a_rope", 2 * KA_), ("f_sum", 4 * TB), ("glz", 8), ("gd_rs", 12)],
    "scaled": [("a_rc", 2 * KA_), ("hy_y", 4), ("gd_normed", 12)],
}


def build(nc, x, ctx_x, weights, smalls, filt, consts, out, dump=None):
    (UNITS, n_units), (SM, n_small), (CO, n_const) = places()

    ctx = ExitStack()
    with ctx:
        def sb(name, cols, rows=P):
            return ctx.enter_context(nc.sbuf_tensor(name, [rows, cols], F32))

        sems = {}

        first = {}
        for shared, signals in SHARED.items():
            at = 0
            for name, total in signals:
                first[name] = (shared, at)
                at += total

        def sem(name):
            shared, _ = first.get(name, (name, 0))
            if shared not in sems:
                sems[shared] = ctx.enter_context(nc.semaphore(shared))
            return sems[shared]

        def after(name, count):
            return sem(name), first.get(name, (name, 0))[1] + count

        h = sb("h", KD * T)[:, :].rearrange("p (k t) -> p k t", k=KD)
        xn_all = sb("xn", KD * TA)
        xn = xn_all[:, 0:KD * T].rearrange("p (k t) -> p k t", k=KD)
        mix = sb("mix", KD * T)[:, :].rearrange("p (k t) -> p k t", k=KD)
        ring = sb("ring", RING * UNIT)[:, :].rearrange("p (s n) -> p s n", s=RING)
        small = sb("small", n_small)
        base = sb("base", 3 * P)
        cst = sb("cst", 2816)
        nb = sb("nb", 6 * T)[:, :].rearrange("p (k t) -> p k t", k=6)
        sq, tmp, rstd, var = nb[:, 0:2], nb[:, 2:4], nb[:, 4], nb[:, 5]
        stat = sb("stat", 64)
        BIG = 20992
        big = sb("big", BIG)
        ident, ones, perm = base[:, 0:P], base[:, P:2 * P], base[:, 2 * P:3 * P]
        bank = [ctx.enter_context(nc.psum_tensor(f"bank{b}", [P, 512], F32)) for b in range(8)]

        def part(a, k, n):
            assert a + k * n <= BIG
            return big[:, a:a + k * n].rearrange("p (k n) -> p k n", k=k)

        def gain(name, k=0):
            return small[:, SM[name] + k:SM[name] + k + 1]

        ring_full = [sem(f"ring_full{s}") for s in range(RING)]
        unit_used = {}
        loaded = sem("loaded")
        links = {}

        def link(eng, ins):
            s = sem(f"link_{eng.engine.name}" if hasattr(eng, "engine") else "link")
            links[s.name] = links.get(s.name, 0) + 1
            ins.then_inc(s, 1)
            eng.wait_ge(s, links[s.name])

        held = {}

        def grab(pe, b, reader, count):
            if b in held:
                pe.wait_ge(*held[b])
            held[b] = (reader, count)
            return bank[b]

        def take(pe, u):
            pe.wait_ge(ring_full[u % RING], 16 * (u // RING + 1))

        def fm_linear(pe, name, chunks, kt, rhs, full, read, then=None, full0=0, read0=0):
            u0 = UNITS[name]
            for f in range(chunks):
                ps = grab(pe, f % 4, *after(read, read0 + f + 1))
                for k in range(kt):
                    blk = f * kt + k
                    u, j = u0 + blk // 8, blk % 8
                    if j == 0:
                        take(pe, u)
                    mm = pe.matmul(ps[:, :], ring[:, u % RING, j * P:(j + 1) * P], rhs(k),
                                   start=(k == 0), stop=(k == kt - 1))
                    unit_used[u] = after(full, full0 + f + 1)
                mm.then_inc(sem(full), 1)
                if then and f:
                    then(f - 1)
            if then:
                then(chunks - 1)

        def tm_linear(pe, name, n, lhs, blocks, full, read, at=0, full0=0):
            u0 = UNITS[name]
            for i, tb in enumerate(blocks):
                ps = grab(pe, (at + i) % 4, *after(read, full0 + i + 1))
                for k in range(KD):
                    u, j = u0 + k // 2, k % 2
                    if i == 0 and j == 0:
                        take(pe, u)
                    mm = pe.matmul(ps[:, 0:n], lhs(k, tb), ring[:, u % RING, j * n:(j + 1) * n],
                                   start=(k == 0), stop=(k == KD - 1))
                    unit_used[u] = after(full, full0 + len(blocks))
                mm.then_inc(sem(full), 1)

        NORMS = ["in", "a", "an", "ffn0", "ffn0n", "b", "bn", "ffn1", "ffn1n", "out2n", "mlpn"]
        squared, summed = sem("norm_squared"), sem("norm_summed")
        var_ready, sd_ready, rstd_ready = sem("norm_var"), sem("norm_sd"), sem("norm_rstd")

        def squares(act, norm, src, ready, k):
            n = NORMS.index(norm) * KD + k
            act.wait_ge(*after(ready, 16 * (3 + KD) if ready == "loaded" else k + 1))
            if k >= 2:
                act.wait_ge(summed, n - 1)
            act.activation(sq[:, k % 2], src[:, k], ACT.Square).then_inc(squared, 1)

        def sum_squares(pe, norm, k):
            n = NORMS.index(norm)
            if k == 0:
                grab(pe, 7, rstd_ready, n + 1)
            pe.wait_ge(squared, n * KD + k + 1)
            pe.matmul(bank[7][:, :], ones, sq[:, k % 2], start=(k == 0), stop=(k == KD - 1)).then_inc(summed, 1)

        def rstd_var(dve, norm):
            n = NORMS.index(norm) + 1
            dve.wait_ge(summed, n * KD)
            dve.tensor_scalar(var, bank[7][:, :], 1.0 / D, EPS, ALU.mult, ALU.add).then_inc(var_ready, 1)

        def rstd_sqrt(act, norm):
            act.wait_ge(var_ready, NORMS.index(norm) + 1)
            act.activation(var, var, ACT.Sqrt).then_inc(sd_ready, 1)

        def rstd_recip(dve, norm):
            n = NORMS.index(norm) + 1
            dve.wait_ge(sd_ready, n)
            dve.reciprocal(rstd, var).then_inc(rstd_ready, 1)
            dve.wait_ge(rstd_ready, n)

        def apply_norm(dve, g, dst, ready):
            for k in range(KD):
                dve.scalar_tensor_tensor(out=dst[:, k], in0=h[:, k], scalar=gain(g, k), in1=rstd,
                                         op0=ALU.mult, op1=ALU.mult).then_inc(sem(ready), 1)

        def out_pe(pe, st, name, kt, rhs):
            fm_linear(pe, name, KD, kt, rhs, st + "_ps", st + "_mix",
                      then=lambda f: sum_squares(pe, st, f))
            for k in range(KD):
                sum_squares(pe, st + "n", k)

        def out_act(act, st):
            for k in range(KD):
                squares(act, st, mix, st + "_mix", k)
            rstd_sqrt(act, st)
            for k in range(KD):
                squares(act, st + "n", h, st + "_h", k)
            rstd_sqrt(act, st + "n")

        def out_dve(dve, st, g):
            for f in range(KD):
                dve.wait_ge(*after(st + "_ps", f + 1))
                dve.tensor_copy(mix[:, f], bank[f % 4][:, :]).then_inc(sem(st + "_mix"), 1)
            rstd_var(dve, st)
            rstd_recip(dve, st)
            dve.wait_ge(*after(st + "_mix", KD))
            for k in range(KD):
                if k >= 2:
                    dve.wait_ge(*after(st + "_h", k - 1))
                dve.scalar_tensor_tensor(out=tmp[:, k % 2], in0=mix[:, k], scalar=gain(g, k), in1=rstd,
                                         op0=ALU.mult, op1=ALU.mult).then_inc(sem(st + "_tmp"), 1)
            rstd_var(dve, st + "n")
            rstd_recip(dve, st + "n")
            dve.wait_ge(*after(st + "_h", KD))

        def out_pool(pool, st):
            for k in range(KD):
                pool.wait_ge(*after(st + "_tmp", k + 1))
                pool.tensor_tensor(h[:, k], h[:, k], tmp[:, k % 2], ALU.add).then_inc(sem(st + "_h"), 1)

        def fm_multi(pe, name, chunks, parts, full, read, blocks=KD):
            u0 = UNITS[name]
            for f in range(chunks):
                for p, (rhs, n) in enumerate(parts):
                    i = f * len(parts) + p
                    ps = grab(pe, i % 4, *after(read, i + 1))
                    take(pe, u0 + f)
                    for k in range(KD):
                        mm = pe.matmul(ps[:, 0:n], ring[:, (u0 + f) % RING, k * P:(k + 1) * P], rhs(k),
                                       start=(k == 0), stop=(k == KD - 1))
                    mm.then_inc(sem(full), 1)
                unit_used[u0 + f] = after(full, (f + 1) * len(parts))

        ff = part(0, KF, T)
        cv, ge = part(KF * T, 4, T), part((KF + 4) * T, 2, T)

        def ffn_pe(pe, l):
            st = f"ffn{l}"
            pe.wait_ge(*after(st + "_xn", KD))
            fm_linear(pe, f"up{l}", 2 * KF, KD, lambda k: xn[:, k], st + "_up", st + "_conv")
            pe.wait_ge(*after(st + "_ff", KF))
            out_pe(pe, st, f"down{l}", KF, lambda k: ff[:, k])

        def ffn_act(act, l):
            st = f"ffn{l}"
            for j in range(KF + 1):
                for i in (2 * j, 2 * j + 1):
                    if j < KF:
                        act.wait_ge(*after(st + "_up", i + 1))
                        if j >= 2:
                            act.wait_ge(*after(st + "_ff", j - 1))
                        act.activation(cv[:, i % 4], bank[i % 4][:, :], ACT.Identity, bias=gain(f"cb{l}", i),
                                       scale=gain(f"cw{l}2", i)).then_inc(sem(st + "_tap"), 1)
                if j >= 1:
                    act.wait_ge(*after(st + "_conv", 2 * j - 1))
                    if j >= 3:
                        act.wait_ge(*after(st + "_ff", j - 2))
                    act.activation(ge[:, (j - 1) % 2], cv[:, (2 * j - 2) % 4], ACT.Gelu_apprx_tanh)\
                       .then_inc(sem(st + "_gelu"), 1)
            out_act(act, st)

        def ffn_dve(dve, l, g):
            st = f"ffn{l}"
            for j in range(KF + 1):
                for i in (2 * j, 2 * j + 1):
                    if j < KF:
                        ps, c = bank[i % 4], cv[:, i % 4]
                        dve.wait_ge(*after(st + "_tap", i + 1))
                        link(dve, dve.scalar_tensor_tensor(
                            out=c[:, 1:T], in0=ps[:, 0:T - 1], scalar=gain(f"cw{l}1", i), in1=c[:, 1:T],
                            op0=ALU.mult, op1=ALU.add))
                        dve.scalar_tensor_tensor(
                            out=c[:, 2:T], in0=ps[:, 0:T - 2], scalar=gain(f"cw{l}0", i), in1=c[:, 2:T],
                            op0=ALU.mult, op1=ALU.add).then_inc(sem(st + "_conv"), 1)
                if j >= 1:
                    dve.wait_ge(*after(st + "_gelu", j))
                    dve.wait_ge(*after(st + "_conv", 2 * j))
                    dve.tensor_tensor(ff[:, j - 1], ge[:, (j - 1) % 2], cv[:, (2 * j - 1) % 4], ALU.mult)\
                       .then_inc(sem(st + "_ff"), 1)
            out_dve(dve, st, g)

        WK = 0

        def attention(st, tasks, G, qT, kT, vT, oT, masks, width, work, sel=None):
            Sb = big[:, work:work + 2 * G * T].rearrange("p (b g n) -> p b g n", b=2, g=G)
            PT = big[:, work + 2 * G * T:work + 4 * G * T].rearrange("p (b g n) -> p b g n", b=2, g=G)
            n = len(tasks)
            mx = lambda t: stat[:, 16 * (t % 4):16 * (t % 4) + G]
            nm = lambda t: stat[:, 16 * (t % 4) + 4:16 * (t % 4) + 5]
            ls = lambda t: stat[:, 16 * (t % 4) + 8:16 * (t % 4) + 8 + G]
            rl = lambda t: stat[:, 16 * (t % 4) + 12:16 * (t % 4) + 13]
            mm_ = lambda t: stat[:, 16 * (t % 4) + 13:16 * (t % 4) + 14]
            lsum = lambda t: stat[:, 16 * (t % 4) + 14:16 * (t % 4) + 15]
            on_act = lambda j: j % 2 == 0
            s = lambda x: sem(f"{st}_{x}")
            at = lambda x, count: after(f"{st}_{x}", count)

            def scores(pe, t):
                tb, heads = tasks[t]
                w = (tb + 1) * P
                for g, hd in enumerate(heads):
                    j = t * G + g
                    ps = grab(pe, j % 4, *at("masked", j + 1))
                    r = HD * (hd % 2)
                    mm = pe.matmul(ps[:, 0:w], qT[r:r + HD, hd // 2, tb * P:(tb + 1) * P],
                                   kT[r:r + HD, hd // 2, 0:w], start=True, stop=(sel is None))
                    if sel is not None:
                        mm = pe.matmul(ps[:, 0:w], sel[0][0:B_HEADS, hd], sel[1][0:B_HEADS, 0:w],
                                       start=False, stop=True)
                    mm.then_inc(s("scores"), 1)

            def turn(pe, t):
                tb, heads = tasks[t]
                for g in range(G):
                    j = t * G + g
                    ps = grab(pe, 4 + j % 2, *at("pt_act" if on_act(j) else "pt_dve", j // 2 + 1))
                    pe.wait_ge(*at("probs", j + 1))
                    for kb in range(tb + 1):
                        mm = pe.transpose(ps[:, kb * P:(kb + 1) * P], Sb[:, t % 2, g, kb * P:(kb + 1) * P], ident)
                    mm.then_inc(s("turned"), 1)

            def values(pe, t):
                tb, heads = tasks[t]
                ps = grab(pe, 6 + t % 2, *at("rows", t + 1))
                for g, hd in enumerate(heads):
                    j = t * G + g
                    if on_act(j):
                        pe.wait_ge(*at("pt_act", j // 2 + 1))
                    else:
                        pe.wait_ge(*at("pt_dve", j // 2 + 1))
                    for kb in range(tb + 1):
                        mm = pe.matmul(ps[:, g * HD:(g + 1) * HD], PT[:, t % 2, g, kb * P:(kb + 1) * P],
                                       vT[:, kb, hd * HD:(hd + 1) * HD], start=(kb == 0), stop=(kb == tb))
                mm.then_inc(s("values"), 1)

            def rows_pe(pe):
                scores(pe, 0)
                for t in range(n + 1):
                    if t + 1 < n:
                        scores(pe, t + 1)
                    if t < n:
                        turn(pe, t)
                    if t >= 1:
                        values(pe, t - 1)

            def take_pt(eng, t, act):
                tb, _ = tasks[t]
                for g in range(G):
                    j = t * G + g
                    if on_act(j) != act:
                        continue
                    eng.wait_ge(*at("turned", j + 1))
                    if t >= 2:
                        eng.wait_ge(*at("values", t - 1))
                    w = (tb + 1) * P
                    if act:
                        ins = eng.activation(PT[:, t % 2, g, 0:w], bank[4 + j % 2][:, 0:w], ACT.Copy)
                    else:
                        ins = eng.tensor_copy(PT[:, t % 2, g, 0:w], bank[4 + j % 2][:, 0:w])
                    ins.then_inc(s("pt_act" if act else "pt_dve"), 1)

            def rows_act(act):
                for t in range(-1, n):
                    if t + 1 < n:
                        tb, _ = tasks[t + 1]
                        act.wait_ge(*at("max", t + 2))
                        if t >= 3:
                            act.wait_ge(*at("rows", t - 2))
                        for g in range(G):
                            sbt = Sb[:, (t + 1) % 2, g, 0:(tb + 1) * P]
                            act.activation(sbt, sbt, ACT.Exp, bias=nm(t + 1), scale=HD ** -0.5,
                                           accum_out=ls(t + 1)[:, g:g + 1]).then_inc(s("probs"), 1)
                    if t >= 0:
                        take_pt(act, t, True)

            def row_max(dve, t):
                tb, _ = tasks[t]
                w = (tb + 1) * P
                for g in range(G):
                    j = t * G + g
                    dve.wait_ge(*at("scores", j + 1))
                    if t >= 2 and g == 0:
                        dve.wait_ge(*at("turned", (t - 1) * G))
                    dve.tensor_tensor_reduce(out=Sb[:, t % 2, g, 0:w], in0=bank[j % 4][:, 0:w],
                                                   in1=masks[:, g, T - w:T], scale=1.0, scalar=-3e38,
                                                   op0=ALU.add, op1=ALU.max, accum_out=mx(t)[:, g:g + 1])\
                       .then_inc(s("masked"), 1)
                dve.wait_ge(*at("masked", (t + 1) * G))
                m = mx(t)
                if G > 1:
                    link(dve, dve.tensor_reduce(mm_(t), mx(t), AX.X, ALU.max))
                    m = mm_(t)
                dve.tensor_scalar(nm(t), m, -(HD ** -0.5), None, ALU.mult).then_inc(s("max"), 1)

            def row_out(dve, t):
                tb, heads = tasks[t]
                dve.wait_ge(*at("probs", (t + 1) * G))
                tot = ls(t)
                if G > 1:
                    link(dve, dve.tensor_reduce(lsum(t), ls(t), AX.X, ALU.add))
                    tot = lsum(t)
                link(dve, dve.reciprocal(rl(t), tot))
                dve.wait_ge(*at("values", t + 1))
                dst = oT[:, tb].rearrange("p (g c) -> p g c", g=G)[:, :, (heads[0] * HD):(heads[0] + 1) * HD]
                dve.tensor_scalar(dst, bank[6 + t % 2][:, 0:G * HD].rearrange("p (g c) -> p g c", g=G),
                                  rl(t), None, ALU.mult).then_inc(s("rows"), 1)

            def rows_dve(dve):
                row_max(dve, 0)
                for t in range(n + 1):
                    if t + 1 < n:
                        row_max(dve, t + 1)
                    if t < n:
                        take_pt(dve, t, False)
                    if t >= 1:
                        row_out(dve, t - 1)
            return rows_pe, rows_act, rows_dve, n

        def flip_pe(pe, st, src, chunks, ready, count):
            pe.wait_ge(*after(ready, count))
            for c in range(chunks):
                ps = grab(pe, 4 + c % 2, *after(st + "_fm", c + 1))
                for tb in range(TB):
                    mm = pe.transpose(ps[:, tb * P:(tb + 1) * P], src[:, tb, c * P:(c + 1) * P], ident)
                mm.then_inc(sem(st + "_flip"), 1)

        def flip_act(act, st, dst, chunks):
            for c in range(chunks):
                act.wait_ge(*after(st + "_flip", c + 1))
                act.activation(dst[:, c], bank[4 + c % 2][:, :], ACT.Copy).then_inc(sem(st + "_fm"), 1)

        KA = A_W // P
        a_q, a_k = part(0, KA, T), part(KA * T, KA, T)
        a_v = part(2 * KA * T, TB, A_W)
        a_o = part(2 * KA * T + TB * A_W, TB, A_W)
        a_work = 2 * KA * T + 2 * TB * A_W
        rope_c, rope_s = cst[:, 0:T], cst[:, T:2 * T]
        a_masks = cst[:, 2 * T:5 * T].rearrange("p (g n) -> p g n", g=3)
        a_tasks = [(tb, [g * A_SLOTS + s for g in range(A_GROUPS)]) for tb in range(TB) for s in range(A_SLOTS)]
        a_pe, a_act, a_dve, a_n = attention("a", a_tasks, A_GROUPS, a_q, a_k, a_v, a_o, a_masks, T, a_work)
        oT = xn

        def mixa_pe(pe):
            pe.wait_ge(loaded, 16 * (3 + KD))
            for k in range(KD):
                sum_squares(pe, "in", k)
            pe.wait_ge(*after("a_xn", KD))
            turned = [0]

            def rotate(f):
                ps = grab(pe, 4 + f % 2, *after("a_rope", f + 1))
                pe.wait_ge(*after("a_raw", f + 1))
                pe.matmul(ps[:, :], perm, nb[:, f % 2], start=True, stop=True).then_inc(sem("a_rot"), 1)
            fm_linear(pe, "a_qk", 2 * KA, KD, lambda k: xn[:, k], "a_qk", "a_raw", then=rotate)
            for n in range(2):
                tm_linear(pe, f"a_v{n}", 384, lambda k, tb: xn[:, k, tb * P:(tb + 1) * P], range(TB), "a_v",
                          "a_vt", full0=n * TB)
            pe.wait_ge(*after("a_rope", 2 * KA))
            pe.wait_ge(*after("a_vt", 2 * TB))
            a_pe(pe)
            flip_pe(pe, "a", a_o, KA, "a_rows", a_n)
            pe.wait_ge(*after("a_fm", KA))
            out_pe(pe, "a", "a_o", KA, lambda k: oT[:, k])

        def mixa_act(act):
            for k in range(KD):
                squares(act, "in", h, "loaded", k)
            rstd_sqrt(act, "in")
            for f in range(2 * KA):
                act.wait_ge(*after("a_qk", f + 1))
                if f >= 2:
                    act.wait_ge(*after("a_rope", f - 1))
                else:
                    act.wait_ge(summed, KD)
                act.activation(nb[:, f % 2], bank[f % 4][:, :], ACT.Copy).then_inc(sem("a_raw"), 1)
            for i in range(2 * TB):
                act.wait_ge(*after("a_v", i + 1))
                act.activation(a_v[:, i % TB, (i // TB) * 384:(i // TB + 1) * 384], bank[i % 4][:, 0:384],
                               ACT.Copy).then_inc(sem("a_vt"), 1)
            a_act(act)
            flip_act(act, "a", oT, KA)
            out_act(act, "a")

        def mixa_dve(dve):
            dve.wait_ge(loaded, 16 * (3 + KD))
            rstd_var(dve, "in")
            rstd_recip(dve, "in")
            apply_norm(dve, "g00", xn, "a_xn")
            for f in range(2 * KA):
                dst = a_q[:, f] if f < KA else a_k[:, f - KA]
                dve.wait_ge(*after("a_raw", f + 1))
                dve.tensor_tensor(dst, nb[:, f % 2], rope_c, ALU.mult).then_inc(sem("a_rc"), 1)
                dve.wait_ge(*after("a_rot", f + 1))
                link(dve, dve.tensor_tensor(tmp[:, f % 2], bank[4 + f % 2][:, :], rope_s, ALU.mult))
                dve.wait_ge(*after("a_rc", f + 1))
                dve.tensor_tensor(dst, dst, tmp[:, f % 2], ALU.add).then_inc(sem("a_rope"), 1)
            a_dve(dve)
            out_dve(dve, "a", "g01")
            apply_norm(dve, "g02", xn, "ffn0_xn")

        b_q, b_k = part(0, KD, T), part(KD * T, KD, T)
        b_v, b_o = part(2 * KD * T, TB, D), part(2 * KD * T + TB * D, TB, D)
        b_work = 2 * KD * T + 2 * TB * D
        b_mask = cst[:, 0:T].rearrange("p (g n) -> p g n", g=1)
        b_sel = cst[:, T:T + B_HEADS * P].rearrange("p (h n) -> p h n", h=B_HEADS)
        b_c = nb[:, 2]
        b_tasks = [(tb, [hd]) for tb in range(TB) for hd in range(B_HEADS)]
        b_pe, b_act, b_dve, b_n = attention("b", b_tasks, 1, b_q, b_k, b_v, b_o, b_mask, T, b_work, sel=(b_sel, b_c))
        xkv = mix

        def mixb_pe(pe):
            pe.wait_ge(loaded, 16 * (4 + KD))
            pe.wait_ge(*after("b_xn", KD))
            fm_linear(pe, "b_q", KD, KD, lambda k: xn[:, k], "b_qk", "b_qkt")
            pe.wait_ge(*after("b_xkv", KD))
            fm_linear(pe, "b_k", KD, KD, lambda k: xkv[:, k], "b_qk", "b_qkt", full0=KD, read0=KD)
            fm_linear(pe, "b_f", 1, KD, lambda k: xkv[:, k], "b_f", "b_z")
            for n in range(2):
                tm_linear(pe, f"b_v{n}", 512, lambda k, tb: xkv[:, k, tb * P:(tb + 1) * P], range(TB), "b_v",
                          "b_vt", at=1, full0=n * TB)
            pe.wait_ge(*after("b_qkt", 2 * KD))
            pe.wait_ge(*after("b_vt", 2 * TB))
            pe.wait_ge(*after("b_c", 1))
            b_pe(pe)
            flip_pe(pe, "b", b_o, KD, "b_rows", b_n)
            pe.wait_ge(*after("b_fm", KD))
            out_pe(pe, "b", "b_o", KD, lambda k: oT[:, k])

        def mixb_act(act):
            for f in range(2 * KD):
                act.wait_ge(*after("b_qk", f + 1))
                dst = b_q[:, f] if f < KD else b_k[:, f - KD]
                act.activation(dst, bank[f % 4][:, :], ACT.Copy).then_inc(sem("b_qkt"), 1)
            act.wait_ge(*after("b_absz", 1))
            z = nb[0:B_HEADS, 3]
            link(act, act.activation(z, z, ACT.Exp, scale=-1.0))
            act.activation(z, z, ACT.Ln, bias=1.0).then_inc(sem("b_ln"), 1)
            for i in range(2 * TB):
                act.wait_ge(*after("b_v", i + 1))
                b = (1 + i) % 4
                act.activation(b_v[:, i % TB, (i // TB) * 512:(i // TB + 1) * 512], bank[b][:, :], ACT.Copy)\
                   .then_inc(sem("b_vt"), 1)
            b_act(act)
            flip_act(act, "b", oT, KD)
            out_act(act, "b")

        def mixb_dve(dve):
            apply_norm(dve, "g10", xn, "b_xn")
            apply_norm(dve, "kvg", xkv, "b_xkv")
            z, az, one = nb[0:B_HEADS, 2], nb[0:B_HEADS, 3], nb[0:B_HEADS, 4]
            dve.wait_ge(*after("b_f", 1))
            dve.tensor_scalar(z, bank[0][0:B_HEADS, :], small[0:B_HEADS, SM["b_f"]:SM["b_f"] + 1], None, ALU.add)\
               .then_inc(sem("b_z"), 1)
            dve.wait_ge(*after("b_z", 1))
            dve.scalar_tensor_tensor(out=az, in0=z, scalar=-1.0, in1=z, op0=ALU.mult, op1=ALU.max).then_inc(sem("b_absz"), 1)
            dve.wait_ge(*after("b_absz", 1))
            link(dve, dve.tensor_scalar(z, z, 0.0, None, ALU.min))
            dve.wait_ge(*after("b_xkv", KD))
            link(dve, dve.memset(one, 1.0))
            dve.wait_ge(*after("b_ln", 1))
            link(dve, dve.tensor_tensor(az, z, az, ALU.subtract))
            dve.tensor_tensor_scan(z, one, az, 0.0, ALU.mult, ALU.add).then_inc(sem("b_c"), 1)
            b_dve(dve)
            out_dve(dve, "b", "g11")
            apply_norm(dve, "g12", xn, "ffn1_xn")

        X2 = xn_all[:, :].rearrange("p (k t) -> p k t", k=KD)
        vecs = sb("vecs", 208)
        silu_c, mod = vecs[:, 0:2 * KD], vecs[:, 2 * KD:2 * KD + 2 * N_MOD * KD]
        G1l, G1c, G2 = (vecs[:, 112 + 8 * n:120 + 8 * n] for n in range(3))
        mods = mod.rearrange("p (m k j) -> p m k j", m=N_MOD, k=KD)
        cx = part(16384, KD, CTX)
        lat = (lambda k: X2[:, k, CTX:TA], T)
        ctxp = (lambda k: X2[:, k, 0:CTX], CTX)

        def column(v, k):
            return v[:, k:k + 1]

        def small_cols(name, n):
            return small[:, SM[name]:SM[name] + n]

        def mod_pe(pe):
            pe.wait_ge(*after("silu_c", 1))
            ps = grab(pe, 0, *after("mod", 1))
            for f in range(N_MOD * KD):
                u = UNITS["mod"] + f
                take(pe, u)
                for k in range(KD):
                    mm = pe.matmul(ps[:, 2 * f:2 * f + 2], ring[:, u % RING, k * P:(k + 1) * P],
                                   silu_c[:, 2 * k:2 * k + 2], start=(k == 0), stop=(k == KD - 1))
                mm.then_inc(sem("mod_ps"), 1)
                unit_used[u] = after("mod_ps", f + 1)
            grab(pe, 7, *after("cx_rstd", 1))
            for k in range(KD):
                pe.wait_ge(*after("cx_sq", k + 1))
                pe.matmul(bank[7][:, 0:CTX], ones, sq[:, k % 2, 0:CTX], start=(k == 0), stop=(k == KD - 1))\
                  .then_inc(sem("cx_sq_used"), 1)
            pe.wait_ge(*after("x2_lat", KD))
            pe.wait_ge(*after("x2_ctx", KD))

        def mod_act(act):
            act.wait_ge(loaded, 16 * (4 + KD))
            act.activation(silu_c, small_cols("c", 2 * KD), ACT.Exp, scale=-1.0).then_inc(sem("exp_c"), 1)
            act.wait_ge(*after("cx_in", 16))
            for k in range(KD):
                if k >= 2:
                    act.wait_ge(*after("cx_sq_used", k - 1))
                act.activation(sq[:, k % 2, 0:CTX], cx[:, k], ACT.Square).then_inc(sem("cx_sq"), 1)
            act.wait_ge(*after("cx_var", 1))
            act.activation(var[:, 0:CTX], var[:, 0:CTX], ACT.Sqrt).then_inc(sem("cx_sd"), 1)
            for k in range(KD):
                act.wait_ge(*after("x2a", k + 1))
                act.activation(X2[:, k, CTX:TA], X2[:, k, CTX:TA], ACT.Identity, bias=mods[:, 0, k, 0:1])\
                   .then_inc(sem("x2_lat"), 1)
            for k in range(KD):
                act.wait_ge(*after("x2b", k + 1))
                act.activation(X2[:, k, 0:CTX], X2[:, k, 0:CTX], ACT.Identity, bias=mods[:, 0, k, 1:2])\
                   .then_inc(sem("x2_ctx"), 1)

        def mod_dve(dve):
            dve.wait_ge(*after("exp_c", 1))
            link(dve, dve.tensor_scalar(silu_c, silu_c, 1.0, None, ALU.add))
            link(dve, dve.reciprocal(silu_c, silu_c))
            dve.tensor_tensor(silu_c, silu_c, small_cols("c", 2 * KD), ALU.mult).then_inc(sem("silu_c"), 1)
            dve.wait_ge(*after("mod_ps", N_MOD * KD))
            dve.tensor_tensor(mod, bank[0][:, 0:2 * N_MOD * KD], small_cols("b_mod", 2 * N_MOD * KD), ALU.add)\
               .then_inc(sem("mod"), 1)
            dve.wait_ge(*after("mod", 1))
            for dst, m, j, g in ((G1l, 1, 0, "n1"), (G1c, 1, 1, "n1"), (G2, 4, 0, "n2")):
                ins = dve.scalar_tensor_tensor(out=dst, in0=mods[:, m, :, j], scalar=1.0, in1=small_cols(g, KD),
                                               op0=ALU.add, op1=ALU.mult)
            link(dve, ins)
            for k in range(KD):
                dve.scalar_tensor_tensor(out=X2[:, k, CTX:TA], in0=h[:, k], scalar=column(G1l, k), in1=rstd,
                                         op0=ALU.mult, op1=ALU.mult).then_inc(sem("x2a"), 1)
            dve.wait_ge(*after("cx_sq_used", KD))
            dve.wait_ge(*after("x2a", KD))
            dve.tensor_scalar(var[:, 0:CTX], bank[7][:, 0:CTX], 1.0 / D, EPS, ALU.mult, ALU.add).then_inc(sem("cx_var"), 1)
            dve.wait_ge(*after("cx_sd", 1))
            dve.reciprocal(rstd[:, 0:CTX], var[:, 0:CTX]).then_inc(sem("cx_rstd"), 1)
            dve.wait_ge(*after("cx_rstd", 1))
            for k in range(KD):
                dve.scalar_tensor_tensor(out=X2[:, k, 0:CTX], in0=cx[:, k], scalar=column(G1c, k), in1=rstd[:, 0:CTX],
                                         op0=ALU.mult, op1=ALU.mult).then_inc(sem("x2b"), 1)

        dft = [part(2048 * n, TB, T) for n in range(4)]
        zT, dec = big[:, 8192:8192 + T], part(8192 + T, TB, 2 * HY_C)
        fw = big[:, 10752:10752 + 1152]
        hsum, hdif = part(12288, TB, T), part(12288 + 2048, TB, T)
        Hc, Hs = part(16384, TB, T), part(16384 + 2048, TB, T)
        u_hy = part(8192, 6, T)
        yT = part(12288, TB, HY_C)
        Yc, Ys = part(13312, TB, HY_C), part(14336, TB, HY_C)
        sp = part(15360, 4, HY_C)
        grid = lambda a: a.rearrange("p (r c) -> p r c", c=CH)
        TWO_PI = 2 * math.pi
        C1 = 6.28125
        C2 = float(np.float32(TWO_PI - C1) // np.float32(2.0 ** -17) * np.float32(2.0 ** -17))
        C3 = TWO_PI - C1 - C2
        MAGIC = 1.5 * 2.0 ** 23
        PI_F = 3.1415925

        def hyena_pe(pe):
            pe.wait_ge(*after("filt_in", 48))
            pe.wait_ge(*after("x2b", KD))
            ps = grab(pe, 4, *after("fa", 1))
            pe.matmul(ps[0:HY_FH, :], fw[0:HY_EMB, 0:HY_FH], zT[0:HY_EMB, :], start=True, stop=True).then_inc(sem("fl"), 1)
            pe.wait_ge(*after("fs", 1))
            ps = grab(pe, 5, *after("fa", 2))
            pe.matmul(ps[0:HY_FH, :], fw[0:HY_FH, HY_FH:2 * HY_FH], nb[0:HY_FH, 0], start=True, stop=True)\
              .then_inc(sem("fl"), 1)
            pe.wait_ge(*after("fs", 2))
            for i in range(2 * TB):
                pt, o = divmod(i, 2)
                ps = grab(pe, 4 + i % 2, *after("f_used", i + 1))
                pe.matmul(ps[:, :], nb[0:HY_FH, 1, pt * P:(pt + 1) * P], fw[0:HY_FH, 128 + o * T:128 + (o + 1) * T],
                          start=True, stop=True).then_inc(sem("f_pos"), 1)
            pe.wait_ge(*after("f_sum", 4 * TB))
            for i in range(2 * TB):
                ft, c = divmod(i, 2)
                ps = grab(pe, i % 4, *after("H", i + 1))
                for pt in range(TB):
                    mm = pe.matmul(ps[:, :], dft[c][:, pt, ft * P:(ft + 1) * P], (hsum, hdif)[c][:, pt],
                                   start=(pt == 0), stop=(pt == TB - 1))
                mm.then_inc(sem("H_ps"), 1)
            fm_multi(pe, "hy", 6, [lat], "hy_ps", "hy_u")
            for o in range(2):
                pe.wait_ge(*after("hy_y" if o else "hy_u", 2 if o else 6))
                for tb in range(TB):
                    ps = grab(pe, 4 + tb % 2, *after("yT", o * TB + tb + 1))
                    for c in range(2):
                        mm = pe.transpose(ps[:, c * P:(c + 1) * P], u_hy[:, c, tb * P:(tb + 1) * P], ident)
                    mm.then_inc(sem("y_turn"), 1)
                pe.wait_ge(*after("yT", (o + 1) * TB))
                pe.wait_ge(*after("H", 2 * TB))
                for ft in range(TB):
                    ps = grab(pe, ft, *after("spec", o * TB + ft + 1))
                    for c in range(2):
                        for tb in range(TB):
                            mm = pe.matmul(ps[:, c * HY_C:(c + 1) * HY_C], dft[c][:, tb, ft * P:(ft + 1) * P], yT[:, tb],
                                           start=(tb == 0), stop=(tb == TB - 1))
                    mm.then_inc(sem("U"), 1)
                pe.wait_ge(*after("Y", (o + 1) * TB))
                for m in range(2):
                    ps = grab(pe, 4 + m, *after("hy_y", 2 * o + m + 1))
                    for ft in range(TB):
                        for c in range(2):
                            mm = pe.matmul(ps[:, :], (Yc, Ys)[c][:, ft, m * P:(m + 1) * P], dft[2 + c][:, ft],
                                           start=(ft == 0 and c == 0), stop=(ft == TB - 1 and c == 1))
                    mm.then_inc(sem("conv"), 1)

        def hyena_act(act):
            for n in range(2):
                act.wait_ge(*after("f_arg", n + 1))
                act.activation(nb[0:HY_FH, n], nb[0:HY_FH, 2], ACT.Sin).then_inc(sem("fs"), 1)
            for i in range(2 * TB):
                act.wait_ge(*after("H_ps", i + 1))
                act.activation((Hc, Hs)[i % 2][:, i // 2], bank[i % 4][:, :], ACT.Copy).then_inc(sem("H"), 1)
            for f in range(6):
                act.wait_ge(*after("hy_ps", f + 1))
                if f == 0:
                    act.wait_ge(*after("H_ps", 2 * TB))
                act.activation(u_hy[:, f], bank[f % 4][:, :], ACT.Identity, bias=gain("hyb", f), scale=gain("hyw1", f))\
                   .then_inc(sem("hy_tap"), 1)
            for i in range(2 * TB):
                act.wait_ge(*after("y_turn", i + 1))
                act.activation(yT[:, i % TB], bank[4 + i % 2][:, 0:HY_C], ACT.Copy).then_inc(sem("yT"), 1)

        def hyena_dve(dve):
            w, m = nb[0:HY_FH, 2], nb[0:HY_FH, 3]
            dve.wait_ge(*after("x2_ctx", KD))
            for n in range(2):
                dve.wait_ge(*after("fl", n + 1))
                if n:
                    dve.wait_ge(*after("fs", 1))
                dve.tensor_scalar(w, bank[4 + n][0:HY_FH, :], gain(f"fb{n + 1}")[0:HY_FH], gain(f"fq{n + 1}")[0:HY_FH],
                                  ALU.add, ALU.mult).then_inc(sem("fa"), 1)
                dve.wait_ge(*after("fa", n + 1))
                link(dve, dve.tensor_scalar(m, w, 1.0 / TWO_PI, MAGIC, ALU.mult, ALU.add))
                link(dve, dve.tensor_scalar(m, m, -MAGIC, None, ALU.add))
                for c in (C1, C2, C3):
                    link(dve, dve.scalar_tensor_tensor(out=w, in0=m, scalar=-c, in1=w, op0=ALU.mult, op1=ALU.add))
                dve.tensor_scalar(w, w, PI_F, -PI_F, ALU.min, ALU.max).then_inc(sem("f_arg"), 1)
            dve.wait_ge(*after("filt_in", 48))
            fb = nb[:, 4]
            for i in range(2 * TB):
                pt, o = divmod(i, 2)
                dve.wait_ge(*after("f_pos", i + 1))
                if i:
                    dve.wait_ge(*after("f_sum", 2 * i))
                dve.tensor_tensor(fb, bank[4 + i % 2][:, :], dec[:, pt], ALU.mult).then_inc(sem("f_used"), 1)
                dve.wait_ge(*after("f_used", i + 1))
                cols = slice(o * HY_C, (o + 1) * HY_C)
                for dst, op in ((hsum, ALU.add), (hdif, ALU.subtract)):
                    dve.tensor_tensor(dst[:, pt, cols], fb[:, 0:HY_C], fb[:, HY_C:], op).then_inc(sem("f_sum"), 1)
            for f in range(6):
                dve.wait_ge(*after("hy_tap", f + 1))
                ps, u = grid(bank[f % 4][:, :]), grid(u_hy[:, f])
                link(dve, dve.scalar_tensor_tensor(out=u[:, :, 1:], in0=ps[:, :, 0:CH - 1], scalar=gain("hyw0", f),
                                                   in1=u[:, :, 1:], op0=ALU.mult, op1=ALU.add))
                dve.scalar_tensor_tensor(out=u[:, :, 0:CH - 1], in0=ps[:, :, 1:], scalar=gain("hyw2", f),
                                         in1=u[:, :, 0:CH - 1], op0=ALU.mult, op1=ALU.add).then_inc(sem("hy_u"), 1)
            dve.wait_ge(*after("hy_u", 6))
            for o in range(2):
                dve.wait_ge(*after("H", 2 * TB))
                for ft in range(TB):
                    dve.wait_ge(*after("U", o * TB + ft + 1))
                    Uc, Us = bank[ft][:, 0:HY_C], bank[ft][:, HY_C:]
                    hc, hs = (a[:, ft, o * HY_C:(o + 1) * HY_C] for a in (Hc, Hs))
                    if o * TB + ft:
                        dve.wait_ge(*after("Y", o * TB + ft))
                    for n, (a, b) in enumerate(((Uc, hc), (Us, hs), (Uc, hs))):
                        dve.tensor_tensor(sp[:, n], a, b, ALU.mult)
                    dve.tensor_tensor(sp[:, 3], Us, hc, ALU.mult).then_inc(sem("spec"), 1)
                    dve.wait_ge(*after("spec", o * TB + ft + 1))
                    dve.tensor_tensor(Yc[:, ft], sp[:, 0], sp[:, 1], ALU.subtract)
                    dve.tensor_tensor(Ys[:, ft], sp[:, 2], sp[:, 3], ALU.add).then_inc(sem("Y"), 1)
                for m in range(2):
                    dve.wait_ge(*after("conv", 2 * o + m + 1))
                    y = u_hy[:, m]
                    link(dve, dve.scalar_tensor_tensor(out=y, in0=y, scalar=gain("hyd", 2 * o + m), in1=bank[4 + m][:, :],
                                                       op0=ALU.mult, op1=ALU.add))
                    dst = y if o == 0 else mix[:, m]
                    dve.tensor_tensor(dst, y, u_hy[:, 2 + 2 * o + m], ALU.mult).then_inc(sem("hy_y"), 1)
                dve.wait_ge(*after("hy_y", 2 * o + 2))

        m_f, m_b = cst[:, 0:P], cst[:, P:2 * P]
        reset = cst[:, 2 * P:2 * P + TA]
        is_fwd, is_bwd, sign = (cst[:, 2 * P + TA + n:2 * P + TA + n + 1] for n in range(3))
        agT, gt = cst[:, 1280:1280 + TA], cst[:, 2048:2048 + TA]
        gl_q, gl_k, gl_v = part(0, 2, T), part(1024, 2, TA), part(2560, NBLK, GW)
        gl_b = part(4864, 4, TA)
        gl_q1, gl_k2 = part(7936, 4, T), part(9984, 4, TA)
        gl_t = gl_k2
        gl_kT = part(13056, NBLK, T)
        gl_S, gl_Sr = part(16128, 4, GLA_DV), part(16512, 4, GLA_DV)
        gl_A = part(16896, 2, T)
        gl_sc = part(17920, 3, 4 * NCH)
        gl_U = part(18064, 4, GLA_DV)
        gl_o = mix[:, 2:5].rearrange("p k t -> p (k t)").rearrange("p (b n) -> p b n", b=TB)
        gl_w2 = big[:, 18448:18448 + 2 * P]
        gl_tot = big[:, 18704:18704 + 4 * NCH]
        gl_d = part(13056, 4, TA)
        gate = part(9984, TB, GW)
        chunks = lambda a: a.rearrange("p (n c) -> p n c", c=CH)

        def gates_pe(pe):
            pe.wait_ge(*after("gla_in", 32))
            fm_multi(pe, "ag", 1, [lat, ctxp], "ag_ps", "ag")
            fm_multi(pe, "gl_q", 2, [lat], "glq_ps", "glq")
            fm_multi(pe, "gl_k", 2, [lat, ctxp], "glk_ps", "glk")
            tm_linear(pe, "gl_v", GW, lambda k, tb: X2[:, k, tb * P:(tb + 1) * P], range(NBLK), "glv_ps", "glv")
            pe.wait_ge(*after("ag", 2))
            for i in range(8):
                dc, p = divmod(i, 2)
                d, c = divmod(dc, 2)
                a, n = ((CTX, T), (0, CTX))[p]
                ps = grab(pe, i % 4, *after("glz", i + 1))
                pe.matmul(ps[:, 0:n], gl_w2[32 * d:32 * d + GLA_RANK, c * P:(c + 1) * P],
                          agT[32 * d:32 * d + GLA_RANK, a:a + n], start=True, stop=True).then_inc(sem("glz_ps"), 1)

        def gates_act(act):
            act.wait_ge(*after("hy_y", 4))
            act.wait_ge(*after("gla_in", 32))
            for p, (a, n) in enumerate(((CTX, T), (0, CTX))):
                act.wait_ge(*after("ag_ps", p + 1))
                act.activation(agT[:, a:a + n], bank[p][:, 0:n], ACT.Copy).then_inc(sem("ag"), 1)
            for c in range(2):
                act.wait_ge(*after("glq_ps", c + 1))
                act.activation(gl_q[:, c], bank[c][:, :], ACT.Copy).then_inc(sem("glq"), 1)
            for i in range(4):
                a, n = ((CTX, T), (0, CTX))[i % 2]
                act.wait_ge(*after("glk_ps", i + 1))
                act.activation(gl_k[:, i // 2, a:a + n], bank[i][:, 0:n], ACT.Copy).then_inc(sem("glk"), 1)
            for i in range(NBLK):
                act.wait_ge(*after("glv_ps", i + 1))
                act.activation(gl_v[:, i], bank[i % 4][:, 0:GW], ACT.Copy).then_inc(sem("glv"), 1)
            hi = nb[64:P, 2:4].rearrange("p k t -> p (k t)")[:, 0:TA]
            act.wait_ge(*after("gt_abs", 1))
            link(act, act.activation(hi, hi, ACT.Exp, scale=-1.0))
            act.activation(hi, hi, ACT.Ln, bias=1.0).then_inc(sem("gt_ln"), 1)
            t = gl_t.rearrange("p k t -> p (k t)")
            act.wait_ge(*after("gla_abs", 1))
            link(act, act.activation(t, t, ACT.Exp, scale=-1.0))
            act.activation(t, t, ACT.Ln, bias=1.0).then_inc(sem("gla_ln"), 1)
            act.wait_ge(*after("gla_diff", 1))
            sc = big[:, 17920:17920 + 12 * NCH]
            act.activation(sc, sc, ACT.Exp).then_inc(sem("gla_esc"), 1)
            d = gl_d.rearrange("p k t -> p (k t)")
            act.activation(gl_b.rearrange("p k t -> p (k t)"), d, ACT.Exp).then_inc(sem("gla_ep"), 1)
            act.wait_ge(*after("gla_ep", 1))
            act.activation(d, d, ACT.Exp, scale=-1.0).then_inc(sem("gla_en"), 1)

        def gates_dve(dve):
            z = nb[64:P, 0:2].rearrange("p k t -> p (k t)")[:, 0:TA]
            az = nb[64:P, 2:4].rearrange("p k t -> p (k t)")[:, 0:TA]
            g = gt[64:P]
            dve.wait_ge(*after("ag", 2))
            dve.wait_ge(*after("x2b", KD))
            link(dve, dve.tensor_scalar(z, agT[64:P], sign[64:P], gain("dt")[64:P], ALU.mult, ALU.add))
            dve.scalar_tensor_tensor(out=az, in0=z, scalar=-1.0, in1=z, op0=ALU.mult, op1=ALU.max).then_inc(sem("gt_abs"), 1)
            dve.wait_ge(*after("gt_ln", 1))
            link(dve, dve.scalar_tensor_tensor(out=z, in0=z, scalar=0.0, in1=az, op0=ALU.max, op1=ALU.add))
            dve.wait_ge(*after("ea", 1))
            link(dve, dve.tensor_scalar(z, z, column(vecs, 136)[64:P], None, ALU.mult))
            link(dve, dve.tensor_copy(g, z))
            dve.wait_ge(*after("gla_in", 32))
            link(dve, dve.tensor_tensor_scan(az[0:32], reset[64:96], z[0:32], 0.0, ALU.mult, ALU.add))
            zc, ac = chunks(z[0:32]), chunks(az[0:32])
            link(dve, dve.tensor_tensor(zc, zc, ac, ALU.subtract))
            link(dve, dve.tensor_tensor(zc, zc, ac[:, :, CH - 1:CH].broadcast_to((32, NCH, CH)), ALU.add))
            link(dve, dve.tensor_scalar(z[0:32], z[0:32], is_bwd[64:96], None, ALU.mult))
            dve.scalar_tensor_tensor(out=g[0:32], in0=az[0:32], scalar=is_fwd[64:96], in1=z[0:32], op0=ALU.mult,
                                     op1=ALU.add).then_inc(sem("gt"), 1)
            for i in range(8):
                dc, p = divmod(i, 2)
                a, n = ((CTX, T), (0, CTX))[p]
                dve.wait_ge(*after("glz_ps", i + 1))
                dve.tensor_scalar(gl_b[:, dc, a:a + n], bank[i % 4][:, 0:n], gain("gla_b", dc), None, ALU.add)\
                   .then_inc(sem("glz"), 1)
            dve.wait_ge(*after("glz", 8))
            b, t, d = (a.rearrange("p k t -> p (k t)") for a in (gl_b, gl_t, gl_d))
            dve.scalar_tensor_tensor(out=t, in0=b, scalar=-1.0, in1=b, op0=ALU.mult, op1=ALU.max).then_inc(sem("gla_abs"), 1)
            dve.wait_ge(*after("gla_abs", 1))
            link(dve, dve.tensor_scalar(b, b, 0.0, 1.0 / GLA_TAU, ALU.min, ALU.mult))
            dve.wait_ge(*after("gla_ln", 1))
            link(dve, dve.scalar_tensor_tensor(out=t, in0=t, scalar=-1.0 / GLA_TAU, in1=b, op0=ALU.mult, op1=ALU.add))
            for dc in range(4):
                ins = dve.tensor_tensor_scan(gl_b[:, dc], reset, gl_t[:, dc], 0.0, ALU.mult, ALU.add)
            link(dve, ins)
            half = 2 * NCH
            bc, tc, dcc = chunks(b), chunks(t), chunks(d)
            tot = gl_tot[:, :]
            link(dve, dve.tensor_copy(tot, bc[:, :, CH - 1]))
            bb, tb_ = bc[:, half:], tc[:, half:]
            link(dve, dve.tensor_tensor(bb, tb_, bb, ALU.subtract))
            link(dve, dve.tensor_tensor(bb, bb, tot[:, half:].unsqueeze(2).broadcast_to((P, half, CH)), ALU.add))
            sc = gl_sc
            link(dve, dve.tensor_copy(sc[:, 0, 0:half], bc[:, 0:half, CH // 2 - 1]))
            link(dve, dve.tensor_copy(sc[:, 0, half:], bc[:, half:, CH // 2]))
            link(dve, dve.tensor_copy(sc[:, 1], tot))
            link(dve, dve.tensor_tensor(sc[:, 2], sc[:, 1], sc[:, 0], ALU.subtract))
            dve.tensor_tensor(dcc, bc, sc[:, 0].unsqueeze(2).broadcast_to((P, 4 * NCH, CH)), ALU.subtract)\
               .then_inc(sem("gla_diff"), 1)
            dve.wait_ge(*after("gla_diff", 1))
            dve.wait_ge(*after("gla_en", 1))
            dve.wait_ge(*after("glq", 2))
            dve.wait_ge(*after("glk", 4))
            for dc in range(4):
                c = dc % 2
                dve.scalar_tensor_tensor(out=gl_q1[:, dc], in0=gl_q[:, c], scalar=GLA_DK ** -0.5, in1=gl_b[:, dc, CTX:TA],
                                         op0=ALU.mult, op1=ALU.mult)
                dve.tensor_tensor(gl_k2[:, dc], gl_k[:, c], gl_d[:, dc], ALU.mult).then_inc(sem("gla_qk"), 1)

        def steps(d):
            return list(range(NCH)) if d == 0 else list(range(CCH))[::-1] + list(range(CCH, NCH))[::-1]

        def gla_pe(pe):
            pe.wait_ge(*after("gla_qk", 4))
            pe.wait_ge(*after("glv", NBLK))
            for b in range(NBLK):
                ps = grab(pe, 4 + b % 2, *after("glkT", b + 1))
                for dc in range(4):
                    mm = pe.transpose(ps[:, dc * P:(dc + 1) * P], gl_k2[:, dc, b * P:(b + 1) * P], ident)
                mm.then_inc(sem("gl_turn"), 1)
            def scores(tb):
                for hh in range(2):
                    ps = grab(pe, 2 * (tb % 2) + hh, *after("gl_A", tb + 1))
                    r = 64 * hh
                    for dc in range(4):
                        mm = pe.matmul(ps[:, dc * P:(dc + 1) * P], gl_k2[r:r + 64, dc, CTX + tb * P:CTX + (tb + 1) * P],
                                       gl_q1[r:r + 64, dc, tb * P:(tb + 1) * P], start=True, stop=True)
                    mm.then_inc(sem("gl_s"), 1)

            def inner(tb):
                pe.wait_ge(*after("gl_A", tb + 1))
                ps = grab(pe, 4 + tb % 2, *after("gl_in", tb + 1))
                for hd in range(GH):
                    mm = pe.matmul(ps[:, hd * GLA_DV:(hd + 1) * GLA_DV], gl_A[:, tb % 2, hd * P:(hd + 1) * P],
                                   gl_v[:, CB + tb, hd * GLA_DV:(hd + 1) * GLA_DV], start=True, stop=True)
                mm.then_inc(sem("gl_o"), 1)
            scores(0)
            for tb in range(TB):
                if tb + 1 < TB:
                    scores(tb + 1)
                inner(tb)
            pe.wait_ge(*after("glkT", NBLK))
            n_in = 0
            for n in range(NCH):
                for dc in range(4):
                    d = dc // 2
                    if dc % 2 == 0:
                        ps = grab(pe, 2 * (n % 2) + d, *after("gl_Su", n + 1))
                    c = steps(d)[n]
                    r = CH * (c % 2)
                    for hh in range(2):
                        hd = 2 * (dc % 2) + hh
                        mm = pe.matmul(ps[64 * hh:64 * hh + 64, (dc % 2) * GLA_DV:(dc % 2 + 1) * GLA_DV],
                                       gl_kT[r:r + CH, c // 2, dc * P + 64 * hh:dc * P + 64 * hh + 64],
                                       gl_v[r:r + CH, c // 2, hd * GLA_DV:(hd + 1) * GLA_DV], start=True, stop=True)
                mm.then_inc(sem("gl_U"), 1)
                if n >= CCH:
                    for d in range(2):
                        c = steps(d)[n] - CCH
                        r = CH * (c % 2)
                        pe.wait_ge(*after("gl_Sr", 2 * (n - CCH) + d + 1))
                        for hd in (0, 2, 1, 3):
                            q, dc = 64 * (hd % 2), 2 * d + hd // 2
                            if hd < 2:
                                ps = grab(pe, 4 + 2 * d + hd, *after("gl_add", 4 * (n - CCH) + 2 * d + hd + 1))
                            mm = pe.matmul(ps[r:r + CH, (hd // 2) * GLA_DV:(hd // 2 + 1) * GLA_DV],
                                           gl_q1[q:q + 64, dc, c * CH:(c + 1) * CH], gl_Sr[q:q + 64, dc, :],
                                           start=True, stop=True)
                        mm.then_inc(sem("gl_x"), 1)

        def gla_act(act):
            for b in range(NBLK):
                act.wait_ge(*after("gl_turn", b + 1))
                act.activation(gl_kT[:, b], bank[4 + b % 2][:, :], ACT.Copy).then_inc(sem("glkT"), 1)

        def gla_dve(dve):
            v4 = lambda a: a.rearrange("p (h n) -> p h n", h=GH)
            for tb in range(TB):
                dve.wait_ge(*after("gl_s", 2 * tb + 2))
                if tb >= 2:
                    dve.wait_ge(*after("gl_o", tb - 1))
                A, B_ = v4(gl_A[:, tb % 2]), v4(tmp[:, 0])
                for dst, at_, m in ((A, 0, m_f), (B_, 2, m_b)):
                    for hh in range(2):
                        ins = dve.tensor_tensor(dst[:, hh::2], v4(bank[2 * (tb % 2) + hh][:, :])[:, at_:at_ + 2],
                                                m.unsqueeze(1).broadcast_to((P, 2, P)), ALU.mult)
                link(dve, ins)
                dve.tensor_tensor(A, A, B_, ALU.add).then_inc(sem("gl_A"), 1)
                dve.wait_ge(*after("gl_o", tb + 1))
                dve.tensor_copy(gl_o[:, tb], bank[4 + tb % 2][:, 0:GW]).then_inc(sem("gl_in"), 1)
            dve.wait_ge(*after("gl_in", TB))
            dve.wait_ge(*after("gla_esc", 1))
            link(dve, dve.memset(gl_S[:, :, :], 0.0))
            scol = lambda kind, d, c: gl_sc[:, kind].rearrange("p (a n) -> p a n", a=4)[:, 2 * d:2 * d + 2, c:c + 1]\
                .broadcast_to((P, 2, GLA_DV))
            adds = 0
            for n in range(NCH):
                dve.wait_ge(*after("gl_U", n + 1))
                if n >= CCH:
                    for d in range(2):
                        if n > CCH:
                            dve.wait_ge(*after("gl_x", 2 * (n - CCH) - 1 + d))
                        dve.tensor_tensor(gl_Sr[:, 2 * d:2 * d + 2], gl_S[:, 2 * d:2 * d + 2], scol(0, d, steps(d)[n]), ALU.mult)\
                           .then_inc(sem("gl_Sr"), 1)
                    dve.wait_ge(*after("gl_Sr", 2 * (n - CCH) + 2))
                for d in range(2):
                    c = steps(d)[n]
                    S, u = gl_S[:, 2 * d:2 * d + 2], gl_U[:, 2 * d:2 * d + 2]
                    dve.tensor_tensor(S, S, scol(1, d, c), ALU.mult)
                    U = bank[2 * (n % 2) + d][:, 0:2 * GLA_DV].rearrange("p (a n) -> p a n", a=2)
                    ins = dve.tensor_tensor(u, U, scol(2, d, c), ALU.mult)
                ins.then_inc(sem("gl_Su"), 1)
                dve.wait_ge(*after("gl_Su", n + 1))
                link(dve, dve.tensor_tensor(gl_S[:, :], gl_S[:, :], gl_U[:, :], ALU.add))
                if n >= CCH:
                    for d in range(2):
                        c = steps(d)[n] - CCH
                        r = CH * (c % 2)
                        dve.wait_ge(*after("gl_x", 2 * (n - CCH) + d + 1))
                        for hh in range(2):
                            o = v4(gl_o[r:r + CH, c // 2])[:, hh::2]
                            x_ = bank[4 + 2 * d + hh][r:r + CH, 0:2 * GLA_DV].rearrange("p (a n) -> p a n", a=2)
                            dve.tensor_tensor(o, o, x_, ALU.add).then_inc(sem("gl_add"), 1)
                        dve.wait_ge(*after("gl_add", 4 * (n - CCH) + 2 * d + 2))

        def heads_pe(pe, st, name, o, turned=True):
            tm_linear(pe, name, GW, lambda k, tb: X2[:, k, CTX + tb * P:CTX + (tb + 1) * P], range(TB),
                      st + "_gps", st + "_gate")

        def heads_flip(pe, st, src):
            pe.wait_ge(*after(st + "_normed", 1))
            for c in range(3):
                ps = grab(pe, 4 + c % 2, *after(st + "_cat", c + 1))
                for tb in range(TB):
                    mm = pe.transpose(ps[:, tb * P:(tb + 1) * P], src[:, tb, c * P:(c + 1) * P], ident)
                mm.then_inc(sem(st + "_flip"), 1)

        def heads_gate(act, st, gate):
            for tb in range(TB):
                act.wait_ge(*after(st + "_gps", tb + 1))
                act.activation(gate[:, tb], bank[tb % 4][:, 0:GW], ACT.Silu).then_inc(sem(st + "_gate"), 1)

        def heads_act(act, st, dst):
            act.wait_ge(*after(st + "_ss", 1))
            act.activation(stat[:, 0:16], stat[:, 0:16], ACT.Sqrt).then_inc(sem(st + "_sd"), 1)
            for c in range(3):
                act.wait_ge(*after(st + "_flip", c + 1))
                act.activation(mix[:, dst + c], bank[4 + c % 2][:, :], ACT.Copy).then_inc(sem(st + "_cat"), 1)

        def heads_dve(dve, st, o, gate, gate_ready, res, gn):
            v = lambda a: a.rearrange("p b (h n) -> p (b h) n", h=GH)
            s16 = stat[:, 0:16]
            link(dve, dve.tensor_tensor(v(res), v(o), v(o), ALU.mult))
            link(dve, dve.tensor_reduce(s16, v(res), AX.X, ALU.add))
            dve.tensor_scalar(s16, s16, 1.0 / GDN_D, EPS, ALU.mult, ALU.add).then_inc(sem(st + "_ss"), 1)
            dve.wait_ge(*after(st + "_sd", 1))
            link(dve, dve.reciprocal(s16, s16))
            link(dve, dve.tensor_tensor(v(res), v(o), s16.unsqueeze(2).broadcast_to((P, 16, GDN_D)), ALU.mult))
            link(dve, dve.tensor_tensor(v(res), v(res), small_cols(gn, GDN_D).unsqueeze(1).broadcast_to((P, 16, GDN_D)), ALU.mult))
            dve.wait_ge(*after(gate_ready, TB))
            dve.tensor_tensor(res, res, gate, ALU.mult).then_inc(sem(st + "_normed"), 1)

        gl_res = part(0, TB, GW)

        gd_q, gd_k = part(0, GH, T), part(2048, GH, TA)
        gd_vT, gd_kT = part(5120, NBLK, GW), part(7424, NBLK, GW)
        selA, selL = (big[:, 9728 + 1024 * n:9728 + 1024 * (n + 1)].rearrange("p (r n) -> p r n", r=8) for n in range(2))
        gd_vf = part(11776, 3, TA)
        gd_wT, gd_u = part(11776, GH, TA), part(14848, NBLK, GW)
        gd_AT = part(17152, TB, T)
        gd_S = big[0:GDN_D, 19200:19200 + GW]
        gd_r = part(19584, 2, GW)
        gd_sc = big[:, 20352:20352 + 8 * NBLK * 8].rearrange("p (s b r) -> p s b r", s=8, b=NBLK)
        gd_o = mix[:, 5:8].rearrange("p k t -> p (k t)").rearrange("p (b n) -> p b n", b=TB)
        gd_gate = xn_all[:, 0:TB * GW].rearrange("p (b n) -> p b n", b=TB)
        gmask = lambda d, strict: cst[:, (2 * d + (0 if strict else 1)) * P:(2 * d + (0 if strict else 1) + 1) * P]
        level = lambda d, n: cst[:, (4 + 6 * d + n) * P:(5 + 6 * d + n) * P]
        wide = lambda m: m.unsqueeze(1).broadcast_to((P, GH, P))
        v4 = lambda a: a.rearrange("p (h n) -> p h n", h=GH)
        work = [[xn_all[:, 1536 + (4 * s + n) * T:1536 + (4 * s + n + 1) * T] for n in range(4)] +
                [nb[:, 2 * s], nb[:, 2 * s + 1]] for s in range(2)]
        GPARTS = [(CTX, T), (0, CTX)]
        NQ, NK, NV = GH, GH, 3
        fills = [("q", f, 0) for f in range(NQ)] + [("k", f, p) for f in range(NK) for p in range(2)] + \
                [("v", f, p) for f in range(NV) for p in range(2)]

        def gd_dst(kind, f, p):
            a, n = GPARTS[p]
            return gd_q[:, f] if kind == "q" else (gd_k if kind == "k" else gd_vf)[:, f, a:a + n]

        def gd_tap(kind, f, j):
            return gain(f"gdw{j}", {"q": 0, "k": GH, "v": 2 * GH}[kind] + f)

        def delta_in_pe(pe):
            i = 0
            for kind, name, chunks_, parts in (("q", "gd_q", NQ, [lat]), ("k", "gd_k", NK, [lat, ctxp]), ("v", "gd_v", NV, [lat, ctxp])):
                u0 = UNITS[name]
                for f in range(chunks_):
                    for rhs, n in parts:
                        ps = grab(pe, i % 4, *after("gd_conv", i + 1))
                        take(pe, u0 + f)
                        for k in range(KD):
                            mm = pe.matmul(ps[:, 0:n], ring[:, (u0 + f) % RING, k * P:(k + 1) * P], rhs(k),
                                           start=(k == 0), stop=(k == KD - 1))
                        mm.then_inc(sem("gd_ps"), 1)
                        i += 1
                    unit_used[u0 + f] = after("gd_ps", i)
            heads_pe(pe, "gd", "gd_g", None)
            for i in range(NQ + 2 * NK):
                ps = grab(pe, 6 + i % 2, *after("gd_rs", i + 1))
                n = GPARTS[fills[i][2]][1]
                pe.wait_ge(*after("gd_sq", i + 1))
                pe.matmul(ps[:, 0:n], ones, sq[:, i % 2, 0:n], start=True, stop=True).then_inc(sem("gd_ss"), 1)
            pe.wait_ge(*after("gd_normed", NQ + 2 * NK))
            pe.wait_ge(*after("gd_silu", len(fills)))
            for i in range(2 * NBLK):
                b, isv = divmod(i, 2)
                ps = grab(pe, 4 + i % 2, *after("gd_tm", i + 1))
                if isv:
                    for c in range(NV):
                        mm = pe.transpose(ps[:, c * P:(c + 1) * P], gd_vf[:, c, b * P:(b + 1) * P], ident)
                else:
                    for c in range(GH):
                        mm = pe.transpose(ps[:, c * GDN_D:(c + 1) * GDN_D], gd_k[0:GDN_D, c, b * P:(b + 1) * P],
                                          ident[0:GDN_D, 0:GDN_D])
                mm.then_inc(sem("gd_turn"), 1)
            pe.wait_ge(*after("gt", 1))
            pe.wait_ge(*after("gdn_in", 32))
            ps = grab(pe, 0, *after("gd_tg", 1))
            for b in range(NBLK):
                mm = pe.transpose(ps[:, b * 64:(b + 1) * 64], gt[64:P, b * P:(b + 1) * P], ident[64:P, 64:P])
            mm.then_inc(sem("gd_gT"), 1)
            ps = grab(pe, 1, *after("gd_gl", 1))
            for r in range(8):
                last_ = chunks(gt[64:P])[:, :, CH - 1 if r < GH else 0]
                mm = pe.matmul(ps[:, r * NCH:(r + 1) * NCH], selA[64:P, r], last_, start=True, stop=True)
            mm.then_inc(sem("gd_last"), 1)

        def delta_in_act(act):
            for i, (kind, f, p) in enumerate(fills):
                dst = gd_dst(kind, f, p)
                n = GPARTS[p][1]
                act.wait_ge(*after("gd_ps", i + 1))
                if i == 0:
                    act.wait_ge(*after("gla_cat", 3))
                act.activation(dst, bank[i % 4][:, 0:n], ACT.Copy, scale=gd_tap(kind, f, GDN_TAPS // 2))\
                   .then_inc(sem("gd_tap"), 1)
                if i >= 1:
                    act.wait_ge(*after("gd_conv", i))
                    act.activation(gd_dst(*fills[i - 1]), gd_dst(*fills[i - 1]), ACT.Silu).then_inc(sem("gd_silu"), 1)
            act.wait_ge(*after("gd_conv", len(fills)))
            act.activation(gd_dst(*fills[-1]), gd_dst(*fills[-1]), ACT.Silu).then_inc(sem("gd_silu"), 1)
            for tb in range(TB):
                act.wait_ge(*after("gd_gps", tb + 1))
                if tb == 0:
                    act.wait_ge(*after("gd_gps", TB))
                act.activation(gd_gate[:, tb], bank[tb % 4][:, 0:GW], ACT.Silu).then_inc(sem("gd_gate"), 1)
            for i in range(NQ + 2 * NK):
                n = GPARTS[fills[i][2]][1]
                act.wait_ge(*after("gd_silu", i + 1))
                if i >= 2:
                    act.wait_ge(*after("gd_ss", i - 1))
                act.activation(sq[:, i % 2, 0:n], gd_dst(*fills[i]), ACT.Square).then_inc(sem("gd_sq"), 1)
                if i >= 1:
                    m = GPARTS[fills[i - 1][2]][1]
                    act.wait_ge(*after("gd_rs", i))
                    act.activation(nb[:, 2 + (i - 1) % 2, 0:m], nb[:, 2 + (i - 1) % 2, 0:m], ACT.Sqrt).then_inc(sem("gd_sd"), 1)
            i = NQ + 2 * NK
            m = GPARTS[fills[i - 1][2]][1]
            act.wait_ge(*after("gd_rs", i))
            act.activation(nb[:, 2 + (i - 1) % 2, 0:m], nb[:, 2 + (i - 1) % 2, 0:m], ACT.Sqrt).then_inc(sem("gd_sd"), 1)
            for i in range(2 * NBLK):
                b, isv = divmod(i, 2)
                act.wait_ge(*after("gd_turn", i + 1))
                act.activation((gd_vT if isv else gd_kT)[:, b], bank[4 + i % 2][:, 0:GW], ACT.Copy).then_inc(sem("gd_tm"), 1)
            act.wait_ge(*after("gd_gl", 1))
            act.activation(big[:, 20352 + 48:20352 + 5 * 48], big[:, 20352 + 48:20352 + 5 * 48], ACT.Exp).then_inc(sem("gd_es"), 1)
            act.activation(stat[:, 0:48], stat[:, 0:48], ACT.Exp).then_inc(sem("gd_es"), 1)
            act.activation(vecs[:, 160:208], vecs[:, 160:208], ACT.Exp).then_inc(sem("gd_es"), 1)

        def delta_in_dve(dve):
            R = GDN_TAPS // 2
            for i, (kind, f, p) in enumerate(fills):
                n = GPARTS[p][1]
                ps, u = bank[i % 4][:, 0:n], gd_dst(kind, f, p)
                if p == 0:
                    ps, u = grid(ps), grid(u)
                else:
                    ps, u = ps.unsqueeze(1), u.unsqueeze(1)
                m = CH if p == 0 else n
                dve.wait_ge(*after("gd_tap", i + 1))
                for j in range(GDN_TAPS):
                    s = j - R
                    if s == 0:
                        continue
                    o0, o1 = max(0, -s), m - max(0, s)
                    ins = dve.scalar_tensor_tensor(out=u[:, :, o0:o1], in0=ps[:, :, o0 + s:o1 + s], scalar=gd_tap(kind, f, j),
                                                   in1=u[:, :, o0:o1], op0=ALU.mult, op1=ALU.add)
                    if j < GDN_TAPS - 1:
                        link(dve, ins)
                ins.then_inc(sem("gd_conv"), 1)
            for i in range(NQ + 2 * NK):
                kind, f, p = fills[i]
                n = GPARTS[p][1]
                v = nb[:, 2 + i % 2, 0:n]
                dve.wait_ge(*after("gd_ss", i + 1))
                if i >= 2:
                    dve.wait_ge(*after("gd_normed", i - 1))
                dve.tensor_scalar(v, bank[6 + i % 2][:, 0:n], EPS, None, ALU.add).then_inc(sem("gd_rs"), 1)
                dve.wait_ge(*after("gd_sd", i + 1))
                link(dve, dve.reciprocal(v, v))
                x_ = gd_dst(kind, f, p)
                dve.scalar_tensor_tensor(out=x_, in0=x_, scalar=GDN_D ** -0.5 if kind == "q" else 1.0, in1=v,
                                         op0=ALU.mult, op1=ALU.mult).then_inc(sem("gd_normed"), 1)
            tg = bank[0][:, 0:NBLK * 64].rearrange("p (b r) -> p b r", b=NBLK)
            gd = gd_sc
            dve.wait_ge(*after("gd_gT", 1))
            link(dve, dve.tensor_scalar(gd[:, 0], tg[:, :, 0:8], -1.0, None, ALU.mult))
            link(dve, dve.tensor_copy(gd[:, 1], tg[:, :, 0:8]))
            link(dve, dve.tensor_copy(gd[:, 2], tg[:, :, 32:40]))
            dve.tensor_tensor(gd[:, 3], gd[:, 1], gd[:, 2], ALU.add).then_inc(sem("gd_tg"), 1)
            dve.wait_ge(*after("gd_last", 1))
            gl = bank[1][:, 0:8 * NCH].rearrange("p (r b two) -> p two b r", r=8, two=2)
            for par in range(2):
                rows_ = slice(64 * par, 64 * par + 64)
                ins = dve.tensor_tensor(gd[rows_, 4], gl[rows_, par], gd[rows_, 0], ALU.add)
            link(dve, ins)
            link(dve, dve.tensor_copy(stat[:, 0:48], bank[1][:, 0:48]))
            dve.tensor_copy(vecs[:, 160:208], bank[1][:, 48:96]).then_inc(sem("gd_gl"), 1)

        def blocks_of(d):
            return list(range(NBLK))

        PER_DIRECTION = {"LT": 6, "gram": 6, "rhs": 6, "wps": 6, "ups": 6, "w": 6, "u": 6, "E": 10, "g": 10, "D": 10,
                         "A": 18, "TT": 18, "x": 18, "T": 15, "X": 15, "y": 12, "yt": 15, "qk": 4, "AT": 4, "S0": 1,
                         "v": 12, "S": 12, "k3": 12, "wS": 12, "kv": 12, "o": 16, "qS": 8, "Av": 8}

        def delta_sems(d):
            base = lambda name: d * PER_DIRECTION[name if name == "S0" else name.rstrip("01")]
            return (lambda name: sem("delta_" + name)), (lambda name, count: base(name) + count)

        def delta_pe(pe, d):
            s, at = delta_sems(d)
            pe.wait_ge(*after("gd_tm", 2 * NBLK))
            pe.wait_ge(*after("gd_gate", TB))

            def gram(b, i):
                ps = grab(pe, i % 2, s("LT"), at("LT", i + 1))
                for hd in range(GH):
                    mm = pe.matmul(ps[:, hd * P:(hd + 1) * P], gd_k[:, hd, b * P:(b + 1) * P], gd_k[:, hd, b * P:(b + 1) * P],
                                   start=True, stop=True)
                mm.then_inc(s("gram"), 1)
                ps = grab(pe, 2 + i % 2, s("E"), at("E", i + 1))
                for hd in range(GH):
                    mm = pe.matmul(ps[:, hd * P:(hd + 1) * P], selL[64:P, GH * d + hd], gt[64:P, b * P:(b + 1) * P],
                                   start=True, stop=True)
                mm.then_inc(s("g"), 1)

            def level_x(i, n):
                L, A, X, Tm, TT, E = work[i % 2]
                pe.wait_ge(s(f"A{i % 2}"), at(f"A{i % 2}", 6 * (i // 2) + n + 1))
                if n == 0:
                    pe.wait_ge(s(f"TT{i % 2}"), at(f"TT{i % 2}", 6 * (i // 2) + 1))
                    ps = grab(pe, 4 + i % 2, s(f"T{i % 2}"), at(f"T{i % 2}", 5 * (i // 2) + 1))
                    for hd in range(GH):
                        mm = pe.transpose(ps[:, hd * P:(hd + 1) * P], TT[:, hd * P:(hd + 1) * P], ident)
                    mm.then_inc(s(f"x{i % 2}"), 1)
                    return
                pe.wait_ge(s(f"T{i % 2}"), at(f"T{i % 2}", 5 * (i // 2) + n))
                pe.wait_ge(s(f"TT{i % 2}"), at(f"TT{i % 2}", 6 * (i // 2) + n))
                ps = grab(pe, 4 + i % 2, s(f"X{i % 2}"), at(f"X{i % 2}", 5 * (i // 2) + n))
                for hd in range(GH):
                    c = slice(hd * P, (hd + 1) * P)
                    mm = pe.matmul(ps[:, c], A[:, c], Tm[:, c], start=True, stop=True)
                mm.then_inc(s(f"x{i % 2}"), 1)

            def level_y(i, n):
                L, A, X, Tm, TT, E = work[i % 2]
                if n == 0:
                    return
                pe.wait_ge(s(f"X{i % 2}"), at(f"X{i % 2}", 5 * (i // 2) + n))
                if n < 5:
                    ps = grab(pe, 6 + i % 2, s(f"T{i % 2}"), at(f"T{i % 2}", 5 * (i // 2) + n + 1))
                    for hd in range(GH):
                        c = slice(hd * P, (hd + 1) * P)
                        mm = pe.matmul(ps[:, c], TT[:, c], X[:, c], start=True, stop=True)
                    mm.then_inc(s(f"y{i % 2}"), 1)
                ps = grab(pe, i % 2, s(f"TT{i % 2}"), at(f"TT{i % 2}", 6 * (i // 2) + n + 1))
                for hd in range(GH):
                    c = slice(hd * P, (hd + 1) * P)
                    mm = pe.matmul(ps[:, c], X[:, c], TT[:, c], start=True, stop=True)
                mm.then_inc(s(f"yt{i % 2}"), 1)

            def right(i, b):
                TT = work[i % 2][4]
                pe.wait_ge(s(f"TT{i % 2}"), at(f"TT{i % 2}", 6 * (i // 2) + 6))
                pe.wait_ge(s("rhs"), at("rhs", i + 1))
                ps = grab(pe, 2 + i % 2, s("w"), at("w", i + 1))
                for hd in range(GH):
                    mm = pe.matmul(ps[0:GDN_D, hd * P:(hd + 1) * P], gd_r[:, 0, hd * GDN_D:(hd + 1) * GDN_D],
                                   TT[:, hd * P:(hd + 1) * P], start=True, stop=True)
                mm.then_inc(s("wps"), 1)
                ps = grab(pe, 4 + i % 2, s("u"), at("u", i + 1))
                for hd in range(GH):
                    mm = pe.matmul(ps[:, hd * GDN_D:(hd + 1) * GDN_D], TT[:, hd * P:(hd + 1) * P],
                                   gd_r[:, 1, hd * GDN_D:(hd + 1) * GDN_D], start=True, stop=True)
                mm.then_inc(s("ups"), 1)

            for i0 in range(0, NBLK, 2):
                for i in (i0, i0 + 1):
                    gram(i, i)
                for n in range(6):
                    for i in (i0, i0 + 1):
                        level_x(i, n)
                    for i in (i0, i0 + 1):
                        level_y(i, n)
                for i in (i0, i0 + 1):
                    right(i, i)
            for tb in range(TB):
                b = CB + tb
                ps = grab(pe, tb % 2, s("AT"), at("AT", tb + 1))
                for hd in range(GH):
                    mm = pe.matmul(ps[:, hd * P:(hd + 1) * P], gd_k[:, hd, b * P:(b + 1) * P],
                                   gd_q[:, hd, tb * P:(tb + 1) * P], start=True, stop=True)
                mm.then_inc(s("qk"), 1)
                ps = grab(pe, 2 + tb % 2, s("E"), at("E", NBLK + tb + 1))
                for hd in range(GH):
                    mm = pe.matmul(ps[:, hd * P:(hd + 1) * P], selA[64:P, GH * d + hd], gt[64:P, b * P:(b + 1) * P],
                                   start=True, stop=True)
                mm.then_inc(s("g"), 1)
            pe.wait_ge(s("AT"), at("AT", TB))
            pe.wait_ge(s("w"), at("w", NBLK))
            pe.wait_ge(s("S0"), at("S0", 1))
            for n, c in enumerate(steps(d)):
                r, b = CH * (c % 2), c // 2
                rows_ = slice(r, r + CH)
                tb = b - CB
                if n:
                    pe.wait_ge(s("S"), at("S", n))
                ps = grab(pe, 0, s("v"), at("v", n + 1))
                for hd in range(GH):
                    v = slice(hd * GDN_D, (hd + 1) * GDN_D)
                    mm = pe.matmul(ps[rows_, v], gd_wT[0:GDN_D, hd, c * CH:(c + 1) * CH], gd_S[:, v], start=True, stop=True)
                mm.then_inc(s("wS"), 1)
                if n >= CCH:
                    ps = grab(pe, 2, s("o"), at("o", 2 * (n - CCH) + 1))
                    for hd in range(GH):
                        v = slice(hd * GDN_D, (hd + 1) * GDN_D)
                        mm = pe.matmul(ps[rows_, v], gd_q[0:GDN_D, hd, (c - CCH) * CH:(c - CCH + 1) * CH], gd_S[:, v],
                                       start=True, stop=True)
                    mm.then_inc(s("qS"), 1)
                pe.wait_ge(s("v"), at("v", n + 1))
                pe.wait_ge(s("k3"), at("k3", n + 1))
                ps = grab(pe, 1, s("S"), at("S", n + 1))
                for hd in range(GH):
                    v = slice(hd * GDN_D, (hd + 1) * GDN_D)
                    mm = pe.matmul(ps[0:GDN_D, v], gd_r[rows_, n % 2, v], gd_vn(n)[rows_, v], start=True, stop=True)
                mm.then_inc(s("kv"), 1)
                if n >= CCH:
                    ps = grab(pe, 3, s("o"), at("o", 2 * (n - CCH) + 2))
                    for hd in range(GH):
                        v = slice(hd * GDN_D, (hd + 1) * GDN_D)
                        mm = pe.matmul(ps[rows_, v], gd_AT[rows_, tb, hd * P + r:hd * P + r + CH], gd_vn(n)[rows_, v],
                                       start=True, stop=True)
                    mm.then_inc(s("Av"), 1)

        def gd_vn(n):
            return nb[:, n % 2, 0:GW]

        def delta_act(act, d):
            s, at = delta_sems(d)

            def decay(i, b, dst):
                act.wait_ge(s("E"), at("E", i + 1))
                for hd in range(GH):
                    ins = act.activation(dst[:, hd * P:(hd + 1) * P], dst[:, hd * P:(hd + 1) * P], ACT.Exp,
                                         bias=gd_sc[:, 0, b, GH * d + hd:GH * d + hd + 1])
                ins.then_inc(s("D"), 1)

            for i0 in range(0, NBLK, 2):
                for i in (i0, i0 + 1):
                    decay(i, i, work[i % 2][5])
                for n in range(6):
                    for i in (i0, i0 + 1):
                        X, Tm = work[i % 2][2], work[i % 2][3]
                        act.wait_ge(s(f"x{i % 2}"), at(f"x{i % 2}", 6 * (i // 2) + n + 1))
                        if n == 0:
                            act.activation(Tm, bank[4 + i % 2][:, :], ACT.Copy).then_inc(s(f"T{i % 2}"), 1)
                        else:
                            act.activation(X, bank[4 + i % 2][:, :], ACT.Copy).then_inc(s(f"X{i % 2}"), 1)
                for i in (i0, i0 + 1):
                    act.wait_ge(s("wps"), at("wps", i + 1))
                    act.activation(gd_wT[0:GDN_D, :, i * P:(i + 1) * P],
                                   bank[2 + i % 2][0:GDN_D, :].rearrange("p (h n) -> p h n", h=GH), ACT.Copy).then_inc(s("w"), 1)
                    act.wait_ge(s("ups"), at("ups", i + 1))
                    act.activation(gd_u[:, i], bank[4 + i % 2][:, 0:GW], ACT.Copy).then_inc(s("u"), 1)
            for tb in range(TB):
                decay(NBLK + tb, CB + tb, work[tb % 2][5])

        def delta_dve(dve, d):
            s, at = delta_sems(d)
            tok = lambda kind, b, rows_=slice(0, P): gd_sc[rows_, kind, b, GH * d:GH * d + GH].unsqueeze(2)\
                .broadcast_to((rows_.stop - rows_.start, GH, GDN_D))
            dve.wait_ge(*after("gd_es", 3))

            def masked(i, dst, m):
                dve.wait_ge(s("g"), at("g", i + 1))
                dve.tensor_tensor(v4(dst), v4(bank[2 + i % 2][:, :]), wide(m), ALU.add).then_inc(s("E"), 1)

            for i0 in range(0, NBLK, 2):
                for i in (i0, i0 + 1):
                    masked(i, work[i % 2][5], gmask(d, True))
                for i in (i0, i0 + 1):
                    L, A, X, Tm, TT, E = work[i % 2]
                    dve.wait_ge(s("gram"), at("gram", i + 1))
                    dve.wait_ge(s("D"), at("D", i + 1))
                    dve.tensor_tensor(L, bank[i % 2][:, :], E, ALU.mult).then_inc(s("LT"), 1)
                    dve.wait_ge(s("LT"), at("LT", i + 1))
                    dve.tensor_tensor(v4(A), v4(L), wide(level(d, 0)), ALU.mult).then_inc(s(f"A{i % 2}"), 1)
                    dve.wait_ge(s(f"A{i % 2}"), at(f"A{i % 2}", 6 * (i // 2) + 1))
                    dve.tensor_tensor(v4(TT), wide(ident), v4(A), ALU.subtract).then_inc(s(f"TT{i % 2}"), 1)
                for n in range(1, 6):
                    for i in (i0, i0 + 1):
                        L, A, X, Tm, TT, E = work[i % 2]
                        if n == 1:
                            dve.wait_ge(s(f"TT{i % 2}"), at(f"TT{i % 2}", 6 * (i // 2) + 1))
                        else:
                            dve.wait_ge(s(f"x{i % 2}"), at(f"x{i % 2}", 6 * (i // 2) + n))
                        dve.tensor_tensor(v4(A), v4(L), wide(level(d, n)), ALU.mult).then_inc(s(f"A{i % 2}"), 1)
                    for i in (i0, i0 + 1):
                        L, A, X, Tm, TT, E = work[i % 2]
                        dve.wait_ge(s(f"yt{i % 2}"), at(f"yt{i % 2}", 5 * (i // 2) + n))
                        if n < 5:
                            dve.tensor_tensor(Tm, Tm, bank[6 + i % 2][:, :], ALU.subtract).then_inc(s(f"T{i % 2}"), 1)
                        dve.tensor_tensor(TT, TT, bank[i % 2][:, :], ALU.subtract).then_inc(s(f"TT{i % 2}"), 1)
                        dve.wait_ge(s(f"TT{i % 2}"), at(f"TT{i % 2}", 6 * (i // 2) + n + 1))
                for i in (i0, i0 + 1):
                    if i:
                        dve.wait_ge(s("ups"), at("ups", i))
                    kT_, vT_ = (a[:, i].rearrange("p (h n) -> p h n", h=GH) for a in (gd_kT, gd_vT))
                    dve.tensor_tensor(v4(gd_r[:, 0]), kT_, tok(3, i), ALU.mult)
                    dve.tensor_tensor(v4(gd_r[:, 1]), vT_, tok(2, i), ALU.mult).then_inc(s("rhs"), 1)
            for tb in range(TB):
                E = work[tb % 2][5]
                masked(NBLK + tb, E, gmask(d, False))
                dve.wait_ge(s("qk"), at("qk", tb + 1))
                dve.wait_ge(s("D"), at("D", NBLK + tb + 1))
                dve.tensor_tensor(gd_AT[:, tb], bank[tb % 2][:, :], E, ALU.mult).then_inc(s("AT"), 1)
                dve.wait_ge(s("AT"), at("AT", tb + 1))
            dve.memset(gd_S, 0.0).then_inc(s("S0"), 1)
            dve.wait_ge(s("S0"), at("S0", 1))
            dve.wait_ge(s("u"), at("u", NBLK))
            glast = (stat[:, 0:48], vecs[:, 160:208])[d].rearrange("p (r c) -> p r c", r=GH)
            S = gd_S.rearrange("p (h n) -> p h n", h=GH)
            for n, c in enumerate(steps(d)):
                r, b = CH * (c % 2), c // 2
                rows_ = slice(r, r + CH)
                if n >= 2:
                    dve.wait_ge(s("kv"), at("kv", n - 1))
                kT_ = gd_kT[rows_, b].rearrange("p (h n) -> p h n", h=GH)
                dve.tensor_tensor(v4(gd_r[rows_, n % 2]), kT_, tok(4, b, rows_), ALU.mult).then_inc(s("k3"), 1)
                dve.wait_ge(s("wS"), at("wS", n + 1))
                if n >= CCH + 2:
                    dve.wait_ge(s("Av"), at("Av", n - CCH - 1))
                dve.tensor_tensor(gd_vn(n)[rows_], gd_u[rows_, b], bank[0][rows_, 0:GW], ALU.subtract).then_inc(s("v"), 1)
                if n >= CCH:
                    dve.wait_ge(s("qS"), at("qS", n - CCH + 1))
                dve.wait_ge(s("kv"), at("kv", n + 1))
                link(dve, dve.tensor_tensor(S, S, glast[0:GDN_D, :, c:c + 1].broadcast_to((GDN_D, GH, GDN_D)), ALU.mult))
                dve.tensor_tensor(gd_S, gd_S, bank[1][0:GDN_D, 0:GW], ALU.add).then_inc(s("S"), 1)
                dve.wait_ge(s("S"), at("S", n + 1))
                if n >= CCH:
                    tb = b - CB
                    o, t = gd_o[rows_, tb], nb[rows_, 2, 0:GW]
                    dve.tensor_tensor(v4(t), v4(bank[2][rows_, 0:GW]), tok(1, b, rows_), ALU.mult).then_inc(s("o"), 1)
                    dve.wait_ge(s("o"), at("o", 2 * (n - CCH) + 1))
                    if d:
                        link(dve, dve.tensor_tensor(o, o, t, ALU.add))
                        t = o
                    dve.wait_ge(s("Av"), at("Av", n - CCH + 1))
                    dve.tensor_tensor(o, t, bank[3][rows_, 0:GW], ALU.add).then_inc(s("o"), 1)
                    dve.wait_ge(s("o"), at("o", 2 * (n - CCH) + 2))

        gd_res = part(11776, TB, GW)

        def close_pe(pe, st, name, kt, rhs):
            fm_linear(pe, name, KD, kt, rhs, st + "_ps", st + "_h")
            for k in range(KD):
                sum_squares(pe, st + "n", k)

        def close_act(act, st):
            for k in range(KD):
                squares(act, st + "n", h, st + "_h", k)
            rstd_sqrt(act, st + "n")

        def close_dve(dve, st, m):
            for f in range(KD):
                dve.wait_ge(*after(st + "_ps", f + 1))
                dve.scalar_tensor_tensor(out=h[:, f], in0=bank[f % 4][:, :], scalar=mods[:, m, f, 0:1], in1=h[:, f],
                                         op0=ALU.mult, op1=ALU.add).then_inc(sem(st + "_h"), 1)
            rstd_var(dve, st + "n")
            rstd_recip(dve, st + "n")
            dve.wait_ge(*after(st + "_h", KD))

        ff2 = part(0, KF2, T)

        def mlp_pe(pe):
            pe.wait_ge(*after("mlp_x", KD))
            fm_linear(pe, "mlp1", KF2, KD, lambda k: xn[:, k], "mlp_up", "mlp_relu")
            pe.wait_ge(*after("mlp_ff", KF2))
            close_pe(pe, "mlp", "mlp2", KF2, lambda k: ff2[:, k])

        def mlp_act(act):
            for k in range(KD):
                act.wait_ge(*after("mlp_a", k + 1))
                act.activation(xn[:, k], xn[:, k], ACT.Identity, bias=mods[:, 3, k, 0:1]).then_inc(sem("mlp_x"), 1)
            for f in range(KF2):
                act.wait_ge(*after("mlp_up", f + 1))
                act.activation(ff2[:, f], bank[f % 4][:, :], ACT.Relu).then_inc(sem("mlp_relu"), 1)
            close_act(act, "mlp")

        def mlp_dve(dve):
            for k in range(KD):
                dve.scalar_tensor_tensor(out=xn[:, k], in0=h[:, k], scalar=column(G2, k), in1=rstd,
                                         op0=ALU.mult, op1=ALU.mult).then_inc(sem("mlp_a"), 1)
            for f in range(KF2):
                dve.wait_ge(*after("mlp_relu", f + 1))
                dve.tensor_tensor(ff2[:, f], ff2[:, f], ff2[:, f], ALU.mult).then_inc(sem("mlp_ff"), 1)
            close_dve(dve, "mlp", 5)
            apply_norm(dve, "nf", mix, "y")

        def block2_pe(pe):
            mod_pe(pe)
            hyena_pe(pe)
            gates_pe(pe)
            gla_pe(pe)
            heads_pe(pe, "gla", "gl_g", None)
            heads_flip(pe, "gla", gl_res)
            delta_in_pe(pe)
            delta_pe(pe, 0)
            delta_pe(pe, 1)
            heads_flip(pe, "gdh", gd_res)
            pe.wait_ge(*after("gdh_cat", 3))
            close_pe(pe, "out2", "out2", KD, lambda k: mix[:, k])
            mlp_pe(pe)

        def block2_act(act):
            mod_act(act)
            act.wait_ge(*after("x2_lat", KD))
            act.activation(column(vecs, 136), gain("a_log"), ACT.Exp).then_inc(sem("ea0"), 1)
            act.wait_ge(*after("ea0", 1))
            act.activation(column(vecs, 136), column(vecs, 136), ACT.Copy, scale=-1.0).then_inc(sem("ea"), 1)
            hyena_act(act)
            gates_act(act)
            gla_act(act)
            heads_gate(act, "gla", gate)
            heads_act(act, "gla", 2)
            delta_in_act(act)
            delta_act(act, 0)
            delta_act(act, 1)
            heads_act(act, "gdh", 5)
            close_act(act, "out2")
            mlp_act(act)

        def block2_dve(dve):
            mod_dve(dve)
            hyena_dve(dve)
            gates_dve(dve)
            gla_dve(dve)
            heads_dve(dve, "gla", gl_o, gate, "gla_gate", gl_res, "gla_ng")
            delta_in_dve(dve)
            delta_dve(dve, 0)
            delta_dve(dve, 1)
            heads_dve(dve, "gdh", gd_o, gd_gate, "gd_gate", gd_res, "gdn_ng")
            close_dve(dve, "out2", 2)
            mlp_dve(dve)

        def block2_pool(pool):
            def load(dst, name, at, n, done):
                pool.dma_start(dst, consts[:, CO[name] + at:CO[name] + at + n]).then_inc(done, 16)
            pool.wait_ge(*after("ffn1_ps", KD))
            pool.dma_start(big[:, 16384:16384 + KD * CTX], ctx_x[:, :]).then_inc(sem("cx_in"), 16)
            load(big[:, 0:8192], "dft", 0, 8192, sem("filt_in"))
            load(big[:, 8192:8192 + 5 * T], "filt", 0, 5 * T, sem("filt_in"))
            pool.dma_start(fw, filt[:, 0:1152]).then_inc(sem("filt_in"), 16)
            load(cst[:, 0:2 * P + TA + 3], "gla", 0, 2 * P + TA + 3, sem("gla_in"))
            pool.wait_ge(*after("conv", 4))
            pool.wait_ge(*after("hy_y", 4))
            pool.dma_start(gl_w2, filt[:, 1152:1152 + 2 * P]).then_inc(sem("gla_in"), 16)
            pool.wait_ge(*after("gla_normed", 1))
            pool.wait_ge(*after("gla_cat", 3))
            load(cst[:, 0:2048], "gdn_m", 0, 2048, sem("gdn_in"))
            load(big[:, 9728:9728 + 2048], "gdn_s", 0, 2048, sem("gdn_in"))


        block = ctx.enter_context(nc.Block())

        @block.tensor
        def _(pe):
            mixa_pe(pe)
            ffn_pe(pe, 0)
            mixb_pe(pe)
            ffn_pe(pe, 1)
            block2_pe(pe)

        @block.sync
        def _(sp):
            def const(dst, name, n):
                sp.dma_start(dst, consts[:, CO[name]:CO[name] + n]).then_inc(loaded, 16)
            for k in range(KD):
                sp.dma_start(h[:, k], x[:, k * T:(k + 1) * T]).then_inc(loaded, 16)
            sp.dma_start(small[:, :], smalls[:, :]).then_inc(loaded, 16)
            const(base[:, :], "base", 3 * P)
            const(cst[:, 0:2560], "mix_a", 2560)
            for u in range(n_units):
                if u == UNITS["up0"] + RING + 2:
                    sp.wait_ge(*after("a_ps", 1))
                    const(cst[:, 0:2560], "mix_b", 2560)
                if u >= RING:
                    sp.wait_ge(*unit_used[u - RING])
                sp.dma_start(ring[:, u % RING], weights[u]).then_inc(ring_full[u % RING], 16)
            for k in range(KD):
                sp.wait_ge(*after("y", k + 1))
                sp.dma_start(out[:, k * T:(k + 1) * T], mix[:, k]).then_inc(sem("stored"), 16)
            sp.wait_ge(*after("stored", 16 * KD))

        @block.scalar
        def _(act):
            mixa_act(act)
            ffn_act(act, 0)
            mixb_act(act)
            ffn_act(act, 1)
            block2_act(act)

        @block.vector
        def _(dve):
            mixa_dve(dve)
            ffn_dve(dve, 0, "g03")
            mixb_dve(dve)
            ffn_dve(dve, 1, "g13")
            block2_dve(dve)

        @block.gpsimd
        def _(pool):
            pool.wait_ge(loaded, 16 * (3 + KD))
            out_pool(pool, "a")
            out_pool(pool, "ffn0")
            out_pool(pool, "b")
            out_pool(pool, "ffn1")
            block2_pool(pool)


def kernel(**inputs):
    import concourse.bacc as bacc
    from concourse.bass_utils import run_bass_kernel_spmd

    i = {k: np.asarray(v) for k, v in inputs.items()}
    arrays = {
        "x": np.ascontiguousarray(i["x"][0].T.reshape(KD, P, T).transpose(1, 0, 2).reshape(P, KD * T)),
        "ctx_x": np.ascontiguousarray(i["ctx_2"][0].T.reshape(KD, P, CTX).transpose(1, 0, 2).reshape(P, KD * CTX)),
        "filt": filter_weights(i),
        "weights": np.concatenate([u for _, u in weight_list(i)]),
        "smalls": np.concatenate([a for _, a in small_list(i)], axis=1),
        "consts": np.concatenate([a for _, a in const_list()], axis=1),
    }
    nc = bacc.Bacc("TRN2", target_bir_lowering=False, num_devices=1)
    aps = {n: nc.dram_tensor(n, a.shape, F32, kind="ExternalInput").ap() for n, a in arrays.items()}
    out = nc.dram_tensor("out", (P, KD * T), F32, kind="ExternalOutput").ap()
    build(nc, out=out, **aps)
    r = run_bass_kernel_spmd(nc, [arrays], core_ids=[0])
    y = r.results[0]["out"]
    return y.reshape(P, KD, T).transpose(2, 1, 0).reshape(1, T, D)
```

```python
from contextlib import ExitStack
import math

import concourse.bass as bass
from concourse import mybir
import numpy as np

F32 = mybir.dt.float32
F32R = mybir.dt.float32r
ALU = mybir.AluOpType
ACT = mybir.ActivationFunctionType
AX = mybir.AxisListType

P = 128
T = 512
TB = T // P
D = 1024
KD = D // P
HD = 64
A_GROUPS = 3
A_SLOTS = 4
A_W = A_GROUPS * A_SLOTS * HD
B_HEADS = 16
D_FF = 2816
KF = D_FF // P
KH = KF // 2
EPS = 1e-6
NEG = -8e30
ROPE_DIM = 16
ROPE_THETA = 500000.0
CTX = 256
CB = CTX // P
TA = T + CTX
NBLK = TA // P
D_FF2 = 4096
KF2 = D_FF2 // P
KH2 = KF2 // 2
N_MOD = 6
CH = 64
NCH, CCH = TA // CH, CTX // CH
HY_C = 256
HY_EMB, HY_FH = 33, 64
GH = 4
GLA_DK, GLA_DV, GLA_RANK = 48, 96, 16
GLA_TAU = 16.0
GDN_D = 96
GW = GH * GDN_D
GDN_TAPS = 7
NFREQ = T
AG = {"gla_f": 0, "gla_b": 32, "decay": 64, "beta": 96}
RING = 4
PARTS = 3
UNIT = 1024


def fm_units(w):
    k, f = w.shape
    blocks = w.reshape(k // P, P, f // P, P).transpose(2, 0, 1, 3).reshape(-1, 8, P, P)
    return blocks.transpose(0, 2, 1, 3).reshape(-1, P, UNIT)


def tm_units(w):
    n = w.shape[1]
    u = w.reshape(4, 2, P, n).transpose(0, 2, 1, 3).reshape(4, P, 2 * n)
    return np.concatenate([u, np.zeros((4, P, UNIT - 2 * n), w.dtype)], axis=2)


def pad_cols(w, groups, size):
    parts = []
    for n, width in enumerate(groups):
        parts += [w[:, n * size:(n + 1) * size], np.zeros((w.shape[0], width - size), w.dtype)]
    return np.concatenate(parts, axis=1)


def vec(v):
    return v.reshape(-1, P).T


MIXER2 = ("hy", "ag", "gl_q", "gl_k", "gl_v", "gl_g", "gd_q", "gd_k", "gd_v", "gd_g")


def part_slots(units, n_units):
    first, end = units[MIXER2[0]], units["out2"]
    slot, before, last = {}, {}, {}
    for u in range(n_units):
        slot[u] = (u - first) % (PARTS - 1) if first <= u < end else u % PARTS
        before[u] = last.get(slot[u])
        last[slot[u]] = u
    return slot, before


def mod_units(w):
    return w.reshape(KD, P, N_MOD, D).transpose(2, 0, 1, 3).reshape(-1, P, D)


def weight_list(i):
    wq = i["w_qkv_a"][0]
    wf = i["w_kvf"]
    out = [("a_qk", fm_units(wq[:, :2 * A_W])),
           ("a_v0", tm_units(wq[:, 2 * A_W:2 * A_W + 384])), ("a_v1", tm_units(wq[:, 2 * A_W + 384:])),
           ("a_o", fm_units(i["w_o_a"][0]))]

    def halves(up_name, down_name, up, down):
        n, k = up.shape[1] // 2, down.shape[0] // 2
        return [unit for s in range(2)
                for unit in ((f"{up_name}{s}", fm_units(up[:, s * n:(s + 1) * n])),
                             (f"{down_name}{s}", fm_units(down[s * k:(s + 1) * k])))]

    def ffn(l):
        up = i["w_up"][l]
        pairs = np.concatenate([up[:, :D_FF].reshape(D, KF, 1, P), up[:, D_FF:].reshape(D, KF, 1, P)], axis=2)
        pairs = pairs.reshape(D, 2 * D_FF)
        return halves(f"up{l}_", f"down{l}_", pairs, i["w_down"][l])

    out += ffn(0)
    out += [("b_q", fm_units(i["w_q_b"][0])), ("b_k", fm_units(wf[:, :D])),
            ("b_f", fm_units(pad_cols(wf[:, 2 * D:], [P], B_HEADS))),
            ("b_v0", tm_units(wf[:, D:D + 512])), ("b_v1", tm_units(wf[:, D + 512:2 * D])),
            ("b_o", fm_units(i["w_o_b"][0]))]
    out += ffn(1)
    w = i["w_in_2"][0]
    gl, gd = w[:, 3 * HY_C:3 * HY_C + 1184], w[:, 3 * HY_C + 1184:]
    kw = GH * GLA_DK
    ranks = gl[:, 2 * kw + 2 * GW:]
    gates = gd[:, 4 * GW:]
    ag = np.concatenate([pad_cols(ranks, [32, 32], GLA_RANK), pad_cols(gates, [32, 32], 2 * GH)], axis=1)
    out += [("hy", fm_units(w[:, :3 * HY_C])),
            ("ag", fm_units(ag)),
            ("gl_q", fm_units(pad_cols(gl[:, :kw], [64] * GH, GLA_DK))),
            ("gl_k", fm_units(pad_cols(gl[:, kw:2 * kw], [64] * GH, GLA_DK))),
            ("gl_v", tm_units(gl[:, 2 * kw:2 * kw + GW])),
            ("gl_g", tm_units(gl[:, 2 * kw + GW:2 * kw + 2 * GW])),
            ("gd_q", fm_units(pad_cols(gd[:, :GW], [P] * GH, GDN_D))),
            ("gd_k", fm_units(pad_cols(gd[:, GW:2 * GW], [P] * GH, GDN_D))),
            ("gd_v", fm_units(gd[:, 2 * GW:3 * GW])),
            ("gd_g", tm_units(gd[:, 3 * GW:4 * GW])),
            ("out2", fm_units(i["w_out_2"][0]))]
    out += halves("mlp1_", "mlp2_", i["w_mlp1_2"][0], i["w_mlp2_2"][0])
    return out


def small_list(i):
    g = i["norm_gains"]
    out = [(f"g{l}{n}", vec(g[l, n])) for l in range(2) for n in range(4)]
    out += [("eps", np.full((P, 1), EPS, np.float32)), ("kvg", vec(i["kv_norm"]))]
    for l in range(2):
        cw = i["conv_w"][l]
        pair = lambda v: v.reshape(2, KF, P).transpose(2, 1, 0).reshape(P, 2 * KF)
        out += [(f"cw{l}{j}", pair(cw[j])) for j in range(3)] + [(f"cb{l}", pair(i["conv_b"][l]))]
    out += [("b_f", np.concatenate([i["b_f"], np.zeros(P - B_HEADS, np.float32)]).reshape(P, 1))]
    both = lambda a, b: np.stack([a, b], axis=2).reshape(P, -1)
    bm = vec(i["b_mod_2"][0])
    out += [("c", both(vec(i["c_2"]), vec(i["c_ctx_2"]))), ("b_mod", bm),
            ("n1", vec(i["norm1_g_2"])), ("n2", vec(i["norm2_g_2"])), ("nf", vec(i["final_norm_g_2"]))]
    out += [(f"hyw{j}", vec(i["hy_conv_w_2"][0, j])) for j in range(3)]
    out += [("hyb", vec(i["hy_conv_b_2"])), ("hyd", vec(i["hy_d_2"]))]

    def rows(parts):
        col = np.zeros((P, 1), np.float32)
        for at, v in parts:
            col[at:at + v.size, 0] = v.ravel()
        return col
    out += [("gla_b", vec(pad_cols(i["gla_b_a_2"].reshape(1, -1), [64] * 8, GLA_DK)))]
    cw = i["gdn_conv_w_2"][0]
    for j in range(GDN_TAPS):
        qk = pad_cols(cw[j:j + 1, :2 * GW], [P] * 8, GDN_D)
        out.append((f"gdw{j}", vec(np.concatenate([qk, cw[j:j + 1, 2 * GW:]], axis=1))))
    out += [("a_log", rows([(AG["decay"], i["gdn_a_log_2"])])), ("dt", rows([(AG["decay"], i["gdn_dt_bias_2"])])),
            ("gla_ng", np.broadcast_to(i["gla_norm_g_2"], (P, GLA_DV))),
            ("gdn_ng", np.broadcast_to(i["gdn_norm_g_2"], (P, GDN_D))),
            ("fb1", rows([(0, i["hy_f_b1_2"])])), ("fb2", rows([(0, i["hy_f_b2_2"])])),
            ("fq1", rows([(0, i["hy_sin_freq_2"][0, 0])])), ("fq2", rows([(0, i["hy_sin_freq_2"][0, 1])]))]
    return out


def filter_weights(i):
    a = np.zeros((P, HY_FH + HY_FH + 4 * HY_C), np.float32)
    a[:HY_EMB, :HY_FH] = i["hy_f_w1_2"][0]
    a[:HY_FH, HY_FH:2 * HY_FH] = i["hy_f_w2_2"][0]
    a[:HY_FH, 2 * HY_FH:] = i["hy_f_w3_2"][0]
    g = np.zeros((P, 2 * P), np.float32)
    for d in range(2):
        g[32 * d:32 * d + GLA_RANK] = pad_cols(i["gla_w_a2_2"][0, d], [64] * GH, GLA_DK)
    return np.concatenate([a, g], axis=1)


def const_list():
    f = np.float32
    eye = np.eye(P, dtype=f)
    inv = f(ROPE_THETA) ** (-np.arange(0, ROPE_DIM, 2, dtype=f) / f(ROPE_DIM))
    ang = (np.arange(T, dtype=f)[:, None] * inv[None, :]).astype(np.float64).T
    c, s = np.ones((P, T)), np.zeros((P, T))
    perm = np.zeros((P, P), f)
    for h in (0, HD):
        c[h:h + 8], c[h + 8:h + 16] = np.cos(ang), np.cos(ang)
        s[h:h + 8], s[h + 8:h + 16] = -np.sin(ang), np.sin(ang)
        for d in range(8):
            perm[h + d, h + 8 + d] = perm[h + 8 + d, h + d] = 1.0
    q, k = np.arange(P)[:, None], np.arange(P)[None, :]
    causal = np.where(q >= k, 0.0, NEG)
    zero = np.zeros((P, P))
    window = np.concatenate([np.full((P, P), NEG)] * 2 + [np.where(k >= q, 0.0, NEG), causal], axis=1)
    masks = [window]
    for r in (4, 16):
        same = (q - k) % r == 0
        masks.append(np.concatenate([np.where(same, 0.0, NEG)] * 3 + [np.where(same & (q >= k), 0.0, NEG)], axis=1))
    fox = np.concatenate([zero] * 3 + [causal], axis=1)
    sel = np.zeros((P, B_HEADS, P))
    for h in range(B_HEADS):
        sel[h, h] = sel[32 + h, h] = -8.0
    out = [("base", np.concatenate([eye, np.ones((P, P)), perm], axis=1)),
           ("mix_a", np.concatenate([c, s] + masks, axis=1)),
           ("mix_b", np.concatenate([fox, sel.reshape(P, -1)], axis=1))]
    n = np.arange(T)
    w = np.outer(n, 2 * np.arange(NFREQ) + 1) % (4 * T) * (np.pi / (2 * T))
    tiles = lambda a: a.reshape(-1, P, a.shape[1]).transpose(1, 0, 2).reshape(P, -1)
    out += [("dft", np.concatenate([tiles(m) for m in (np.cos(w), np.sin(w), np.cos(w).T / T, np.sin(w).T / T)], axis=1))]
    t = np.linspace(0.0, 1.0, T).astype(f)[:, None]
    bands = (HY_EMB - 1) // 2
    fr = np.linspace(1e-4, bands - 1, bands).astype(f)
    ang = ((f(2 * math.pi) * np.arange(T, dtype=f) / f(T))[:, None] * fr[None, :]).astype(f).astype(np.float64)
    z = np.concatenate([t, np.cos(ang), -np.sin(ang)], axis=1).T
    z = np.concatenate([z, np.zeros((P - HY_EMB, T))], axis=0)
    deltas = np.abs(np.linspace(math.log(1e-2) / 1.5, math.log(1e-2) / 0.3, HY_C)).astype(f)
    dec = np.exp(-(t * deltas[None, :]).astype(np.float64))
    back = dec.copy()
    back[0] = 0.0
    out += [("filt", np.concatenate([z, tiles(np.concatenate([dec, back], axis=1))], axis=1))]
    j, i = np.arange(P)[:, None], np.arange(P)[None, :]
    same = j // CH == i // CH
    m0 = [same & (i >= j), same & (i <= j)]
    reset = np.broadcast_to((np.arange(TA) % CH != 0).astype(f), (P, TA))
    fwd = np.zeros((P, 2))
    fwd[AG["decay"]:AG["decay"] + GH, 0] = 1
    fwd[AG["decay"] + GH:AG["decay"] + 2 * GH, 1] = 1
    sign = np.ones((P, 1))
    sign[AG["beta"]:] = -1
    out += [("gla", np.concatenate([m * 1.0 for m in m0] + [reset, fwd, sign], axis=1))]
    add = lambda m: np.where(m, 0.0, NEG)
    dm = []
    for d in range(2):
        later = (i > j) if d == 0 else (i < j)
        dm += [add(same & later), add(m0[d])]
    for d in range(2):
        m = 1
        while m < CH:
            pair = (i // (2 * m) == j // (2 * m)) & (i // m != j // m)
            dm.append((pair & ((i > j) if d == 0 else (i < j))) * 1.0)
            m *= 2
    sela, sell = np.zeros((P, 8, P)), np.zeros((P, 8, P))
    for r in range(8):
        sela[AG["decay"] + r, r] = 1
        sell[AG["decay"] + r, r] = sell[AG["beta"] + r, r] = 1
    out += [("gdn_m", np.concatenate(dm, axis=1)), ("gdn_s", np.concatenate([sela.reshape(P, -1), sell.reshape(P, -1)], axis=1))]
    return [(n, a.astype(f)) for n, a in out]


SHAPES = {
    "norm_gains": (2, 4, D), "w_qkv_a": (1, D, 3 * A_W), "w_o_a": (1, A_W, D), "w_q_b": (1, D, D),
    "w_o_b": (1, D, D), "kv_norm": (D,), "w_kvf": (D, 2 * D + B_HEADS), "b_f": (B_HEADS,),
    "w_up": (2, D, 2 * D_FF), "conv_w": (2, 3, 2 * D_FF), "conv_b": (2, 2 * D_FF), "w_down": (2, D_FF, D),
    "c_2": (1, D), "c_ctx_2": (D,), "norm1_g_2": (1, D), "norm2_g_2": (1, D), "w_mod_2": (1, D, N_MOD * D),
    "b_mod_2": (1, N_MOD * D), "w_in_2": (1, D, 3504), "w_out_2": (1, D, D), "hy_conv_w_2": (1, 3, 3 * HY_C),
    "hy_conv_b_2": (1, 3 * HY_C), "hy_f_b1_2": (1, HY_FH), "hy_f_b2_2": (1, HY_FH), "hy_sin_freq_2": (1, 2, HY_FH),
    "hy_d_2": (1, 2, HY_C), "gla_b_a_2": (1, 2, GH * GLA_DK), "gla_norm_g_2": (1, GLA_DV),
    "gdn_conv_w_2": (1, GDN_TAPS, 3 * GW), "gdn_a_log_2": (1, 2, GH), "gdn_dt_bias_2": (1, 2, GH),
    "gdn_norm_g_2": (1, GDN_D), "w_mlp1_2": (1, D, D_FF2), "w_mlp2_2": (1, D_FF2, D), "final_norm_g_2": (D,),
}


def starts(pairs, axis):
    at, out = 0, {}
    for name, a in pairs:
        out[name] = at
        at += a.shape[axis]
    return out, at


def places():
    z = {k: np.broadcast_to(np.float32(0), s) for k, s in SHAPES.items()}
    return starts(weight_list(z), 0), starts(small_list(z), 1), starts(const_list(), 1)


A_TILES = A_W // P
FFN_UP = [[(f"ffn{l}_{n}{s}", c) for s in range(2) for n, c in (("up", 2 * KH), ("ps", KD))] for l in range(2)]
SHARED = {
    "projected": [("a_qk", 2 * A_TILES), ("a_v", 2 * TB), ("a_ps", KD), *FFN_UP[0], ("b_qk", 2 * KD),
                  ("b_f", 1), ("b_v", 2 * TB), ("b_ps", KD), *FFN_UP[1],
                  ("hy_ps", 6), ("ag_ps", 2), ("glq_ps", 2), ("glk_ps", 4), ("glv_ps", NBLK), ("glz_ps", 8),
                  ("gla_gps", TB), ("gd_ps", 18), ("gd_gps", TB), ("out2_ps", KD), ("mlp_up0", KH2), ("mlp_ps0", KD),
                  ("mlp_up1", KH2), ("mlp_ps1", KD)],
    "turned": [("a_turned", 48), ("a_flip", A_TILES), ("b_turned", 64), ("b_flip", KD), ("y_turn", 2 * TB),
               ("gl_turn", NBLK), ("gla_flip", 3), ("gd_turn", 2 * NBLK), ("gd_gT", 1), ("gdh_flip", 3)],
    "scored": [("a_scores", 48), ("b_scores", 64), ("fl", 2), ("f_pos", 2 * TB), ("H_ps", 2 * TB), ("gl_s", 2 * TB),
               ("gd_ss", 12)],
    "weighted": [("a_values", 16), ("b_values", 64), ("U", 2 * TB), ("gl_o", TB)],
    "rotated": [("a_rot", 2 * A_TILES), ("conv", 4), ("gl_U", NCH)],
    "crossed": [("cx_sq_used", KD), ("gl_x", 2 * (NCH - CCH))],
    "copied": [("a_raw", 2 * A_TILES), ("a_vt", 2 * TB), ("b_qkt", 2 * KD), ("b_vt", 2 * TB),
               ("H", 2 * TB), ("yT", 2 * TB), ("ag", 2), ("glq", 2), ("glk", 4), ("glv", NBLK), ("gla_gate", TB), ("glkT", NBLK),
               ("gla_cat", 3), ("gd_gate", TB), ("gd_tm", 2 * NBLK), ("gdh_cat", 3), ("mlp_relu", KF2)],
    "hi": [("a_xnh", KD), ("a_fh", A_TILES), ("ffn0_xnh", KD), ("ffn0_ffh", KF), ("b_xnh", KD), ("b_xkvh", KD), ("b_fh", KD),
           ("ffn1_xnh", KD), ("ffn1_ffh", KF), ("out2_xh", KD), ("mlp_xh", KD), ("mlp_sh", KF2)],
    "lo": [("a_xnl", KD), ("a_fm", A_TILES), ("ffn0_xnl", KD), ("ffn0_ffl", KF), ("b_xnl", KD), ("b_xkvl", KD), ("b_fm", KD),
           ("ffn1_xnl", KD), ("ffn1_ffl", KF), ("x2al", KD), ("x2bl", KD), ("out2_xl", KD), ("mlp_xl", KD), ("mlp_sl", KF2)],
    "probs": [("a_probs", 48), ("b_probs", 64), ("fs", 2)],
    "pt_act": [("a_pt_act", 24), ("b_pt_act", 32)],
    "gelu": [("ffn0_gelu", KF), ("ffn1_gelu", KF)],
    "tap": [("ffn0_tap", 2 * KF), ("ffn1_tap", 2 * KF), ("hy_tap", 6), ("gd_tap", 18)],
    "looked_up": [("b_ln", 1), ("exp_c", 1), ("cx_sd", 1), ("ea0", 1), ("ea", 1), ("gt_ln", 1), ("gla_ln", 1),
                  ("gla_esc", 1), ("gla_ep", 1), ("gla_en", 1), ("gla_sd", 1), ("gd_sd", 12), ("gd_es", 3), ("gdh_sd", 1)],
    "squared": [("x2_lat", KD), ("cx_sq", KD), ("x2_ctx", KD), ("gd_sq", 12)],
    "mixed": [("a_mix", KD), ("ffn0_mix", 2 * KD), ("b_mix", KD), ("ffn1_mix", 2 * KD)],
    "tmp": [("a_tmp", KD), ("ffn0_tmp", KD), ("b_tmp", KD), ("ffn1_tmp", KD)],
    "residual": [(st + "_h", KD) for st in ("a", "ffn0", "b", "ffn1", "out2")] + [("mlp_h", 2 * KD)],
    "masked": [("a_masked", 48), ("b_masked", 64), ("f_used", 2 * TB)],
    "pt_dve": [("a_pt_dve", 24), ("b_pt_dve", 32)],
    "rows": [("a_rows", 16), ("b_rows", 64), ("spec", 2 * TB), ("gl_in", TB)],
    "max": [("a_max", 16), ("b_max", 64), ("Y", 2 * TB), ("gl_A", TB)],
    "convolved": [("ffn0_conv", 2 * KF), ("ffn1_conv", 2 * KF), ("hy_u", 6), ("gd_conv", 18)],
    "ff": [("ffn0_ff", KF), ("ffn1_ff", KF), ("mlp_sq", KF2)],
    "normed": [(n, KD) for n in ("a_xn", "ffn0_xn", "b_xn", "b_xkv", "ffn1_xn", "x2a", "x2b", "mlp_a", "y")],
    "stepped": [("b_z", 1), ("b_absz", 1), ("b_c", 1), ("silu_c", 1), ("mod", 1), ("cx_rstd", 1),
                ("gt_abs", 1), ("gla_abs", 1), ("gla_diff", 1), ("gt", 1), ("gla_qk", 4), ("gla_ss", 1), ("gla_normed", 1),
                ("gd_tg", 1), ("gd_gl", 1), ("gdh_ss", 1), ("gdh_normed", 1)],
    "roped": [("a_rope", 2 * A_TILES), ("f_sum", 4 * TB), ("glz", 8)],
    "scaled": [("a_rc", 2 * A_TILES), ("hy_y", 4), ("gd_normed", 12)],
}


def build(nc, x, ctx_x, weights, mod_w, smalls, filt, consts, out, dump=None):
    (UNITS, n_units), (SM, n_small), (CO, n_const) = places()

    ctx = ExitStack()
    with ctx:
        def sb(name, cols, rows=P):
            return ctx.enter_context(nc.sbuf_tensor(name, [rows, cols], F32))

        twin = {}

        def two_views(name, cols):
            with nc.sbuf_tensor(name, [P, cols], F32) as t:
                pass
            twin[t.name] = ctx.enter_context(nc.sbuf_tensor(name + "_r", [P, cols], F32R))
            return t

        def rounded(a):
            return bass.AP(tensor=twin[a.tensor.name], offset=a.offset, ap=a.ap)

        def value(a):
            return rounded(a).bitcast(F32)

        h_store = nc.dram_tensor("h_store", (P, KD * T), F32, kind="Internal").ap()
        sems = {}

        first = {}
        for shared, signals in SHARED.items():
            at = 0
            for name, total in signals:
                first[name] = (shared, at)
                at += total

        def sem(name):
            shared, _ = first.get(name, (name, 0))
            if shared not in sems:
                sems[shared] = ctx.enter_context(nc.semaphore(shared))
            return sems[shared]

        def after(name, count):
            return sem(name), first.get(name, (name, 0))[1] + count

        h = two_views("h", KD * T)[:, :].rearrange("p (k t) -> p k t", k=KD)
        xn_all = two_views("xn", KD * TA)
        xn = xn_all[:, 0:KD * T].rearrange("p (k t) -> p k t", k=KD)
        mix = two_views("mix", KD * T)[:, :].rearrange("p (k t) -> p k t", k=KD)
        ring = sb("ring", RING * UNIT)[:, :].rearrange("p (s n) -> p s n", s=RING)
        parts_all = two_views("parts", 2 * PARTS * UNIT)
        parts = parts_all[:, :].rearrange("p (x s n) -> p x s n", x=2, s=PARTS)
        w_hi, w_lo = parts[:, 0], parts[:, 1]
        small = sb("small", n_small)
        base = sb("base", 3 * P)
        cst = two_views("cst", 2816)
        nb = two_views("nb", 6 * T)[:, :].rearrange("p (k t) -> p k t", k=6)
        sq, tmp, rstd, var = nb[:, 0:2], nb[:, 2:4], nb[:, 4], nb[:, 5]
        stat = sb("stat", 64)
        BIG = 20992
        big = two_views("big", BIG)
        ident, ones, perm = base[:, 0:P], base[:, P:2 * P], base[:, 2 * P:3 * P]
        bank = [ctx.enter_context(nc.psum_tensor(f"bank{b}", [P, 512], F32)) for b in range(8)]

        def part(a, k, n):
            assert a + k * n <= BIG
            return big[:, a:a + k * n].rearrange("p (k n) -> p k n", k=k)

        def gain(name, k=0):
            return small[:, SM[name] + k:SM[name] + k + 1]

        ring_full = [sem(f"ring_full{s}") for s in range(RING)]
        slot_of, before = part_slots(UNITS, n_units)
        part_ready = sem("part_ready")
        product_done = {}
        small_in, cst_in = sem("small_in"), sem("cst_in")
        h_in = [sem(f"h_in{k}") for k in range(KD)]
        links = {}

        def link(eng, ins):
            s = sem(f"link_{eng.engine.name}" if hasattr(eng, "engine") else "link")
            links[s.name] = links.get(s.name, 0) + 1
            ins.then_inc(s, 1)
            eng.wait_ge(s, links[s.name])

        held = {}

        def grab(pe, b, reader, count):
            if b in held:
                pe.wait_ge(*held[b])
            held[b] = (reader, count)
            return bank[b]

        def take(pe, u):
            pe.wait_ge(part_ready, u + 1)

        def split_units(pool, first, last):
            for u in range(first, last):
                slot, w = slot_of[u], ring[:, u % RING]
                pool.wait_ge(ring_full[u % RING], 16 * (u // RING + 1))
                if before[u] is not None:
                    pool.wait_ge(*product_done[before[u]])
                pool.tensor_scalar(rounded(w_hi[:, slot]), w, 1.0, 0.0, ALU.mult, ALU.add).then_inc(sem("hi_ready"), 1)
                pool.wait_ge(sem("hi_ready"), u + 1)
                pool.tensor_tensor(rounded(w_lo[:, slot]), w, value(w_hi[:, slot]), ALU.subtract).then_inc(part_ready, 1)

        def weight(u, cols):
            return w_hi[:, slot_of[u], cols], w_lo[:, slot_of[u], cols]

        def hi_lo_product(pe, ps, w, x, start, stop):
            for n, (a, b) in enumerate(((0, 0), (0, 1), (1, 0))):
                mm = pe.matmul(ps, rounded(w[a]), rounded(x[b]), start=(start and n == 0), stop=(stop and n == 2))
            return mm

        def split_act(act, x, hi, k, ready, done):
            act.wait_ge(*ready)
            act.activation(rounded(hi[:, k]), x[:, k], ACT.Copy).then_inc(sem(done), 1)

        def split_dve(dve, x, hi, lo, k, ready, done):
            dve.wait_ge(*ready)
            dve.tensor_tensor(rounded(lo[:, k]), x[:, k], value(hi[:, k]), ALU.subtract).then_inc(sem(done), 1)

        def fm_linear(pe, name, chunks, kt, x, full, read, ready=None, then=None, full0=0, read0=0):
            u0 = UNITS[name]

            def product(ps, f, k):
                blk = f * kt + k
                u, j = u0 + blk // 8, blk % 8
                if j == 0:
                    take(pe, u)
                cols = slice(j * P, (j + 1) * P)
                mm = hi_lo_product(pe, ps[:, :], weight(u, cols),
                                   (x[0][:, k], x[1][:, k]), k == 0, k == kt - 1)
                product_done[u] = after(full, full0 + f + 1)
                if k == kt - 1:
                    mm.then_inc(sem(full), 1)

            lead = min(PARTS, chunks) if ready and kt == KD else 1
            first = [grab(pe, f % 4, *after(read, read0 + f + 1)) for f in range(lead)]
            for k in range(kt):
                if ready:
                    pe.wait_ge(*after(ready[0], ready[1] + k + 1))
                for f in range(lead):
                    product(first[f], f, k)
            for f in range(chunks):
                if f >= lead:
                    ps = grab(pe, f % 4, *after(read, read0 + f + 1))
                    for k in range(kt):
                        product(ps, f, k)
                if then:
                    then(f)

        def token_blocks(x):
            return lambda k, i: (x[0][:, k, i * P:(i + 1) * P], x[1][:, k, i * P:(i + 1) * P])

        unit_count = [0]

        def tm_linear(pe, name, n, x, blocks, full, read, at=0, full0=0):
            u0 = UNITS[name]
            banks = [(at + i) % 4 if blocks <= 4 else i for i in range(blocks)]
            ps = [grab(pe, b, *after(read, full0 + i + 1)) for i, b in enumerate(banks)]
            for u in range(u0, u0 + 4):
                take(pe, u)
                for i in range(blocks):
                    for j in range(2):
                        k = 2 * (u - u0) + j
                        mm = hi_lo_product(pe, ps[i][:, 0:n], x(k, i), weight(u, slice(j * n, (j + 1) * n)),
                                           k == 0, k == KD - 1)
                    if u == u0 + 3:
                        mm.then_inc(sem(full), 1)
                if u == u0 + 3:
                    product_done[u] = after(full, full0 + blocks)
                else:
                    unit_count[0] += 1
                    mm.then_inc(sem("unit_done"), 1)
                    product_done[u] = (sem("unit_done"), unit_count[0])

        NORMS = ["in", "a", "an", "ffn0", "ffn0n", "b", "bn", "ffn1", "ffn1n", "out2n", "mlpn"]
        squared, summed = sem("norm_squared"), sem("norm_summed")
        sd_ready, rstd_ready = sem("norm_sd"), sem("norm_rstd")

        def squares(act, norm, src, ready, k, ready0=0):
            n = NORMS.index(norm) * KD + k
            if ready == "h_in":
                act.wait_ge(h_in[k], 16)
            else:
                act.wait_ge(*after(ready, ready0 + k + 1))
            if k >= 2:
                act.wait_ge(summed, n - 1)
            act.activation(sq[:, k % 2], src[:, k], ACT.Square).then_inc(squared, 1)

        ADDED = ["a", "ffn0", "b", "ffn1"]
        added = lambda norm, k: (sem("norm_added"), (KD - 1) * ADDED.index(norm) + k)

        def squares_added(act, norm, ready, k, ready0=0):
            act.wait_ge(*after(ready, ready0 + k + 1))
            if k == 0:
                act.wait_ge(rstd_ready, NORMS.index(norm))
            if k >= 3:
                act.wait_ge(*added(norm, k - 2))
            act.activation(sq[:, k % 2] if k else var, mix[:, k], ACT.Square).then_inc(squared, 1)

        def add_squares(dve, norm, k):
            dve.wait_ge(squared, NORMS.index(norm) * KD + k + 1)
            if k > 1:
                dve.wait_ge(*added(norm, k - 1))
            dve.tensor_tensor(var, var, sq[:, k % 2], ALU.add).then_inc(sem("norm_added"), 1)

        def sum_added(pe, norm):
            grab(pe, 7, rstd_ready, NORMS.index(norm) + 1)
            pe.wait_ge(*added(norm, KD - 1))
            pe.matmul(bank[7][:, :], ones, var, start=True, stop=True).then_inc(summed, KD)

        def sum_squares(pe, norm, k):
            n = NORMS.index(norm)
            if k == 0:
                grab(pe, 7, rstd_ready, n + 1)
            pe.wait_ge(squared, n * KD + k + 1)
            pe.matmul(bank[7][:, :], ones, sq[:, k % 2], start=(k == 0), stop=(k == KD - 1)).then_inc(summed, 1)

        def rstd_sqrt(act, norm):
            act.wait_ge(summed, (NORMS.index(norm) + 1) * KD)
            act.activation(var, bank[7][:, :], ACT.Sqrt, bias=gain("eps"), scale=1.0 / D).then_inc(sd_ready, 1)

        def rstd_recip(dve, norm):
            n = NORMS.index(norm) + 1
            dve.wait_ge(sd_ready, n)
            dve.reciprocal(rstd, var).then_inc(rstd_ready, 1)
            dve.wait_ge(rstd_ready, n)

        def norm_dve(dve, g, hi, lo, st):
            for k in range(KD + 1):
                if k < KD:
                    dve.scalar_tensor_tensor(out=lo[:, k], in0=h[:, k], scalar=gain(g, k), in1=rstd,
                                             op0=ALU.mult, op1=ALU.mult).then_inc(sem(st), 1)
                if k:
                    split_dve(dve, lo, hi, lo, k - 1, after(st + "h", k), st + "l")

        def norm_act(act, hi, lo, st):
            for k in range(KD):
                split_act(act, lo, hi, k, after(st, k + 1), st + "h")

        def out_pe(pe, st, name, kt, x, ready, half=1, ps=None, mod=None):
            fm_linear(pe, name, KD, kt, x, ps or st + "_ps", st + "_mix", ready=ready, read0=KD * (half if ps else 0),
                      then=mod)
            if half:
                sum_added(pe, st)
                for k in range(KD):
                    sum_squares(pe, st + "n", k)

        def out_act(act, st, mix0=0):
            for k in range(KD):
                squares_added(act, st, st + "_mix", k, mix0)
            rstd_sqrt(act, st)
            for k in range(KD):
                squares(act, st + "n", h, st + "_h", k)
            rstd_sqrt(act, st + "n")

        def out_dve(dve, st, g, half=None, then=None):
            ps = st + "_ps" + ("" if half is None else str(half))
            for f in range(KD + 1):
                if then and f < KD:
                    then(f)
                if f >= 2 and half != 0:
                    add_squares(dve, st, f - 1)
                if f == KD:
                    break
                dve.wait_ge(*after(ps, f + 1))
                if half == 1:
                    dve.tensor_tensor(mix[:, f], mix[:, f], bank[f % 4][:, :], ALU.add).then_inc(sem(st + "_mix"), 1)
                else:
                    dve.tensor_copy(mix[:, f], bank[f % 4][:, :]).then_inc(sem(st + "_mix"), 1)
            if half == 0:
                return
            rstd_recip(dve, st)
            dve.wait_ge(*after(st + "_mix", 2 * KD if half == 1 else KD))
            for k in range(KD + 1):
                if k < KD:
                    dve.scalar_tensor_tensor(out=tmp[:, k % 2], in0=mix[:, k], scalar=gain(g, k), in1=rstd,
                                             op0=ALU.mult, op1=ALU.mult).then_inc(sem(st + "_tmp"), 1)
                if k:
                    dve.wait_ge(*after(st + "_tmp", k))
                    dve.tensor_tensor(h[:, k - 1], h[:, k - 1], tmp[:, (k - 1) % 2], ALU.add).then_inc(sem(st + "_h"), 1)
                    dve.wait_ge(*after(st + "_h", k))
            rstd_recip(dve, st + "n")

        def fm_multi(pe, name, chunks, parts, full, read, blocks=KD):
            u0 = UNITS[name]
            for f in range(chunks):
                for p, (rhs, n) in enumerate(parts):
                    i = f * len(parts) + p
                    ps = grab(pe, i % 4, *after(read, i + 1))
                    take(pe, u0 + f)
                    for k in range(KD):
                        mm = hi_lo_product(pe, ps[:, 0:n], weight(u0 + f, slice(k * P, (k + 1) * P)), rhs(k),
                                           k == 0, k == KD - 1)
                    mm.then_inc(sem(full), 1)
                product_done[u0 + f] = after(full, (f + 1) * len(parts))

        ff_hi, ff_lo = part(0, KH, T), part(KH * T, KH, T)
        cv, ge = part(2 * KH * T, 4, T), part((2 * KH + 4) * T, 2, T)
        ffn_x = (xn, part((2 * KH + 6) * T, KD, T))

        def ffn_pe(pe, l):
            st = f"ffn{l}"
            for s in range(2):
                fm_linear(pe, f"up{l}_{s}", 2 * KH, KD, ffn_x, f"{st}_up{s}", st + "_conv", read0=2 * KH * s,
                          ready=None if s else (st + "_xnl", 0))
                fm = (lambda f, s=s: mod_sums(pe, s, f)) if l else None
                out_pe(pe, st, f"down{l}_{s}", KH, (ff_hi, ff_lo), (st + "_ffl", KH * s), half=s, ps=f"{st}_ps{s}", mod=fm)
            if l:
                mod_vector(pe, 3)
                mod_vector(pe, 5)

        def ffn_act(act, l):
            st = f"ffn{l}"
            for s in range(2):
                for j in range(KH + 2):
                    if j < KH:
                        for i in (2 * j, 2 * j + 1):
                            act.wait_ge(*after(f"{st}_up{s}", i + 1))
                            if j >= 2:
                                act.wait_ge(*after(st + "_ff", KH * s + j - 1))
                            act.activation(cv[:, i % 4], bank[i % 4][:, :], ACT.Identity,
                                           bias=gain(f"cb{l}", 2 * KH * s + i), scale=gain(f"cw{l}2", 2 * KH * s + i))\
                               .then_inc(sem(st + "_tap"), 1)
                    if 1 <= j <= KH:
                        act.wait_ge(*after(st + "_conv", 2 * KH * s + 2 * j - 1))
                        if j >= 3:
                            act.wait_ge(*after(st + "_ff", KH * s + j - 2))
                        act.activation(ge[:, (j - 1) % 2], cv[:, (2 * j - 2) % 4], ACT.Gelu_apprx_tanh)\
                           .then_inc(sem(st + "_gelu"), 1)
                    if j >= 2:
                        split_act(act, ff_lo, ff_hi, j - 2, after(st + "_ff", KH * s + j - 1), st + "_ffh")
            out_act(act, st, KD)

        def ffn_dve(dve, l, g):
            st = f"ffn{l}"
            for s in range(2):
                for j in range(KH + 2):
                    if j < KH:
                        for i in (2 * j, 2 * j + 1):
                            ps, c, w = bank[i % 4], cv[:, i % 4], 2 * KH * s + i
                            dve.wait_ge(*after(st + "_tap", w + 1))
                            link(dve, dve.scalar_tensor_tensor(
                                out=c[:, 1:T], in0=ps[:, 0:T - 1], scalar=gain(f"cw{l}1", w), in1=c[:, 1:T],
                                op0=ALU.mult, op1=ALU.add))
                            dve.scalar_tensor_tensor(
                                out=c[:, 2:T], in0=ps[:, 0:T - 2], scalar=gain(f"cw{l}0", w), in1=c[:, 2:T],
                                op0=ALU.mult, op1=ALU.add).then_inc(sem(st + "_conv"), 1)
                    if 1 <= j <= KH:
                        dve.wait_ge(*after(st + "_gelu", KH * s + j))
                        dve.wait_ge(*after(st + "_conv", 2 * KH * s + 2 * j))
                        dve.tensor_tensor(ff_lo[:, j - 1], ge[:, (j - 1) % 2], cv[:, (2 * j - 1) % 4], ALU.mult)\
                           .then_inc(sem(st + "_ff"), 1)
                    if j >= 2:
                        split_dve(dve, ff_lo, ff_hi, ff_lo, j - 2, after(st + "_ffh", KH * s + j - 1), st + "_ffl")
                out_dve(dve, st, g, half=s, then=(lambda f, s=s: mod_products(dve, s, f)) if l else None)

        MIXED = (0, 2, 3, 1)

        def attention(st, tasks, G, qT, kT, vT, oT, masks, width, work, sel=None):
            Sb = big[:, work:work + 3 * G * T].rearrange("p (b g n) -> p b g n", b=3, g=G)
            PT = big[:, work + 3 * G * T:work + 5 * G * T].rearrange("p (b g n) -> p b g n", b=2, g=G)
            n = len(tasks)
            mx = lambda t: stat[:, 16 * (t % 4):16 * (t % 4) + G]
            nm = lambda t: stat[:, 16 * (t % 4) + 4:16 * (t % 4) + 5]
            ls = lambda t: stat[:, 16 * (t % 4) + 8:16 * (t % 4) + 8 + G]
            rl = lambda t: stat[:, 16 * (t % 4) + 12:16 * (t % 4) + 13]
            mm_ = lambda t: stat[:, 16 * (t % 4) + 13:16 * (t % 4) + 14]
            lsum = lambda t: stat[:, 16 * (t % 4) + 14:16 * (t % 4) + 15]
            on_act = lambda j: j % 2 == 0
            s = lambda x: sem(f"{st}_{x}")
            at = lambda x, count: after(f"{st}_{x}", count)

            def scores(pe, t):
                tb, heads = tasks[t]
                w = (tb + 1) * P
                for g, hd in enumerate(heads):
                    j = t * G + g
                    ps = grab(pe, j % 4, *at("masked", j + 1))
                    r = HD * (hd % 2)
                    mm = pe.matmul(ps[:, 0:w], qT[r:r + HD, hd // 2, tb * P:(tb + 1) * P],
                                   kT[r:r + HD, hd // 2, 0:w], start=True, stop=(sel is None))
                    if sel is not None:
                        mm = pe.matmul(ps[:, 0:w], rounded(sel[0][:, hd]), rounded(sel[1][:, 0:w]),
                                       start=False, stop=True)
                    mm.then_inc(s("scores"), 1)

            def turn(pe, t):
                tb, heads = tasks[t]
                for g in range(G):
                    j = t * G + g
                    ps = grab(pe, 4 + j % 2, *at("pt_act" if on_act(j) else "pt_dve", j // 2 + 1))
                    pe.wait_ge(*at("probs", j + 1))
                    for kb in range(tb + 1):
                        mm = pe.transpose(ps[:, kb * P:(kb + 1) * P], Sb[:, t % 3, g, kb * P:(kb + 1) * P], ident)
                    mm.then_inc(s("turned"), 1)

            def values(pe, t):
                tb, heads = tasks[t]
                ps = grab(pe, 6 + t % 2, *at("rows", t + 1))
                for g, hd in enumerate(heads):
                    j = t * G + g
                    if on_act(j):
                        pe.wait_ge(*at("pt_act", j // 2 + 1))
                    else:
                        pe.wait_ge(*at("pt_dve", j // 2 + 1))
                    for kb in range(tb + 1):
                        mm = pe.matmul(ps[:, g * HD:(g + 1) * HD], PT[:, t % 2, g, kb * P:(kb + 1) * P],
                                       vT[:, kb, hd * HD:(hd + 1) * HD], start=(kb == 0), stop=(kb == tb))
                mm.then_inc(s("values"), 1)

            def rows_pe(pe):
                scores(pe, 0)
                scores(pe, 1)
                for t in range(n + 1):
                    if t + 2 < n:
                        scores(pe, t + 2)
                    if t < n:
                        turn(pe, t)
                    if t >= 1:
                        values(pe, t - 1)

            def take_pt(eng, t, act):
                tb, _ = tasks[t]
                for g in range(G):
                    j = t * G + g
                    if on_act(j) != act:
                        continue
                    eng.wait_ge(*at("turned", j + 1))
                    if t >= 2:
                        eng.wait_ge(*at("values", t - 1))
                    w = (tb + 1) * P
                    if act:
                        ins = eng.activation(PT[:, t % 2, g, 0:w], bank[4 + j % 2][:, 0:w], ACT.Copy)
                    else:
                        ins = eng.tensor_copy(PT[:, t % 2, g, 0:w], bank[4 + j % 2][:, 0:w])
                    ins.then_inc(s("pt_act" if act else "pt_dve"), 1)

            def rows_act(act):
                for t in range(-1, n):
                    if t + 1 < n:
                        tb, _ = tasks[t + 1]
                        act.wait_ge(*at("max", t + 2))
                        if t >= 3:
                            act.wait_ge(*at("rows", t - 2))
                        for g in range(G):
                            sbt = Sb[:, (t + 1) % 3, g, 0:(tb + 1) * P]
                            act.activation(sbt, sbt, ACT.Exp, bias=nm(t + 1), scale=HD ** -0.5,
                                           accum_out=ls(t + 1)[:, g:g + 1]).then_inc(s("probs"), 1)
                    if t >= 0:
                        take_pt(act, t, True)

            def row_max(dve, t):
                tb, _ = tasks[t]
                w = (tb + 1) * P
                for g in range(G):
                    j = t * G + g
                    dve.wait_ge(*at("scores", j + 1))
                    if t >= 3 and g == 0:
                        dve.wait_ge(*at("turned", (t - 2) * G))
                    dve.tensor_tensor_reduce(out=Sb[:, t % 3, g, 0:w], in0=bank[j % 4][:, 0:w],
                                                   in1=masks[:, g, T - w:T], scale=1.0, scalar=-3e38,
                                                   op0=ALU.add, op1=ALU.max, accum_out=mx(t)[:, g:g + 1])\
                       .then_inc(s("masked"), 1)
                dve.wait_ge(*at("masked", (t + 1) * G))
                m = mx(t)
                if G > 1:
                    link(dve, dve.tensor_reduce(mm_(t), mx(t), AX.X, ALU.max))
                    m = mm_(t)
                dve.tensor_scalar(nm(t), m, -(HD ** -0.5), None, ALU.mult).then_inc(s("max"), 1)

            def row_out(dve, t):
                tb, heads = tasks[t]
                dve.wait_ge(*at("probs", (t + 1) * G))
                tot = ls(t)
                if G > 1:
                    link(dve, dve.tensor_reduce(lsum(t), ls(t), AX.X, ALU.add))
                    tot = lsum(t)
                link(dve, dve.reciprocal(rl(t), tot))
                dve.wait_ge(*at("values", t + 1))
                dst = oT[:, tb].rearrange("p (g c) -> p g c", g=G)[:, :, (heads[0] * HD):(heads[0] + 1) * HD]
                dve.tensor_scalar(dst, bank[6 + t % 2][:, 0:G * HD].rearrange("p (g c) -> p g c", g=G),
                                  rl(t), None, ALU.mult).then_inc(s("rows"), 1)

            def rows_dve(dve):
                row_max(dve, 0)
                row_max(dve, 1)
                for t in range(n + 1):
                    if t + 2 < n:
                        row_max(dve, t + 2)
                    if t < n:
                        take_pt(dve, t, False)
                    if t >= 1:
                        row_out(dve, t - 1)
            return rows_pe, rows_act, rows_dve, n

        def flip_pe(pe, st, src, chunks, ready, count):
            pe.wait_ge(*after(ready, count))
            for c in range(chunks):
                ps = grab(pe, 4 + c % 2, *after(st + "_fm", c + 1))
                for tb in range(TB):
                    mm = pe.transpose(ps[:, tb * P:(tb + 1) * P], src[:, tb, c * P:(c + 1) * P], ident)
                mm.then_inc(sem(st + "_flip"), 1)

        def flip_act(act, st, hi, chunks):
            for c in range(chunks):
                act.wait_ge(*after(st + "_flip", c + 1))
                act.activation(rounded(hi[:, c]), bank[4 + c % 2][:, :], ACT.Copy).then_inc(sem(st + "_fh"), 1)

        def flip_dve(dve, st, hi, lo, chunks):
            for c in range(chunks):
                dve.wait_ge(*after(st + "_fh", c + 1))
                dve.tensor_tensor(rounded(lo[:, c]), bank[4 + c % 2][:, :], value(hi[:, c]), ALU.subtract)\
                   .then_inc(sem(st + "_fm"), 1)

        KA = A_W // P
        a_q, a_k = part(0, KA, T), part(KA * T, KA, T)
        a_v = part(2 * KA * T, TB, A_W)
        a_o = part(2 * KA * T + TB * A_W, TB, A_W)
        a_work = 2 * KA * T + 2 * TB * A_W
        rope_c, rope_s = cst[:, 0:T], cst[:, T:2 * T]
        a_masks = cst[:, 2 * T:5 * T].rearrange("p (g n) -> p g n", g=3)
        a_tasks = [(tb, [g * A_SLOTS + s for g in range(A_GROUPS)]) for s in range(A_SLOTS) for tb in MIXED]
        a_pe, a_act, a_dve, a_n = attention("a", a_tasks, A_GROUPS, a_q, a_k, a_v, a_o, a_masks, T, a_work)
        a_x = (xn, mix)
        a_oT = (xn, part(0, KA, T))

        def mixa_pe(pe):
            pe.wait_ge(small_in, 32)
            for k in range(KD):
                sum_squares(pe, "in", k)
            def rotate(f):
                ps = grab(pe, 4 + f % 2, *after("a_rope", f + 1))
                pe.wait_ge(*after("a_raw", f + 1))
                pe.matmul(ps[:, :], perm, nb[:, f % 2], start=True, stop=True).then_inc(sem("a_rot"), 1)
            fm_linear(pe, "a_qk", 2 * KA, KD, a_x, "a_qk", "a_raw", ready=("a_xnl", 0),
                      then=lambda f: rotate(f - 1) if f else None)
            rotate(2 * KA - 1)
            for n in range(2):
                tm_linear(pe, f"a_v{n}", 384, token_blocks(a_x), TB, "a_v", "a_vt", full0=n * TB)
            pe.wait_ge(*after("a_rope", 2 * KA))
            pe.wait_ge(*after("a_vt", 2 * TB))
            a_pe(pe)
            flip_pe(pe, "a", a_o, KA, "a_rows", a_n)
            out_pe(pe, "a", "a_o", KA, a_oT, ("a_fm", 0))

        def mixa_act(act):
            act.wait_ge(small_in, 32)
            for k in range(KD):
                squares(act, "in", h, "h_in", k)
            rstd_sqrt(act, "in")
            norm_act(act, *a_x, "a_xn")
            for f in range(2 * KA):
                act.wait_ge(*after("a_qk", f + 1))
                if f >= 2:
                    act.wait_ge(*after("a_rope", f - 1))
                else:
                    act.wait_ge(summed, KD)
                act.activation(nb[:, f % 2], bank[f % 4][:, :], ACT.Copy).then_inc(sem("a_raw"), 1)
            for i in range(2 * TB):
                act.wait_ge(*after("a_v", i + 1))
                act.activation(a_v[:, i % TB, (i // TB) * 384:(i // TB + 1) * 384], bank[i % 4][:, 0:384],
                               ACT.Copy).then_inc(sem("a_vt"), 1)
            a_act(act)
            flip_act(act, "a", a_oT[0], KA)
            out_act(act, "a")
            norm_act(act, *ffn_x, "ffn0_xn")

        def mixa_dve(dve):
            dve.wait_ge(small_in, 32)
            for k in range(KD):
                dve.wait_ge(h_in[k], 16)
            rstd_recip(dve, "in")
            norm_dve(dve, "g00", *a_x, "a_xn")
            dve.wait_ge(cst_in, 16)
            for f in range(2 * KA):
                dst = a_q[:, f] if f < KA else a_k[:, f - KA]
                dve.wait_ge(*after("a_raw", f + 1))
                dve.tensor_tensor(dst, nb[:, f % 2], rope_c, ALU.mult).then_inc(sem("a_rc"), 1)
                dve.wait_ge(*after("a_rot", f + 1))
                link(dve, dve.tensor_tensor(tmp[:, f % 2], bank[4 + f % 2][:, :], rope_s, ALU.mult))
                dve.wait_ge(*after("a_rc", f + 1))
                dve.tensor_tensor(dst, dst, tmp[:, f % 2], ALU.add).then_inc(sem("a_rope"), 1)
            a_dve(dve)
            flip_dve(dve, "a", *a_oT, KA)
            out_dve(dve, "a", "g01")
            norm_dve(dve, "g02", *ffn_x, "ffn0_xn")

        b_q, b_k = part(0, KD, T), part(KD * T, KD, T)
        b_v, b_o = part(2 * KD * T, TB, D), part(2 * KD * T + TB * D, TB, D)
        b_work = 2 * KD * T + 2 * TB * D
        b_mask = cst[:, 0:T].rearrange("p (g n) -> p g n", g=1)
        b_sel = cst[:, T:T + B_HEADS * P].rearrange("p (h n) -> p h n", h=B_HEADS)
        b_c = nb[:, 0]
        b_tasks = [(tb, [hd]) for hd in range(B_HEADS) for tb in MIXED]
        b_pe, b_act, b_dve, b_n = attention("b", b_tasks, 1, b_q, b_k, b_v, b_o, b_mask, T, b_work, sel=(b_sel, b_c))
        b_x, b_xkv = (xn, mix), (part(12288, KD, T), part(12288 + KD * T, KD, T))
        b_oT = (xn, part(0, KD, T))

        def mixb_pe(pe):
            pe.wait_ge(cst_in, 32)
            fm_linear(pe, "b_q", KD, KD, b_x, "b_qk", "b_qkt", ready=("b_xnl", 0))
            fm_linear(pe, "b_k", KD, KD, b_xkv, "b_qk", "b_qkt", full0=KD, read0=KD, ready=("b_xkvl", 0))
            fm_linear(pe, "b_f", 1, KD, b_xkv, "b_f", "b_z")
            for n in range(2):
                tm_linear(pe, f"b_v{n}", 512, token_blocks(b_xkv), TB, "b_v", "b_vt", at=1, full0=n * TB)
            pe.wait_ge(*after("b_qkt", 2 * KD))
            pe.wait_ge(*after("b_vt", 2 * TB))
            pe.wait_ge(*after("b_c", 1))
            pe.wait_ge(sem("b_sel"), 1)
            b_pe(pe)
            flip_pe(pe, "b", b_o, KD, "b_rows", b_n)
            out_pe(pe, "b", "b_o", KD, b_oT, ("b_fm", 0))

        def mixb_act(act):
            norm_act(act, *b_x, "b_xn")
            norm_act(act, *b_xkv, "b_xkv")
            for f in range(2 * KD):
                act.wait_ge(*after("b_qk", f + 1))
                dst = b_q[:, f] if f < KD else b_k[:, f - KD]
                act.activation(dst, bank[f % 4][:, :], ACT.Copy).then_inc(sem("b_qkt"), 1)
            act.wait_ge(*after("b_absz", 1))
            z = nb[0:B_HEADS, 3]
            link(act, act.activation(z, z, ACT.Exp, scale=-1.0))
            act.activation(z, z, ACT.Ln, bias=1.0).then_inc(sem("b_ln"), 1)
            for i in range(2 * TB):
                act.wait_ge(*after("b_v", i + 1))
                b = (1 + i) % 4
                act.activation(b_v[:, i % TB, (i // TB) * 512:(i // TB + 1) * 512], bank[b][:, :], ACT.Copy)\
                   .then_inc(sem("b_vt"), 1)
            act.wait_ge(cst_in, 32)
            act.activation(rounded(cst[:, T:T + B_HEADS * P]), cst[:, T:T + B_HEADS * P], ACT.Copy)\
               .then_inc(sem("b_sel"), 1)
            b_act(act)
            flip_act(act, "b", b_oT[0], KD)
            mod_start_act(act)
            out_act(act, "b")
            norm_act(act, *ffn_x, "ffn1_xn")

        def mixb_dve(dve):
            norm_dve(dve, "g10", *b_x, "b_xn")
            norm_dve(dve, "kvg", *b_xkv, "b_xkv")
            z, az, one = nb[0:B_HEADS, 2], nb[0:B_HEADS, 3], nb[0:B_HEADS, 4]
            dve.wait_ge(*after("b_f", 1))
            dve.tensor_scalar(z, bank[0][0:B_HEADS, :], small[0:B_HEADS, SM["b_f"]:SM["b_f"] + 1], None, ALU.add)\
               .then_inc(sem("b_z"), 1)
            dve.wait_ge(*after("b_z", 1))
            dve.scalar_tensor_tensor(out=az, in0=z, scalar=-1.0, in1=z, op0=ALU.mult, op1=ALU.max).then_inc(sem("b_absz"), 1)
            dve.wait_ge(*after("b_absz", 1))
            link(dve, dve.tensor_scalar(z, z, 0.0, None, ALU.min))
            dve.wait_ge(*after("b_xkv", KD))
            link(dve, dve.memset(one, 1.0))
            dve.wait_ge(*after("b_ln", 1))
            link(dve, dve.tensor_tensor(az, z, az, ALU.subtract))
            link(dve, dve.tensor_tensor_scan(z, one, az, 0.0, ALU.mult, ALU.add))
            dve.wait_ge(cst_in, 32)
            c_rows = lambda a, b: rounded(b_c[a:b])
            link(dve, dve.tensor_scalar(c_rows(0, P), cst[:, 0:T], 0.0, None, ALU.mult))
            link(dve, dve.tensor_copy(c_rows(0, B_HEADS), z))
            dve.tensor_tensor(c_rows(32, 32 + B_HEADS), z, value(b_c[0:B_HEADS]), ALU.subtract).then_inc(sem("b_c"), 1)
            b_dve(dve)
            flip_dve(dve, "b", *b_oT, KD)
            out_dve(dve, "b", "g11")
            norm_dve(dve, "g12", *ffn_x, "ffn1_xn")
            mod_start_dve(dve)

        X2 = xn_all[:, :].rearrange("p (k t) -> p k t", k=KD)
        vecs = sb("vecs", 208)
        silu_c, mod_l, mod_c = vecs[:, 0:2 * KD], vecs[:, 2 * KD:8 * KD], vecs[:, 8 * KD:10 * KD]
        G1l, G1c, G2 = (vecs[:, 112 + 8 * n:120 + 8 * n] for n in range(3))
        mod_lat, mod_ctx = mod_l.rearrange("p (m k) -> p m k", m=N_MOD), mod_c.rearrange("p (m k) -> p m k", m=2)
        cx = mix[:, 0:KD * CTX // T].rearrange("p k t -> p (k t)").rearrange("p (k t) -> p k t", k=KD)
        def ctx_lo(k):
            return parts[:, k // 4, PARTS - 1, (k % 4) * CTX:(k % 4 + 1) * CTX]
        lat = (lambda k: (X2[:, k, CTX:TA], h[:, k]), T)
        ctxp = (lambda k: (X2[:, k, 0:CTX], ctx_lo(k)), CTX)

        def X2_block(k, b):
            lo = ctx_lo(k)[:, b * P:(b + 1) * P] if b < CB else h[:, k, (b - CB) * P:(b - CB + 1) * P]
            return X2[:, k, b * P:(b + 1) * P], lo

        def column(v, k):
            return v[:, k:k + 1]

        def small_cols(name, n):
            return small[:, SM[name]:SM[name] + n]

        mod_ring = cst[:, 0:2 * UNIT].rearrange("p (s n) -> p s n", s=2)
        acc_a, acc_b = (big[:, (2 * KH + 6 + KD) * T + n * D:(2 * KH + 6 + KD) * T + (n + 1) * D] for n in range(2))
        acc_c, acc_d = (nb[:, n:n + 2].rearrange("p k t -> p (k t)") for n in (2, 4))
        mod_acc = {0: (acc_a, acc_b), 1: (acc_c, acc_d), 2: (acc_a,), 3: (acc_b,), 4: (acc_c,), 5: (acc_a,)}
        MOD_ORDER = [0, 1, 2, 4, 3, 5]
        mod_free = {2: 1, 3: 1, 4: 2, 5: 3}
        mod_full = [sem(f"mod_full{s}") for s in range(2)]
        MOD_UNITS = N_MOD * KD
        PER_CHUNK = MOD_UNITS // 2 // KD

        def mod_start_act(act):
            act.wait_ge(*after("b_flip", KD))
            act.activation(silu_c, small_cols("c", 2 * KD), ACT.Exp, scale=-1.0).then_inc(sem("exp_c"), 1)

        def mod_start_dve(dve):
            dve.wait_ge(*after("exp_c", 1))
            link(dve, dve.tensor_scalar(silu_c, silu_c, 1.0, None, ALU.add))
            link(dve, dve.reciprocal(silu_c, silu_c))
            dve.tensor_tensor(silu_c, silu_c, small_cols("c", 2 * KD), ALU.mult).then_inc(sem("silu_c"), 1)
            dve.wait_ge(*after("silu_c", 1))

        def mod_products(dve, s, f):
            for n in range((s * KD + f) * PER_CHUNK, (s * KD + f + 1) * PER_CHUNK):
                m, k = divmod(n, KD)
                w = mod_ring[:, n % 2]
                dve.wait_ge(mod_full[n % 2], 16 * (n // 2 + 1))
                if n:
                    dve.wait_ge(sem("mod_used"), n)
                if k == 0 and m in mod_free:
                    dve.wait_ge(sem("mod_ps"), mod_free[m])
                for j, acc in enumerate(mod_acc[m]):
                    c = column(silu_c, 2 * k + j)
                    if k == 0:
                        ins = dve.tensor_scalar(acc, w, c, None, ALU.mult)
                    else:
                        ins = dve.scalar_tensor_tensor(out=acc, in0=w, scalar=c, in1=acc, op0=ALU.mult, op1=ALU.add)
                ins.then_inc(sem("mod_used"), 1)

        def mod_vector(pe, m):
            pe.wait_ge(sem("mod_used"), KD * (m + 1))
            for j, acc in enumerate(mod_acc[m]):
                for k in range(KD):
                    col = j * MOD_UNITS + m * KD + k
                    mm = pe.matmul(bank[6][:, col:col + 1], acc[:, k * P:(k + 1) * P], ones[:, 0:1], start=True, stop=True)
            mm.then_inc(sem("mod_ps"), 1)

        def mod_sums(pe, s, f):
            if (s, f) == (0, 3):
                grab(pe, 6, *after("mod", 1))
            due = {(0, 3): 0, (0, 6): 1, (1, 0): 2, (1, 6): 4}
            if (s, f) in due:
                mod_vector(pe, due[s, f])

        def mod_load(sp, n):
            if n == 0:
                sp.wait_ge(*after("b_ps", 1))
            if n >= 2:
                sp.wait_ge(sem("mod_used"), n - 1)
            sp.dma_start(mod_ring[:, n % 2], mod_w[n]).then_inc(mod_full[n % 2], 16)

        mod_due = {}
        for n in range(MOD_UNITS):
            s, f = divmod(n // PER_CHUNK, KD)
            mod_due.setdefault(UNITS[f"down1_{s}"] + f * KH // 8 + RING, []).append(n)

        def mod_pe(pe):
            grab(pe, 7, *after("cx_rstd", 1))
            for k in range(KD):
                pe.wait_ge(*after("cx_sq", k + 1))
                pe.matmul(bank[7][:, 0:CTX], ones, sq[:, k % 2, 0:CTX], start=(k == 0), stop=(k == KD - 1))\
                  .then_inc(sem("cx_sq_used"), 1)
            pe.wait_ge(*after("x2al", KD))

        def x2_act(act):
            for k in range(KD):
                act.wait_ge(*after("x2a", k + 1))
                act.activation(rounded(X2[:, k, CTX:TA]), h[:, k], ACT.Identity, bias=mod_lat[:, 0, k:k + 1])\
                   .then_inc(sem("x2_lat"), 1)

        def mod_act(act):
            act.wait_ge(*after("cx_in", 16))
            for k in range(KD):
                if k >= 2:
                    act.wait_ge(*after("cx_sq_used", k - 1))
                act.activation(sq[:, k % 2, 0:CTX], cx[:, k], ACT.Square).then_inc(sem("cx_sq"), 1)
            act.wait_ge(*after("cx_sq_used", KD))
            act.activation(var[:, 0:CTX], bank[7][:, 0:CTX], ACT.Sqrt, bias=gain("eps"), scale=1.0 / D)\
               .then_inc(sem("cx_sd"), 1)
            for k in range(KD):
                act.wait_ge(*after("x2b", k + 1))
                act.activation(rounded(X2[:, k, 0:CTX]), ctx_lo(k), ACT.Identity, bias=mod_ctx[:, 0, k:k + 1])\
                   .then_inc(sem("x2_ctx"), 1)

        def mod_dve(dve):
            dve.wait_ge(sem("mod_ps"), N_MOD)
            dve.tensor_tensor(mod_l, bank[6][:, 0:MOD_UNITS], small_cols("b_mod", MOD_UNITS), ALU.add)
            dve.tensor_tensor(mod_c, bank[6][:, MOD_UNITS:MOD_UNITS + 2 * KD], small_cols("b_mod", 2 * KD), ALU.add)\
               .then_inc(sem("mod"), 1)
            dve.wait_ge(*after("mod", 1))
            for dst, m, v, g in ((G1l, 1, mod_lat, "n1"), (G1c, 1, mod_ctx, "n1"), (G2, 4, mod_lat, "n2")):
                ins = dve.scalar_tensor_tensor(out=dst, in0=v[:, m], scalar=1.0, in1=small_cols(g, KD),
                                               op0=ALU.add, op1=ALU.mult)
            link(dve, ins)
            dve.wait_ge(sem("h_out"), 16)
            for k in range(KD + 1):
                if k < KD:
                    dve.scalar_tensor_tensor(out=h[:, k], in0=h[:, k], scalar=column(G1l, k), in1=rstd,
                                             op0=ALU.mult, op1=ALU.mult).then_inc(sem("x2a"), 1)
                if k:
                    dve.wait_ge(*after("x2_lat", k))
                    dve.scalar_tensor_tensor(out=rounded(h[:, k - 1]), in0=h[:, k - 1], scalar=mod_lat[:, 0, k - 1:k],
                                             in1=value(X2[:, k - 1, CTX:TA]), op0=ALU.add, op1=ALU.subtract)\
                       .then_inc(sem("x2al"), 1)
            dve.wait_ge(*after("x2a", KD))
            dve.wait_ge(*after("cx_sd", 1))
            dve.reciprocal(rstd[:, 0:CTX], var[:, 0:CTX]).then_inc(sem("cx_rstd"), 1)
            dve.wait_ge(*after("cx_rstd", 1))
            for k in range(KD + 1):
                if k < KD:
                    dve.scalar_tensor_tensor(out=ctx_lo(k), in0=cx[:, k], scalar=column(G1c, k), in1=rstd[:, 0:CTX],
                                             op0=ALU.mult, op1=ALU.mult).then_inc(sem("x2b"), 1)
                if k:
                    dve.wait_ge(*after("x2_ctx", k))
                    dve.scalar_tensor_tensor(out=rounded(ctx_lo(k - 1)), in0=ctx_lo(k - 1), scalar=mod_ctx[:, 0, k - 1:k],
                                             in1=value(X2[:, k - 1, 0:CTX]), op0=ALU.add, op1=ALU.subtract)\
                       .then_inc(sem("x2bl"), 1)

        dft = [part(2048 * n, TB, T) for n in range(4)]
        zT, dec = big[:, 8192:8192 + T], part(8192 + T, TB, 2 * HY_C)
        fw = big[:, 10752:10752 + 1152]
        hsum, hdif = part(12288, TB, T), part(12288 + 2048, TB, T)
        Hc, Hs = part(16384, TB, T), part(16384 + 2048, TB, T)
        u_hy = part(8192, 6, T)
        yT = part(12288, TB, HY_C)
        Yc, Ys = part(13312, TB, HY_C), part(14336, TB, HY_C)
        sp = part(15360, 4, HY_C)
        grid = lambda a: a.rearrange("p (r c) -> p r c", c=CH)
        TWO_PI = 2 * math.pi
        C1 = 6.28125
        C2 = float(np.float32(TWO_PI - C1) // np.float32(2.0 ** -17) * np.float32(2.0 ** -17))
        C3 = TWO_PI - C1 - C2
        MAGIC = 1.5 * 2.0 ** 23
        PI_F = 3.1415925

        def filter_pe(pe):
            pe.wait_ge(*after("filt_in", 32))
            ps = grab(pe, 4, *after("fa", 1))
            pe.matmul(ps[0:HY_FH, :], fw[0:HY_EMB, 0:HY_FH], zT[0:HY_EMB, :], start=True, stop=True).then_inc(sem("fl"), 1)
            pe.wait_ge(*after("fs", 1))
            ps = grab(pe, 5, *after("fa", 2))
            pe.matmul(ps[0:HY_FH, :], fw[0:HY_FH, HY_FH:2 * HY_FH], nb[0:HY_FH, 0], start=True, stop=True)\
              .then_inc(sem("fl"), 1)
            pe.wait_ge(*after("fs", 2))
            for i in range(2 * TB):
                pt, o = divmod(i, 2)
                ps = grab(pe, 4 + i % 2, *after("f_used", i + 1))
                pe.matmul(ps[:, :], nb[0:HY_FH, 1, pt * P:(pt + 1) * P], fw[0:HY_FH, 128 + o * T:128 + (o + 1) * T],
                          start=True, stop=True).then_inc(sem("f_pos"), 1)
            pe.wait_ge(*after("f_sum", 4 * TB))
            pe.wait_ge(sem("dft_in"), 16)
            for i in range(2 * TB):
                ft, c = divmod(i, 2)
                ps = grab(pe, i % 4, *after("H", i + 1))
                for pt in range(TB):
                    mm = pe.matmul(ps[:, :], dft[c][:, pt, ft * P:(ft + 1) * P], (hsum, hdif)[c][:, pt],
                                   start=(pt == 0), stop=(pt == TB - 1))
                mm.then_inc(sem("H_ps"), 1)

        def hyena_pe(pe):
            fm_multi(pe, "hy", 6, [lat], "hy_ps", "hy_u")
            for o in range(2):
                pe.wait_ge(*after("hy_y" if o else "hy_u", 2 if o else 6))
                for tb in range(TB):
                    ps = grab(pe, 4 + tb % 2, *after("yT", o * TB + tb + 1))
                    for c in range(2):
                        mm = pe.transpose(ps[:, c * P:(c + 1) * P], u_hy[:, c, tb * P:(tb + 1) * P], ident)
                    mm.then_inc(sem("y_turn"), 1)
                pe.wait_ge(*after("yT", (o + 1) * TB))
                pe.wait_ge(*after("H", 2 * TB))
                for ft in range(TB):
                    ps = grab(pe, ft, *after("spec", o * TB + ft + 1))
                    for c in range(2):
                        for tb in range(TB):
                            mm = pe.matmul(ps[:, c * HY_C:(c + 1) * HY_C], dft[c][:, tb, ft * P:(ft + 1) * P], yT[:, tb],
                                           start=(tb == 0), stop=(tb == TB - 1))
                    mm.then_inc(sem("U"), 1)
                pe.wait_ge(*after("Y", (o + 1) * TB))
                for m in range(2):
                    ps = grab(pe, 4 + m, *after("hy_y", 2 * o + m + 1))
                    for ft in range(TB):
                        for c in range(2):
                            mm = pe.matmul(ps[:, :], (Yc, Ys)[c][:, ft, m * P:(m + 1) * P], dft[2 + c][:, ft],
                                           start=(ft == 0 and c == 0), stop=(ft == TB - 1 and c == 1))
                    mm.then_inc(sem("conv"), 1)

        def filter_act(act):
            for n in range(2):
                act.wait_ge(*after("f_arg", n + 1))
                act.activation(nb[0:HY_FH, n], nb[0:HY_FH, 2], ACT.Sin).then_inc(sem("fs"), 1)
            x2_act(act)
            for i in range(2 * TB):
                act.wait_ge(*after("H_ps", i + 1))
                act.activation((Hc, Hs)[i % 2][:, i // 2], bank[i % 4][:, :], ACT.Copy).then_inc(sem("H"), 1)

        def hyena_act(act):
            for f in range(6):
                act.wait_ge(*after("hy_ps", f + 1))
                if f == 0:
                    act.wait_ge(*after("H_ps", 2 * TB))
                act.activation(u_hy[:, f], bank[f % 4][:, :], ACT.Identity, bias=gain("hyb", f), scale=gain("hyw1", f))\
                   .then_inc(sem("hy_tap"), 1)
            for i in range(2 * TB):
                act.wait_ge(*after("y_turn", i + 1))
                act.activation(yT[:, i % TB], bank[4 + i % 2][:, 0:HY_C], ACT.Copy).then_inc(sem("yT"), 1)

        def filter_dve(dve):
            w, m = nb[0:HY_FH, 2], nb[0:HY_FH, 3]
            for n in range(2):
                dve.wait_ge(*after("fl", n + 1))
                if n:
                    dve.wait_ge(*after("fs", 1))
                dve.tensor_scalar(w, bank[4 + n][0:HY_FH, :], gain(f"fb{n + 1}")[0:HY_FH], gain(f"fq{n + 1}")[0:HY_FH],
                                  ALU.add, ALU.mult).then_inc(sem("fa"), 1)
                dve.wait_ge(*after("fa", n + 1))
                link(dve, dve.tensor_scalar(m, w, 1.0 / TWO_PI, MAGIC, ALU.mult, ALU.add))
                link(dve, dve.tensor_scalar(m, m, -MAGIC, None, ALU.add))
                for c in (C1, C2, C3):
                    link(dve, dve.scalar_tensor_tensor(out=w, in0=m, scalar=-c, in1=w, op0=ALU.mult, op1=ALU.add))
                dve.tensor_scalar(w, w, PI_F, -PI_F, ALU.min, ALU.max).then_inc(sem("f_arg"), 1)
            dve.wait_ge(*after("filt_in", 32))
            fb = cst[:, 1280:1280 + T]
            for i in range(2 * TB):
                pt, o = divmod(i, 2)
                dve.wait_ge(*after("f_pos", i + 1))
                if i:
                    dve.wait_ge(*after("f_sum", 2 * i))
                dve.tensor_tensor(fb, bank[4 + i % 2][:, :], dec[:, pt], ALU.mult).then_inc(sem("f_used"), 1)
                dve.wait_ge(*after("f_used", i + 1))
                cols = slice(o * HY_C, (o + 1) * HY_C)
                for dst, op in ((hsum, ALU.add), (hdif, ALU.subtract)):
                    dve.tensor_tensor(dst[:, pt, cols], fb[:, 0:HY_C], fb[:, HY_C:], op).then_inc(sem("f_sum"), 1)

        def hyena_dve(dve):
            for f in range(6):
                dve.wait_ge(*after("hy_tap", f + 1))
                ps, u = grid(bank[f % 4][:, :]), grid(u_hy[:, f])
                link(dve, dve.scalar_tensor_tensor(out=u[:, :, 1:], in0=ps[:, :, 0:CH - 1], scalar=gain("hyw0", f),
                                                   in1=u[:, :, 1:], op0=ALU.mult, op1=ALU.add))
                dve.scalar_tensor_tensor(out=u[:, :, 0:CH - 1], in0=ps[:, :, 1:], scalar=gain("hyw2", f),
                                         in1=u[:, :, 0:CH - 1], op0=ALU.mult, op1=ALU.add).then_inc(sem("hy_u"), 1)
            dve.wait_ge(*after("hy_u", 6))
            for o in range(2):
                dve.wait_ge(*after("H", 2 * TB))
                for ft in range(TB):
                    dve.wait_ge(*after("U", o * TB + ft + 1))
                    Uc, Us = bank[ft][:, 0:HY_C], bank[ft][:, HY_C:]
                    hc, hs = (a[:, ft, o * HY_C:(o + 1) * HY_C] for a in (Hc, Hs))
                    if o * TB + ft:
                        dve.wait_ge(*after("Y", o * TB + ft))
                    for n, (a, b) in enumerate(((Uc, hc), (Us, hs), (Uc, hs))):
                        dve.tensor_tensor(sp[:, n], a, b, ALU.mult)
                    dve.tensor_tensor(sp[:, 3], Us, hc, ALU.mult).then_inc(sem("spec"), 1)
                    dve.wait_ge(*after("spec", o * TB + ft + 1))
                    dve.tensor_tensor(Yc[:, ft], sp[:, 0], sp[:, 1], ALU.subtract)
                    dve.tensor_tensor(Ys[:, ft], sp[:, 2], sp[:, 3], ALU.add).then_inc(sem("Y"), 1)
                for m in range(2):
                    dve.wait_ge(*after("conv", 2 * o + m + 1))
                    y = u_hy[:, m]
                    link(dve, dve.scalar_tensor_tensor(out=y, in0=y, scalar=gain("hyd", 2 * o + m), in1=bank[4 + m][:, :],
                                                       op0=ALU.mult, op1=ALU.add))
                    dst = y if o == 0 else mix[:, m]
                    dve.tensor_tensor(dst, y, u_hy[:, 2 + 2 * o + m], ALU.mult).then_inc(sem("hy_y"), 1)
                dve.wait_ge(*after("hy_y", 2 * o + 2))

        m_f, m_b = cst[:, 0:P], cst[:, P:2 * P]
        reset = cst[:, 2 * P:2 * P + TA]
        is_fwd, is_bwd, sign = (cst[:, 2 * P + TA + n:2 * P + TA + n + 1] for n in range(3))
        agT, gt = cst[:, 1280:1280 + TA], cst[:, 2048:2048 + TA]
        gl_q, gl_k, gl_v = part(0, 2, T), part(1024, 2, TA), part(2560, NBLK, GW)
        gl_b = part(4864, 4, TA)
        gl_q1, gl_k2 = part(7936, 4, T), part(9984, 4, TA)
        gl_t = gl_k2
        gl_kT = part(13056, NBLK, T)
        gl_S, gl_Sr = part(16128, 4, GLA_DV), part(16512, 4, GLA_DV)
        gl_A = part(16896, 2, T)
        gl_sc = part(17920, 3, 4 * NCH)
        gl_U = part(18064, 4, GLA_DV)
        gl_o = mix[:, 2:5].rearrange("p k t -> p (k t)").rearrange("p (b n) -> p b n", b=TB)
        gl_w2 = big[:, 18448:18448 + 2 * P]
        gl_tot = big[:, 18704:18704 + 4 * NCH]
        gl_d = part(13056, 4, TA)
        gate = mix[:, 5:8].rearrange("p k t -> p (k t)").rearrange("p (b n) -> p b n", b=TB)
        chunks = lambda a: a.rearrange("p (n c) -> p n c", c=CH)

        def gates_pe(pe):
            pe.wait_ge(*after("gla_in", 32))
            pe.wait_ge(*after("x2bl", KD))
            fm_multi(pe, "ag", 1, [lat, ctxp], "ag_ps", "ag")
            fm_multi(pe, "gl_q", 2, [lat], "glq_ps", "glq")
            fm_multi(pe, "gl_k", 2, [lat, ctxp], "glk_ps", "glk")
            tm_linear(pe, "gl_v", GW, lambda k, i: X2_block(k, i), NBLK, "glv_ps", "glv")
            pe.wait_ge(*after("ag", 2))
            for i in range(8):
                dc, p = divmod(i, 2)
                d, c = divmod(dc, 2)
                a, n = ((CTX, T), (0, CTX))[p]
                ps = grab(pe, i % 4, *after("glz", i + 1))
                pe.matmul(ps[:, 0:n], gl_w2[32 * d:32 * d + GLA_RANK, c * P:(c + 1) * P],
                          agT[32 * d:32 * d + GLA_RANK, a:a + n], start=True, stop=True).then_inc(sem("glz_ps"), 1)
            heads_pe(pe, "gla", "gl_g")

        def gates_act(act):
            act.wait_ge(*after("hy_y", 4))
            act.wait_ge(*after("gla_in", 32))
            for p, (a, n) in enumerate(((CTX, T), (0, CTX))):
                act.wait_ge(*after("ag_ps", p + 1))
                act.activation(agT[:, a:a + n], bank[p][:, 0:n], ACT.Copy).then_inc(sem("ag"), 1)
            for c in range(2):
                act.wait_ge(*after("glq_ps", c + 1))
                act.activation(gl_q[:, c], bank[c][:, :], ACT.Copy).then_inc(sem("glq"), 1)
            for i in range(4):
                a, n = ((CTX, T), (0, CTX))[i % 2]
                act.wait_ge(*after("glk_ps", i + 1))
                act.activation(gl_k[:, i // 2, a:a + n], bank[i][:, 0:n], ACT.Copy).then_inc(sem("glk"), 1)
            for i in range(NBLK):
                act.wait_ge(*after("glv_ps", i + 1))
                act.activation(gl_v[:, i], bank[i][:, 0:GW], ACT.Copy).then_inc(sem("glv"), 1)
            hi = nb[64:P, 2:4].rearrange("p k t -> p (k t)")[:, 0:TA]
            act.wait_ge(*after("gt_abs", 1))
            link(act, act.activation(hi, hi, ACT.Exp, scale=-1.0))
            act.activation(hi, hi, ACT.Ln, bias=1.0).then_inc(sem("gt_ln"), 1)
            t = gl_t.rearrange("p k t -> p (k t)")
            act.wait_ge(*after("gla_abs", 1))
            link(act, act.activation(t, t, ACT.Exp, scale=-1.0))
            act.activation(t, t, ACT.Ln, bias=1.0).then_inc(sem("gla_ln"), 1)
            act.wait_ge(*after("gla_diff", 1))
            sc = big[:, 17920:17920 + 12 * NCH]
            act.activation(sc, sc, ACT.Exp).then_inc(sem("gla_esc"), 1)
            d = gl_d.rearrange("p k t -> p (k t)")
            act.activation(gl_b.rearrange("p k t -> p (k t)"), d, ACT.Exp).then_inc(sem("gla_ep"), 1)
            act.wait_ge(*after("gla_ep", 1))
            act.activation(d, d, ACT.Exp, scale=-1.0).then_inc(sem("gla_en"), 1)
            heads_gate(act, "gla", gate)

        def gates_dve(dve):
            z = nb[64:P, 0:2].rearrange("p k t -> p (k t)")[:, 0:TA]
            az = nb[64:P, 2:4].rearrange("p k t -> p (k t)")[:, 0:TA]
            g = gt[64:P]
            dve.wait_ge(*after("ag", 2))
            dve.wait_ge(*after("x2b", KD))
            link(dve, dve.tensor_scalar(z, agT[64:P], sign[64:P], gain("dt")[64:P], ALU.mult, ALU.add))
            dve.scalar_tensor_tensor(out=az, in0=z, scalar=-1.0, in1=z, op0=ALU.mult, op1=ALU.max).then_inc(sem("gt_abs"), 1)
            for i in range(8):
                dc, p = divmod(i, 2)
                a, n = ((CTX, T), (0, CTX))[p]
                dve.wait_ge(*after("glz_ps", i + 1))
                dve.tensor_scalar(gl_b[:, dc, a:a + n], bank[i % 4][:, 0:n], gain("gla_b", dc), None, ALU.add)\
                   .then_inc(sem("glz"), 1)
            dve.wait_ge(*after("glz", 8))
            b, t, d = (a.rearrange("p k t -> p (k t)") for a in (gl_b, gl_t, gl_d))
            dve.scalar_tensor_tensor(out=t, in0=b, scalar=-1.0, in1=b, op0=ALU.mult, op1=ALU.max).then_inc(sem("gla_abs"), 1)
            dve.wait_ge(*after("gla_abs", 1))
            link(dve, dve.tensor_scalar(b, b, 0.0, 1.0 / GLA_TAU, ALU.min, ALU.mult))
            dve.wait_ge(*after("gla_ln", 1))
            link(dve, dve.scalar_tensor_tensor(out=t, in0=t, scalar=-1.0 / GLA_TAU, in1=b, op0=ALU.mult, op1=ALU.add))
            for dc in range(4):
                ins = dve.tensor_tensor_scan(gl_b[:, dc], reset, gl_t[:, dc], 0.0, ALU.mult, ALU.add)
            link(dve, ins)
            half = 2 * NCH
            bc, tc, dcc = chunks(b), chunks(t), chunks(d)
            tot = gl_tot[:, :]
            link(dve, dve.tensor_copy(tot, bc[:, :, CH - 1]))
            bb, tb_ = bc[:, half:], tc[:, half:]
            link(dve, dve.tensor_tensor(bb, tb_, bb, ALU.subtract))
            link(dve, dve.tensor_tensor(bb, bb, tot[:, half:].unsqueeze(2).broadcast_to((P, half, CH)), ALU.add))
            sc = gl_sc
            link(dve, dve.tensor_copy(sc[:, 0, 0:half], bc[:, 0:half, CH // 2 - 1]))
            link(dve, dve.tensor_copy(sc[:, 0, half:], bc[:, half:, CH // 2]))
            link(dve, dve.tensor_copy(sc[:, 1], tot))
            link(dve, dve.tensor_tensor(sc[:, 2], sc[:, 1], sc[:, 0], ALU.subtract))
            dve.tensor_tensor(dcc, bc, sc[:, 0].unsqueeze(2).broadcast_to((P, 4 * NCH, CH)), ALU.subtract)\
               .then_inc(sem("gla_diff"), 1)
            dve.wait_ge(*after("gt_ln", 1))
            link(dve, dve.scalar_tensor_tensor(out=z, in0=z, scalar=0.0, in1=az, op0=ALU.max, op1=ALU.add))
            dve.wait_ge(*after("ea", 1))
            link(dve, dve.tensor_scalar(z, z, column(vecs, 136)[64:P], None, ALU.mult))
            link(dve, dve.tensor_copy(g, z))
            dve.wait_ge(*after("gla_in", 32))
            link(dve, dve.tensor_tensor_scan(az[0:32], reset[64:96], z[0:32], 0.0, ALU.mult, ALU.add))
            zc, ac = chunks(z[0:32]), chunks(az[0:32])
            link(dve, dve.tensor_tensor(zc, zc, ac, ALU.subtract))
            link(dve, dve.tensor_tensor(zc, zc, ac[:, :, CH - 1:CH].broadcast_to((32, NCH, CH)), ALU.add))
            link(dve, dve.tensor_scalar(z[0:32], z[0:32], is_bwd[64:96], None, ALU.mult))
            dve.scalar_tensor_tensor(out=g[0:32], in0=az[0:32], scalar=is_fwd[64:96], in1=z[0:32], op0=ALU.mult,
                                     op1=ALU.add).then_inc(sem("gt"), 1)
            dve.wait_ge(*after("gla_diff", 1))
            dve.wait_ge(*after("glq", 2))
            dve.wait_ge(*after("glk", 4))
            dve.wait_ge(*after("gla_ep", 1))
            for dc in range(4):
                c = dc % 2
                dve.scalar_tensor_tensor(out=gl_q1[:, dc], in0=gl_q[:, c], scalar=GLA_DK ** -0.5, in1=gl_b[:, dc, CTX:TA],
                                         op0=ALU.mult, op1=ALU.mult)
            dve.wait_ge(*after("gla_en", 1))
            for dc in range(4):
                dve.tensor_tensor(gl_k2[:, dc], gl_k[:, dc % 2], gl_d[:, dc], ALU.mult).then_inc(sem("gla_qk"), 1)

        def steps(d):
            return list(range(NCH)) if d == 0 else list(range(CCH))[::-1] + list(range(CCH, NCH))[::-1]

        def gla_pe(pe):
            pe.wait_ge(*after("gla_qk", 4))
            pe.wait_ge(*after("glv", NBLK))
            for b in range(NBLK):
                ps = grab(pe, 4 + b % 2, *after("glkT", b + 1))
                for dc in range(4):
                    mm = pe.transpose(ps[:, dc * P:(dc + 1) * P], gl_k2[:, dc, b * P:(b + 1) * P], ident)
                mm.then_inc(sem("gl_turn"), 1)
            def scores(tb):
                for hh in range(2):
                    ps = grab(pe, 2 * (tb % 2) + hh, *after("gl_A", tb + 1))
                    r = 64 * hh
                    for dc in range(4):
                        mm = pe.matmul(ps[:, dc * P:(dc + 1) * P], gl_k2[r:r + 64, dc, CTX + tb * P:CTX + (tb + 1) * P],
                                       gl_q1[r:r + 64, dc, tb * P:(tb + 1) * P], start=True, stop=True)
                    mm.then_inc(sem("gl_s"), 1)

            def inner(tb):
                pe.wait_ge(*after("gl_A", tb + 1))
                ps = grab(pe, 4 + tb % 2, *after("gl_in", tb + 1))
                for hd in range(GH):
                    mm = pe.matmul(ps[:, hd * GLA_DV:(hd + 1) * GLA_DV], gl_A[:, tb % 2, hd * P:(hd + 1) * P],
                                   gl_v[:, CB + tb, hd * GLA_DV:(hd + 1) * GLA_DV], start=True, stop=True)
                mm.then_inc(sem("gl_o"), 1)
            scores(0)
            for tb in range(TB):
                if tb + 1 < TB:
                    scores(tb + 1)
                inner(tb)
            pe.wait_ge(*after("glkT", NBLK))
            n_in = 0
            for n in range(NCH):
                for dc in range(4):
                    d = dc // 2
                    if dc % 2 == 0:
                        ps = grab(pe, 2 * (n % 2) + d, *after("gl_Su", n + 1))
                    c = steps(d)[n]
                    r = CH * (c % 2)
                    for hh in range(2):
                        hd = 2 * (dc % 2) + hh
                        mm = pe.matmul(ps[64 * hh:64 * hh + 64, (dc % 2) * GLA_DV:(dc % 2 + 1) * GLA_DV],
                                       gl_kT[r:r + CH, c // 2, dc * P + 64 * hh:dc * P + 64 * hh + 64],
                                       gl_v[r:r + CH, c // 2, hd * GLA_DV:(hd + 1) * GLA_DV], start=True, stop=True)
                mm.then_inc(sem("gl_U"), 1)
                if n >= CCH:
                    for d in range(2):
                        c = steps(d)[n] - CCH
                        r = CH * (c % 2)
                        pe.wait_ge(*after("gl_Sr", 2 * (n - CCH) + d + 1))
                        for hd in (0, 2, 1, 3):
                            q, dc = 64 * (hd % 2), 2 * d + hd // 2
                            if hd < 2:
                                ps = grab(pe, 4 + 2 * d + hd, *after("gl_add", 4 * (n - CCH) + 2 * d + hd + 1))
                            mm = pe.matmul(ps[r:r + CH, (hd // 2) * GLA_DV:(hd // 2 + 1) * GLA_DV],
                                           gl_q1[q:q + 64, dc, c * CH:(c + 1) * CH], gl_Sr[q:q + 64, dc, :],
                                           start=True, stop=True)
                        mm.then_inc(sem("gl_x"), 1)

        def gla_act(act):
            for b in range(NBLK):
                act.wait_ge(*after("gl_turn", b + 1))
                act.activation(gl_kT[:, b], bank[4 + b % 2][:, :], ACT.Copy).then_inc(sem("glkT"), 1)

        def gla_dve(dve):
            v4 = lambda a: a.rearrange("p (h n) -> p h n", h=GH)
            for tb in range(TB):
                dve.wait_ge(*after("gl_s", 2 * tb + 2))
                if tb >= 2:
                    dve.wait_ge(*after("gl_o", tb - 1))
                A, B_ = v4(gl_A[:, tb % 2]), v4(tmp[:, 0])
                for dst, at_, m in ((A, 0, m_f), (B_, 2, m_b)):
                    for hh in range(2):
                        ins = dve.tensor_tensor(dst[:, hh::2], v4(bank[2 * (tb % 2) + hh][:, :])[:, at_:at_ + 2],
                                                m.unsqueeze(1).broadcast_to((P, 2, P)), ALU.mult)
                link(dve, ins)
                dve.tensor_tensor(A, A, B_, ALU.add).then_inc(sem("gl_A"), 1)
                dve.wait_ge(*after("gl_o", tb + 1))
                dve.tensor_copy(gl_o[:, tb], bank[4 + tb % 2][:, 0:GW]).then_inc(sem("gl_in"), 1)
            dve.wait_ge(*after("gl_in", TB))
            dve.wait_ge(*after("gla_esc", 1))
            link(dve, dve.memset(gl_S[:, :, :], 0.0))
            scol = lambda kind, d, c: gl_sc[:, kind].rearrange("p (a n) -> p a n", a=4)[:, 2 * d:2 * d + 2, c:c + 1]\
                .broadcast_to((P, 2, GLA_DV))
            adds = 0
            for n in range(NCH):
                dve.wait_ge(*after("gl_U", n + 1))
                if n >= CCH:
                    for d in range(2):
                        if n > CCH:
                            dve.wait_ge(*after("gl_x", 2 * (n - CCH) - 1 + d))
                        dve.tensor_tensor(gl_Sr[:, 2 * d:2 * d + 2], gl_S[:, 2 * d:2 * d + 2], scol(0, d, steps(d)[n]), ALU.mult)\
                           .then_inc(sem("gl_Sr"), 1)
                    dve.wait_ge(*after("gl_Sr", 2 * (n - CCH) + 2))
                for d in range(2):
                    c = steps(d)[n]
                    S, u = gl_S[:, 2 * d:2 * d + 2], gl_U[:, 2 * d:2 * d + 2]
                    dve.tensor_tensor(S, S, scol(1, d, c), ALU.mult)
                    U = bank[2 * (n % 2) + d][:, 0:2 * GLA_DV].rearrange("p (a n) -> p a n", a=2)
                    ins = dve.tensor_tensor(u, U, scol(2, d, c), ALU.mult)
                ins.then_inc(sem("gl_Su"), 1)
                dve.wait_ge(*after("gl_Su", n + 1))
                link(dve, dve.tensor_tensor(gl_S[:, :], gl_S[:, :], gl_U[:, :], ALU.add))
                if n >= CCH:
                    for d in range(2):
                        c = steps(d)[n] - CCH
                        r = CH * (c % 2)
                        dve.wait_ge(*after("gl_x", 2 * (n - CCH) + d + 1))
                        for hh in range(2):
                            o = v4(gl_o[r:r + CH, c // 2])[:, hh::2]
                            x_ = bank[4 + 2 * d + hh][r:r + CH, 0:2 * GLA_DV].rearrange("p (a n) -> p a n", a=2)
                            dve.tensor_tensor(o, o, x_, ALU.add).then_inc(sem("gl_add"), 1)
                        dve.wait_ge(*after("gl_add", 4 * (n - CCH) + 2 * d + 2))

        def heads_pe(pe, st, name):
            tm_linear(pe, name, GW, lambda k, i: X2_block(k, CB + i), TB,
                      st + "_gps", st + "_gate")

        def heads_flip(pe, st, src):
            pe.wait_ge(*after(st + "_normed", 1))
            for c in range(3):
                ps = grab(pe, 4 + c % 2, *after(st + "_cat", c + 1))
                for tb in range(TB):
                    mm = pe.transpose(ps[:, tb * P:(tb + 1) * P], src[:, tb, c * P:(c + 1) * P], ident)
                mm.then_inc(sem(st + "_flip"), 1)

        def heads_gate(act, st, gate):
            for tb in range(TB):
                act.wait_ge(*after(st + "_gps", tb + 1))
                act.activation(gate[:, tb], bank[tb % 4][:, 0:GW], ACT.Silu).then_inc(sem(st + "_gate"), 1)

        def heads_act(act, st, dst):
            act.wait_ge(*after(st + "_ss", 1))
            act.activation(stat[:, 0:16], stat[:, 0:16], ACT.Sqrt).then_inc(sem(st + "_sd"), 1)
            for c in range(3):
                act.wait_ge(*after(st + "_flip", c + 1))
                act.activation(mix[:, dst + c], bank[4 + c % 2][:, :], ACT.Copy).then_inc(sem(st + "_cat"), 1)

        def heads_dve(dve, st, o, gate, gate_ready, res, gn):
            v = lambda a: a.rearrange("p b (h n) -> p (b h) n", h=GH)
            s16 = stat[:, 0:16]
            link(dve, dve.tensor_tensor(v(res), v(o), v(o), ALU.mult))
            link(dve, dve.tensor_reduce(s16, v(res), AX.X, ALU.add))
            dve.tensor_scalar(s16, s16, 1.0 / GDN_D, EPS, ALU.mult, ALU.add).then_inc(sem(st + "_ss"), 1)
            dve.wait_ge(*after(st + "_sd", 1))
            link(dve, dve.reciprocal(s16, s16))
            link(dve, dve.tensor_tensor(v(res), v(o), s16.unsqueeze(2).broadcast_to((P, 16, GDN_D)), ALU.mult))
            link(dve, dve.tensor_tensor(v(res), v(res), small_cols(gn, GDN_D).unsqueeze(1).broadcast_to((P, 16, GDN_D)), ALU.mult))
            dve.wait_ge(*after(gate_ready, TB))
            dve.tensor_tensor(res, res, gate, ALU.mult).then_inc(sem(st + "_normed"), 1)

        gl_res = part(0, TB, GW)

        gd_q, gd_k = part(0, GH, T), part(2048, GH, TA)
        gd_vT, gd_kT = part(5120, NBLK, GW), part(7424, NBLK, GW)
        selA, selL = (big[:, 9728 + 1024 * n:9728 + 1024 * (n + 1)].rearrange("p (r n) -> p r n", r=8) for n in range(2))
        gd_vf = part(11776, 3, TA)
        gd_wT, gd_u = part(11776, GH, TA), part(14848, NBLK, GW)
        gd_AT = part(17152, TB, T)
        gd_S = big[0:GDN_D, 19200:19200 + GW]
        gd_r = part(19584, 2, GW)
        gd_sc = big[:, 20352:20352 + 8 * NBLK * 8].rearrange("p (s b r) -> p s b r", s=8, b=NBLK)
        gd_o = mix[:, 5:8].rearrange("p k t -> p (k t)").rearrange("p (b n) -> p b n", b=TB)
        gd_gate = xn_all[:, 0:TB * GW].rearrange("p (b n) -> p b n", b=TB)
        gmask = lambda d, strict: cst[:, (2 * d + (0 if strict else 1)) * P:(2 * d + (0 if strict else 1) + 1) * P]
        level = lambda d, n: cst[:, (4 + 6 * d + n) * P:(5 + 6 * d + n) * P]
        wide = lambda m: m.unsqueeze(1).broadcast_to((P, GH, P))
        v4 = lambda a: a.rearrange("p (h n) -> p h n", h=GH)
        tile = lambda n: xn_all[:, 1536 + n * T:1536 + (n + 1) * T]
        GPARTS = [(CTX, T), (0, CTX)]
        NQ, NK, NV = GH, GH, 3
        fills = [("q", f, 0) for f in range(NQ)] + [("k", f, p) for f in range(NK) for p in range(2)] + \
                [("v", f, p) for f in range(NV) for p in range(2)]

        def gd_dst(kind, f, p):
            a, n = GPARTS[p]
            return gd_q[:, f] if kind == "q" else (gd_k if kind == "k" else gd_vf)[:, f, a:a + n]

        def gd_tap(kind, f, j):
            return gain(f"gdw{j}", {"q": 0, "k": GH, "v": 2 * GH}[kind] + f)

        NL2 = NQ + 2 * NK

        def items(i):
            return (2 * (i - NL2), 2 * (i - NL2) + 1) if i >= NL2 else ()

        def delta_in_pe(pe):
            i = 0
            for kind, name, chunks_, parts in (("q", "gd_q", NQ, [lat]), ("k", "gd_k", NK, [lat, ctxp]), ("v", "gd_v", NV, [lat, ctxp])):
                u0 = UNITS[name]
                for f in range(chunks_):
                    for rhs, n in parts:
                        ps = grab(pe, i % 4, *after("gd_conv", i + 1))
                        take(pe, u0 + f)
                        for k in range(KD):
                            mm = hi_lo_product(pe, ps[:, 0:n], weight(u0 + f, slice(k * P, (k + 1) * P)), rhs(k),
                                               k == 0, k == KD - 1)
                        mm.then_inc(sem("gd_ps"), 1)
                        i += 1
                        if kind == "v":
                            for m in items(i - 1):
                                ps = grab(pe, 6 + m % 2, *after("gd_sd", m + 1))
                                w = GPARTS[fills[m][2]][1]
                                pe.wait_ge(*after("gd_sq", m + 1))
                                pe.matmul(ps[:, 0:w], ones, sq[:, m % 2, 0:w], start=True, stop=True).then_inc(sem("gd_ss"), 1)
                    product_done[u0 + f] = after("gd_ps", i)
            heads_pe(pe, "gd", "gd_g")
            pe.wait_ge(*after("gd_normed", NQ + 2 * NK))
            pe.wait_ge(*after("gd_silu", len(fills)))
            for i in range(2 * NBLK):
                b, isv = divmod(i, 2)
                ps = grab(pe, 4 + i % 2, *after("gd_tm", i + 1))
                if isv:
                    for c in range(NV):
                        mm = pe.transpose(ps[:, c * P:(c + 1) * P], gd_vf[:, c, b * P:(b + 1) * P], ident)
                else:
                    for c in range(GH):
                        mm = pe.transpose(ps[:, c * GDN_D:(c + 1) * GDN_D], gd_k[0:GDN_D, c, b * P:(b + 1) * P],
                                          ident[0:GDN_D, 0:GDN_D])
                mm.then_inc(sem("gd_turn"), 1)
            pe.wait_ge(*after("gt", 1))
            pe.wait_ge(*after("gdn_in", 32))
            ps = grab(pe, 0, *after("gd_tg", 1))
            for b in range(NBLK):
                mm = pe.transpose(ps[:, b * 64:(b + 1) * 64], gt[64:P, b * P:(b + 1) * P], ident[64:P, 64:P])
            mm.then_inc(sem("gd_gT"), 1)
            ps = grab(pe, 1, *after("gd_gl", 1))
            for r in range(8):
                last_ = chunks(gt[64:P])[:, :, CH - 1 if r < GH else 0]
                mm = pe.matmul(ps[:, r * NCH:(r + 1) * NCH], selA[64:P, r], last_, start=True, stop=True)
            mm.then_inc(sem("gd_last"), 1)

        def delta_in_act(act):
            act.wait_ge(*after("gla_cat", 3))
            for i, (kind, f, p) in enumerate(fills):
                dst = gd_dst(kind, f, p)
                n = GPARTS[p][1]
                for m in items(i):
                    w = GPARTS[fills[m][2]][1]
                    act.wait_ge(*after("gd_silu", m + 1))
                    if m >= 2:
                        act.wait_ge(*after("gd_ss", m - 1))
                    act.activation(sq[:, m % 2, 0:w], gd_dst(*fills[m]), ACT.Square).then_inc(sem("gd_sq"), 1)
                act.wait_ge(*after("gd_ps", i + 1))
                act.activation(dst, bank[i % 4][:, 0:n], ACT.Copy, scale=gd_tap(kind, f, GDN_TAPS // 2))\
                   .then_inc(sem("gd_tap"), 1)
                if i >= 1:
                    act.wait_ge(*after("gd_conv", i))
                    act.activation(gd_dst(*fills[i - 1]), gd_dst(*fills[i - 1]), ACT.Silu).then_inc(sem("gd_silu"), 1)
                for m in items(i):
                    w = GPARTS[fills[m][2]][1]
                    act.wait_ge(*after("gd_ss", m + 1))
                    if m >= 2:
                        act.wait_ge(*after("gd_normed", m - 1))
                    act.activation(nb[:, 2 + m % 2, 0:w], bank[6 + m % 2][:, 0:w], ACT.Sqrt, bias=gain("eps"))\
                       .then_inc(sem("gd_sd"), 1)
            act.wait_ge(*after("gd_conv", len(fills)))
            act.activation(gd_dst(*fills[-1]), gd_dst(*fills[-1]), ACT.Silu).then_inc(sem("gd_silu"), 1)
            for tb in range(TB):
                act.wait_ge(*after("gd_gps", tb + 1))
                if tb == 0:
                    act.wait_ge(*after("gd_gps", TB))
                act.activation(gd_gate[:, tb], bank[tb % 4][:, 0:GW], ACT.Silu).then_inc(sem("gd_gate"), 1)
            for i in range(2 * NBLK):
                b, isv = divmod(i, 2)
                act.wait_ge(*after("gd_turn", i + 1))
                act.activation((gd_vT if isv else gd_kT)[:, b], bank[4 + i % 2][:, 0:GW], ACT.Copy).then_inc(sem("gd_tm"), 1)
            act.wait_ge(*after("gd_gl", 1))
            act.activation(big[:, 20352 + 48:20352 + 5 * 48], big[:, 20352 + 48:20352 + 5 * 48], ACT.Exp).then_inc(sem("gd_es"), 1)
            act.activation(stat[:, 0:48], stat[:, 0:48], ACT.Exp).then_inc(sem("gd_es"), 1)
            act.activation(vecs[:, 160:208], vecs[:, 160:208], ACT.Exp).then_inc(sem("gd_es"), 1)

        def delta_in_dve(dve):
            R = GDN_TAPS // 2
            for i, (kind, f, p) in enumerate(fills):
                n = GPARTS[p][1]
                ps, u = bank[i % 4][:, 0:n], gd_dst(kind, f, p)
                if p == 0:
                    ps, u = grid(ps), grid(u)
                else:
                    ps, u = ps.unsqueeze(1), u.unsqueeze(1)
                m = CH if p == 0 else n
                dve.wait_ge(*after("gd_tap", i + 1))
                for j in range(GDN_TAPS):
                    s = j - R
                    if s == 0:
                        continue
                    o0, o1 = max(0, -s), m - max(0, s)
                    ins = dve.scalar_tensor_tensor(out=u[:, :, o0:o1], in0=ps[:, :, o0 + s:o1 + s], scalar=gd_tap(kind, f, j),
                                                   in1=u[:, :, o0:o1], op0=ALU.mult, op1=ALU.add)
                    if j < GDN_TAPS - 1:
                        link(dve, ins)
                ins.then_inc(sem("gd_conv"), 1)
                for m in items(i):
                    kind_m, _, part_m = fills[m]
                    v = nb[:, 2 + m % 2, 0:GPARTS[part_m][1]]
                    dve.wait_ge(*after("gd_sd", m + 1))
                    link(dve, dve.reciprocal(v, v))
                    x_ = gd_dst(*fills[m])
                    dve.scalar_tensor_tensor(out=x_, in0=x_, scalar=GDN_D ** -0.5 if kind_m == "q" else 1.0, in1=v,
                                             op0=ALU.mult, op1=ALU.mult).then_inc(sem("gd_normed"), 1)
            tg = bank[0][:, 0:NBLK * 64].rearrange("p (b r) -> p b r", b=NBLK)
            gd = gd_sc
            dve.wait_ge(*after("gd_gT", 1))
            link(dve, dve.tensor_scalar(gd[:, 0], tg[:, :, 0:8], -1.0, None, ALU.mult))
            link(dve, dve.tensor_copy(gd[:, 1], tg[:, :, 0:8]))
            link(dve, dve.tensor_copy(gd[:, 2], tg[:, :, 32:40]))
            dve.tensor_tensor(gd[:, 3], gd[:, 1], gd[:, 2], ALU.add).then_inc(sem("gd_tg"), 1)
            dve.wait_ge(*after("gd_last", 1))
            gl = bank[1][:, 0:8 * NCH].rearrange("p (r b two) -> p two b r", r=8, two=2)
            for par in range(2):
                rows_ = slice(64 * par, 64 * par + 64)
                ins = dve.tensor_tensor(gd[rows_, 4], gl[rows_, par], gd[rows_, 0], ALU.add)
            link(dve, ins)
            link(dve, dve.tensor_copy(stat[:, 0:48], bank[1][:, 0:48]))
            dve.tensor_copy(vecs[:, 160:208], bank[1][:, 48:96]).then_inc(sem("gd_gl"), 1)

        SETS = 3
        GROUPS = 2 * NBLK // SETS
        dl = lambda name: sem("delta_" + name)
        LEVELS = 6
        work = [[tile(n) for n in (s, SETS + s, 2 * SETS + s)] + [nb[:, 2 * s], nb[:, 2 * s + 1]] for s in range(SETS)]
        lanes = parts_all[:, :]
        gd_wTs = [gd_wT, lanes[:, 0:GH * TA].rearrange("p (h n) -> p h n", h=GH)]
        gd_us = [gd_u, lanes[:, GH * TA:GH * TA + NBLK * GW].rearrange("p (b n) -> p b n", b=NBLK)]
        gd_rs = [gd_r, lanes[:, GH * TA + NBLK * GW:GH * TA + (NBLK + 2) * GW].rearrange("p (b n) -> p b n", b=2)]
        gd_ATs = [gd_AT, xn_all[:, 1536:1536 + TB * T].rearrange("p (b n) -> p b n", b=TB)]
        gd_Ss = [gd_S, tile(8)[0:GDN_D, 0:GW]]

        def set_of(i):
            return i // NBLK, i % NBLK, i % SETS, i // SETS

        heads4 = [slice(hd * P, (hd + 1) * P) for hd in range(GH)]

        def decay_rows(pe, b_, d, b, sel_, reader):
            ps = grab(pe, b_, *reader)
            for hd in range(GH):
                mm = pe.matmul(ps[:, heads4[hd]], sel_[64:P, GH * d + hd], gt[64:P, b * P:(b + 1) * P],
                               start=True, stop=True)
            mm.then_inc(dl("g"), 1)

        def inverse_pe(pe):
            pe.wait_ge(*after("gd_tm", 2 * NBLK))
            pe.wait_ge(*after("gd_gate", TB))

            def gram(i):
                d, b, j, q = set_of(i)
                ps = grab(pe, j, dl("LT"), i + 1)
                for hd in range(GH):
                    k_ = gd_k[:, hd, b * P:(b + 1) * P]
                    mm = pe.matmul(ps[:, heads4[hd]], k_, k_, start=True, stop=True)
                mm.then_inc(dl("gram"), 1)
                decay_rows(pe, SETS + j, d, b, selL, (dl("E"), i + 1))

            def turn_T(i, n):
                d, b, j, q = set_of(i)
                TT = work[j][4]
                pe.wait_ge(dl(f"TT{j}"), LEVELS * q + n + 1)
                ps = grab(pe, SETS + j, dl(f"c{j}"), 10 * q + 2 * n + 1)
                for c in heads4:
                    mm = pe.transpose(ps[:, c], TT[:, c], ident)
                mm.then_inc(dl(f"x{j}"), 1)

            def product_x(i, n):
                d, b, j, q = set_of(i)
                L, A, X, Tm, TT = work[j]
                pe.wait_ge(dl(f"A{j}"), LEVELS * q + n + 1)
                pe.wait_ge(dl(f"c{j}"), 10 * q + 2 * n - 1)
                ps = grab(pe, SETS + j, dl(f"c{j}"), 10 * q + 2 * n)
                for c in heads4:
                    mm = pe.matmul(ps[:, c], A[:, c], Tm[:, c], start=True, stop=True)
                mm.then_inc(dl(f"x{j}"), 1)

            def product_y(i, n):
                d, b, j, q = set_of(i)
                L, A, X, Tm, TT = work[j]
                pe.wait_ge(dl(f"c{j}"), 10 * q + 2 * n)
                ps = grab(pe, j, dl(f"TT{j}"), LEVELS * q + n + 1)
                for c in heads4:
                    mm = pe.matmul(ps[:, c], X[:, c], TT[:, c], start=True, stop=True)
                mm.then_inc(dl(f"yt{j}"), 1)

            def right(i):
                d, b, j, q = set_of(i)
                TT, r_ = work[j][4], gd_rs[i % 2]
                pe.wait_ge(dl(f"TT{j}"), LEVELS * (q + 1))
                pe.wait_ge(dl("rhs"), i + 1)
                ps = grab(pe, 6, dl("w"), i + 1)
                for hd, c in enumerate(heads4):
                    mm = pe.matmul(ps[0:GDN_D, c], r_[:, 0, hd * GDN_D:(hd + 1) * GDN_D], TT[:, c], start=True, stop=True)
                mm.then_inc(dl("wps"), 1)
                ps = grab(pe, 7, dl("u"), i + 1)
                for hd, c in enumerate(heads4):
                    mm = pe.matmul(ps[:, hd * GDN_D:(hd + 1) * GDN_D], TT[:, c], r_[:, 1, hd * GDN_D:(hd + 1) * GDN_D],
                                   start=True, stop=True)
                mm.then_inc(dl("ups"), 1)

            for q in range(GROUPS + 1):
                three = range(SETS * q, SETS * (q + 1))
                if q < GROUPS:
                    for i in three:
                        gram(i)
                if q:
                    for i in three:
                        right(i - SETS)
                if q == GROUPS:
                    break
                for i in three:
                    turn_T(i, 0)
                for n in range(1, LEVELS):
                    for i in three:
                        product_x(i, n)
                    for i in three:
                        product_y(i, n)
                    if n < LEVELS - 1:
                        for i in three:
                            turn_T(i, n)
            for tb in range(TB):
                b = CB + tb
                ps = grab(pe, tb % 2, dl("AT"), 2 * tb + 2)
                for hd in range(GH):
                    mm = pe.matmul(ps[:, heads4[hd]], gd_k[:, hd, b * P:(b + 1) * P],
                                   gd_q[:, hd, tb * P:(tb + 1) * P], start=True, stop=True)
                mm.then_inc(dl("qk"), 1)
                for d in range(2):
                    decay_rows(pe, 2 + d, d, b, selA, (dl("E"), 2 * NBLK + 2 * tb + d + 1))

        def decay_act(act, i, d, b, dst):
            act.wait_ge(dl("E"), i + 1)
            for hd, c in enumerate(heads4):
                ins = act.activation(dst[:, c], dst[:, c], ACT.Exp, bias=gd_sc[:, 0, b, GH * d + hd:GH * d + hd + 1])
            ins.then_inc(dl("D"), 1)

        def inverse_act(act):
            def copy(i, n, x):
                d, b, j, q = set_of(i)
                count = 10 * q + 2 * n + (0 if x else 1)
                act.wait_ge(dl(f"x{j}"), count)
                act.activation(work[j][2 if x else 3], bank[SETS + j][:, :], ACT.Copy).then_inc(dl(f"c{j}"), 1)

            def take_right(i):
                d, b, j, q = set_of(i)
                act.wait_ge(dl("wps"), i + 1)
                act.activation(gd_wTs[d][0:GDN_D, :, b * P:(b + 1) * P], v4(bank[6][0:GDN_D, :]), ACT.Copy)\
                   .then_inc(dl("w"), 1)
                act.wait_ge(dl("ups"), i + 1)
                act.activation(gd_us[d][:, b], bank[7][:, 0:GW], ACT.Copy).then_inc(dl("u"), 1)

            for q in range(GROUPS + 1):
                three = range(SETS * q, SETS * (q + 1))
                if q < GROUPS:
                    for i in three:
                        d, b, j, _ = set_of(i)
                        decay_act(act, i, d, b, work[j][2])
                if q:
                    for i in three:
                        take_right(i - SETS)
                if q == GROUPS:
                    break
                for i in three:
                    copy(i, 0, False)
                for n in range(1, LEVELS):
                    for i in three:
                        copy(i, n, True)
                    if n < LEVELS - 1:
                        for i in three:
                            copy(i, n, False)
            for i in range(2 * TB):
                decay_act(act, 2 * NBLK + i, i % 2, CB + i // 2, work[i % 2][2])

        def inverse_dve(dve):
            tok = lambda kind, d, b: gd_sc[:, kind, b, GH * d:GH * d + GH].unsqueeze(2).broadcast_to((P, GH, GDN_D))
            dve.wait_ge(*after("gd_es", 3))

            def masked(i, b_, dst, m):
                dve.wait_ge(dl("g"), i + 1)
                dve.tensor_tensor(v4(dst), v4(bank[b_][:, :]), wide(m), ALU.add).then_inc(dl("E"), 1)

            def mask_level(i, n):
                d, b, j, q = set_of(i)
                L, A = work[j][0:2]
                if n == 1:
                    dve.wait_ge(dl(f"TT{j}"), LEVELS * q + 1)
                else:
                    dve.wait_ge(dl(f"x{j}"), 10 * q + 2 * n - 2)
                dve.tensor_tensor(v4(A), v4(L), wide(level(d, n)), ALU.mult).then_inc(dl(f"A{j}"), 1)

            def right_sides(i):
                d, b, j, q = set_of(i)
                if i >= 2:
                    dve.wait_ge(dl("ups"), i - 1)
                kT_, vT_ = (a[:, b].rearrange("p (h n) -> p h n", h=GH) for a in (gd_kT, gd_vT))
                dve.tensor_tensor(v4(gd_rs[i % 2][:, 0]), kT_, tok(3, d, b), ALU.mult)
                dve.tensor_tensor(v4(gd_rs[i % 2][:, 1]), vT_, tok(2, d, b), ALU.mult).then_inc(dl("rhs"), 1)

            for q in range(GROUPS + 1):
                three = range(SETS * q, SETS * (q + 1))
                if q:
                    right_sides(SETS * (q - 1))
                    right_sides(SETS * (q - 1) + 1)
                if q < GROUPS:
                    for i in three:
                        d, b, j, _ = set_of(i)
                        masked(i, SETS + j, work[j][2], gmask(d, True))
                if q:
                    right_sides(SETS * (q - 1) + 2)
                if q == GROUPS:
                    break
                for i in three:
                    d, b, j, _ = set_of(i)
                    L, A, X, Tm, TT = work[j]
                    dve.wait_ge(dl("gram"), i + 1)
                    dve.wait_ge(dl("D"), i + 1)
                    dve.tensor_tensor(L, bank[j][:, :], X, ALU.mult).then_inc(dl("LT"), 1)
                for i in three:
                    d, b, j, _ = set_of(i)
                    L, A, X, Tm, TT = work[j]
                    dve.wait_ge(dl("LT"), i + 1)
                    dve.tensor_tensor(v4(A), v4(L), wide(level(d, 0)), ALU.mult).then_inc(dl(f"A{j}"), 1)
                for i in three:
                    d, b, j, _ = set_of(i)
                    L, A, X, Tm, TT = work[j]
                    dve.wait_ge(dl(f"A{j}"), LEVELS * q + 1)
                    if q:
                        dve.wait_ge(dl("ups"), i - SETS + 1)
                    dve.tensor_tensor(v4(TT), wide(ident), v4(A), ALU.subtract).then_inc(dl(f"TT{j}"), 1)
                for i in three:
                    mask_level(i, 1)
                for n in range(1, LEVELS):
                    if n < LEVELS - 1:
                        for i in three:
                            mask_level(i, n + 1)
                    for i in three:
                        j = i % SETS
                        TT = work[j][4]
                        dve.wait_ge(dl(f"yt{j}"), 5 * q + n)
                        dve.tensor_tensor(TT, TT, bank[j][:, :], ALU.subtract).then_inc(dl(f"TT{j}"), 1)
            for i in range(2 * TB):
                tb, d = divmod(i, 2)
                E = work[d][2]
                if i >= 2:
                    dve.wait_ge(dl("AT"), i - 1)
                masked(2 * NBLK + i, 2 + d, E, gmask(d, False))
                dve.wait_ge(dl("qk"), tb + 1)
                dve.wait_ge(dl("D"), 2 * NBLK + i + 1)
                dve.tensor_tensor(gd_ATs[d][:, tb], bank[tb % 2][:, :], E, ALU.mult).then_inc(dl("AT"), 1)

        def gd_vn(d, n):
            return nb[:, 2 * d + n % 2, 0:GW]

        def place(d, n):
            c = steps(d)[n]
            r = CH * (c % 2)
            return c, r, slice(r, r + CH), c // 2

        def recur_pe(pe):
            pe.wait_ge(dl("AT"), 2 * TB)
            pe.wait_ge(dl("w"), 2 * NBLK)
            pe.wait_ge(dl("Sz"), 1)
            value_cols = [slice(hd * GDN_D, (hd + 1) * GDN_D) for hd in range(GH)]
            for n in range(NCH):
                for d in range(2):
                    c, r, rows_, b = place(d, n)
                    S = gd_Ss[d]
                    if n:
                        pe.wait_ge(dl(f"S{d}"), n)
                    ps = grab(pe, 4 * d, dl(f"v{d}"), n + 1)
                    for hd, v in enumerate(value_cols):
                        mm = pe.matmul(ps[rows_, v], gd_wTs[d][0:GDN_D, hd, c * CH:(c + 1) * CH], S[:, v], start=True, stop=True)
                    mm.then_inc(dl(f"wS{d}"), 1)
                    if n >= CCH:
                        ps = grab(pe, 4 * d + 2, dl(f"t{d}"), n - CCH + 1)
                        for hd, v in enumerate(value_cols):
                            mm = pe.matmul(ps[rows_, v], gd_q[0:GDN_D, hd, (c - CCH) * CH:(c - CCH + 1) * CH], S[:, v],
                                           start=True, stop=True)
                        mm.then_inc(dl(f"qS{d}"), 1)
                for d in range(2):
                    c, r, rows_, b = place(d, n)
                    pe.wait_ge(dl(f"v{d}"), n + 1)
                    pe.wait_ge(sem("keys_decayed"), 2 * n + d + 1)
                    ps = grab(pe, 4 * d + 1, dl(f"S{d}"), n + 1)
                    for v in value_cols:
                        mm = pe.matmul(ps[0:GDN_D, v], gd_rs[d][rows_, n % 2, v], gd_vn(d, n)[rows_, v], start=True, stop=True)
                    mm.then_inc(dl(f"kv{d}"), 1)
                    if n >= CCH:
                        ps = grab(pe, 4 * d + 3, dl(f"o{d}"), n - CCH + 1)
                        for hd, v in enumerate(value_cols):
                            mm = pe.matmul(ps[rows_, v], gd_ATs[d][rows_, b - CB, hd * P + r:hd * P + r + CH],
                                           gd_vn(d, n)[rows_, v], start=True, stop=True)
                        mm.then_inc(dl(f"Av{d}"), 1)

        def recur_act(act):
            for n in range(CCH, NCH):
                for d in range(2):
                    c, r, rows_, b = place(d, n)
                    act.wait_ge(dl(f"qS{d}"), n - CCH + 1)
                    if n > CCH:
                        act.wait_ge(dl(f"o{d}"), n - CCH)
                    for hd in range(GH):
                        v = slice(hd * GDN_D, (hd + 1) * GDN_D)
                        ins = act.activation(nb[rows_, 4 + d, v], bank[4 * d + 2][rows_, v], ACT.Copy,
                                             scale=gd_sc[rows_, 1, b, GH * d + hd:GH * d + hd + 1])
                    ins.then_inc(dl(f"t{d}"), 1)

        def recur_pool(pool):
            pool.wait_ge(dl("ups"), 2 * NBLK)
            for n in range(NCH):
                for d in range(2):
                    c, r, rows_, b = place(d, n)
                    if n >= 2:
                        pool.wait_ge(dl(f"kv{d}"), n - 1)
                    kT_ = gd_kT[rows_, b].rearrange("p (h n) -> p h n", h=GH)
                    e = gd_sc[rows_, 4, b, GH * d:GH * d + GH].unsqueeze(2).broadcast_to((CH, GH, GDN_D))
                    pool.tensor_tensor(v4(gd_rs[d][rows_, n % 2]), kT_, e, ALU.mult).then_inc(sem("keys_decayed"), 1)

        def recur_dve(dve):
            dve.memset(gd_Ss[0], 0.0)
            dve.wait_ge(dl("u"), 2 * NBLK)
            dve.memset(gd_Ss[1], 0.0).then_inc(dl("Sz"), 1)
            dve.wait_ge(dl("Sz"), 1)
            glast = [a.rearrange("p (r c) -> p r c", r=GH) for a in (stat[:, 0:48], vecs[:, 160:208])]
            for n in range(NCH):
                k = n - CCH
                for d in range(2):
                    c, r, rows_, b = place(d, n)
                    dve.wait_ge(dl(f"wS{d}"), n + 1)
                    if k >= 2:
                        dve.wait_ge(dl(f"Av{d}"), k - 1)
                    dve.tensor_tensor(gd_vn(d, n)[rows_], gd_us[d][rows_, b], bank[4 * d][rows_, 0:GW], ALU.subtract)\
                       .then_inc(dl(f"v{d}"), 1)
                for d in range(2):
                    c, r, rows_, b = place(d, n)
                    S = gd_Ss[d]
                    if k >= 0:
                        dve.wait_ge(dl(f"qS{d}"), k + 1)
                    link(dve, dve.tensor_tensor(v4(S), v4(S), glast[d][0:GDN_D, :, c:c + 1].broadcast_to((GDN_D, GH, GDN_D)),
                                                ALU.mult))
                    dve.wait_ge(dl(f"kv{d}"), n + 1)
                    dve.tensor_tensor(S, S, bank[4 * d + 1][0:GDN_D, 0:GW], ALU.add).then_inc(dl(f"S{d}"), 1)
                for d in range(2):
                    if k < 0:
                        dve.wait_ge(dl(f"S{d}"), n + 1)
                        continue
                    c, r, rows_, b = place(d, n)
                    o, t = gd_o[rows_, b - CB], nb[rows_, 4 + d, 0:GW]
                    dve.wait_ge(dl(f"t{d}"), k + 1)
                    if k >= (NCH - CCH) // 2:
                        dve.wait_ge(dl(f"o{1 - d}"), NCH - CCH - k)
                        link(dve, dve.tensor_tensor(t, o, t, ALU.add))
                    dve.wait_ge(dl(f"Av{d}"), k + 1)
                    dve.tensor_tensor(o, t, bank[4 * d + 3][rows_, 0:GW], ALU.add).then_inc(dl(f"o{d}"), 1)
                    dve.wait_ge(dl(f"S{d}"), n + 1)
            for d in range(2):
                dve.wait_ge(dl(f"o{d}"), NCH - CCH)

        gd_res = part(11776, TB, GW)

        def close_pe(pe, st, name, kt, x, ready, half=None):
            s = "" if half is None else str(half)
            fm_linear(pe, name, KD, kt, x, f"{st}_ps{s}", st + "_h", ready=ready, read0=KD * (half or 0))
            if half != 0:
                for k in range(KD):
                    sum_squares(pe, st + "n", k)

        def close_act(act, st, h0=0):
            for k in range(KD):
                squares(act, st + "n", h, st + "_h", k, h0)
            rstd_sqrt(act, st + "n")

        def close_dve(dve, st, m, half=None):
            s = "" if half is None else str(half)
            for f in range(KD):
                dve.wait_ge(*after(f"{st}_ps{s}", f + 1))
                dve.scalar_tensor_tensor(out=h[:, f], in0=bank[f % 4][:, :], scalar=mod_lat[:, m, f:f + 1], in1=h[:, f],
                                         op0=ALU.mult, op1=ALU.add).then_inc(sem(st + "_h"), 1)
            dve.wait_ge(*after(st + "_h", KD * (1 + (half or 0))))
            if half != 0:
                rstd_recip(dve, st + "n")

        ff2_hi, ff2_lo = part(0, KH2, T), part(KH2 * T, KH2, T)
        mlp_x = (xn, part(2 * KH2 * T, KD, T))
        out2_x = (xn, mix)

        def mlp_pe(pe):
            for s in range(2):
                fm_linear(pe, f"mlp1_{s}", KH2, KD, mlp_x, f"mlp_up{s}", "mlp_relu", read0=KH2 * s,
                          ready=None if s else ("mlp_xl", 0))
                close_pe(pe, "mlp", f"mlp2_{s}", KH2, (ff2_hi, ff2_lo), ("mlp_sl", KH2 * s), s)

        def mlp_act(act):
            hi, lo = mlp_x
            for k in range(KD):
                act.wait_ge(*after("mlp_a", k + 1))
                act.activation(rounded(hi[:, k]), lo[:, k], ACT.Identity, bias=mod_lat[:, 3, k:k + 1])\
                   .then_inc(sem("mlp_xh"), 1)
            for s in range(2):
                for f in range(KH2):
                    act.wait_ge(*after(f"mlp_up{s}", f + 1))
                    act.activation(ff2_lo[:, f], bank[f % 4][:, :], ACT.Relu).then_inc(sem("mlp_relu"), 1)
                    act.wait_ge(*after("mlp_relu", KH2 * s + f + 1))
                    act.activation(rounded(ff2_hi[:, f]), ff2_lo[:, f], ACT.Square).then_inc(sem("mlp_sh"), 1)
            close_act(act, "mlp", KD)

        def mlp_dve(dve):
            hi, lo = mlp_x
            for k in range(KD + 1):
                if k < KD:
                    dve.scalar_tensor_tensor(out=lo[:, k], in0=h[:, k], scalar=column(G2, k), in1=rstd,
                                             op0=ALU.mult, op1=ALU.mult).then_inc(sem("mlp_a"), 1)
                if k:
                    dve.wait_ge(*after("mlp_xh", k))
                    dve.scalar_tensor_tensor(out=rounded(lo[:, k - 1]), in0=lo[:, k - 1],
                                             scalar=mod_lat[:, 3, k - 1:k], in1=value(hi[:, k - 1]),
                                             op0=ALU.add, op1=ALU.subtract).then_inc(sem("mlp_xl"), 1)
            for s in range(2):
                for f in range(KH2 + 1):
                    if f < KH2:
                        dve.wait_ge(*after("mlp_sh", KH2 * s + f + 1))
                        dve.tensor_tensor(ff2_lo[:, f], ff2_lo[:, f], ff2_lo[:, f], ALU.mult).then_inc(sem("mlp_sq"), 1)
                    if f:
                        split_dve(dve, ff2_lo, ff2_hi, ff2_lo, f - 1, after("mlp_sq", KH2 * s + f), "mlp_sl")
                close_dve(dve, "mlp", 5, s)
            for k in range(KD):
                dve.scalar_tensor_tensor(out=mix[:, k], in0=h[:, k], scalar=gain("nf", k), in1=rstd,
                                         op0=ALU.mult, op1=ALU.mult).then_inc(sem("y"), 1)

        def block2_pe(pe):
            filter_pe(pe)
            mod_pe(pe)
            hyena_pe(pe)
            gates_pe(pe)
            gla_pe(pe)
            heads_flip(pe, "gla", gl_res)
            delta_in_pe(pe)
            inverse_pe(pe)
            recur_pe(pe)
            heads_flip(pe, "gdh", gd_res)
            close_pe(pe, "out2", "out2", KD, out2_x, ("out2_xl", 0))
            mlp_pe(pe)

        def block2_act(act):
            filter_act(act)
            mod_act(act)
            act.wait_ge(*after("x2_lat", KD))
            act.activation(column(vecs, 136), gain("a_log"), ACT.Exp).then_inc(sem("ea0"), 1)
            act.wait_ge(*after("ea0", 1))
            act.activation(column(vecs, 136), column(vecs, 136), ACT.Copy, scale=-1.0).then_inc(sem("ea"), 1)
            hyena_act(act)
            gates_act(act)
            gla_act(act)
            heads_act(act, "gla", 2)
            delta_in_act(act)
            inverse_act(act)
            recur_act(act)
            heads_act(act, "gdh", 5)
            act.wait_ge(*after("gdh_cat", 3))
            for k in range(KD):
                split_act(act, mix, xn, k, after("hy_y", 4), "out2_xh")
            close_act(act, "out2")
            mlp_act(act)

        def block2_dve(dve):
            filter_dve(dve)
            mod_dve(dve)
            hyena_dve(dve)
            gates_dve(dve)
            gla_dve(dve)
            heads_dve(dve, "gla", gl_o, gate, "gla_gate", gl_res, "gla_ng")
            delta_in_dve(dve)
            inverse_dve(dve)
            recur_dve(dve)
            heads_dve(dve, "gdh", gd_o, gd_gate, "gd_gate", gd_res, "gdn_ng")
            for k in range(KD):
                split_dve(dve, mix, xn, mix, k, after("out2_xh", k + 1), "out2_xl")
            dve.wait_ge(sem("h_back"), 16)
            close_dve(dve, "out2", 2)
            mlp_dve(dve)

        def block2_pool(pool):
            def load(dst, name, at, n, done):
                pool.dma_start(dst, consts[:, CO[name] + at:CO[name] + at + n]).then_inc(done, 16)
            pool.wait_ge(*after("ffn1_ps1", KD))
            pool.wait_ge(sem("mod_used"), MOD_UNITS)
            load(big[:, 8192:8192 + 5 * T], "filt", 0, 5 * T, sem("filt_in"))
            pool.dma_start(fw, filt[:, 0:1152]).then_inc(sem("filt_in"), 16)
            load(big[:, 0:8192], "dft", 0, 8192, sem("dft_in"))
            pool.wait_ge(*after("ffn1_h", KD))
            pool.dma_start(h_store[:, :], h.rearrange("p k t -> p (k t)")).then_inc(sem("h_out"), 16)
            pool.dma_start(mix[:, 0:KD * CTX // T], ctx_x[:, :].rearrange("p (k t) -> p k t", t=T)).then_inc(sem("cx_in"), 16)
            load(cst[:, 0:2 * P + TA + 3], "gla", 0, 2 * P + TA + 3, sem("gla_in"))
            split_units(pool, UNITS["hy"], UNITS["gl_q"])
            pool.wait_ge(*after("conv", 4))
            pool.wait_ge(*after("hy_y", 4))
            pool.dma_start(gl_w2, filt[:, 1152:1152 + 2 * P]).then_inc(sem("gla_in"), 16)
            split_units(pool, UNITS["gl_q"], UNITS["gd_k"])
            pool.wait_ge(*after("gla_normed", 1))
            pool.wait_ge(*after("gla_cat", 3))
            load(cst[:, 0:2048], "gdn_m", 0, 2048, sem("gdn_in"))
            load(big[:, 9728:9728 + 2048], "gdn_s", 0, 2048, sem("gdn_in"))


        block = ctx.enter_context(nc.Block())

        @block.tensor
        def _(pe):
            mixa_pe(pe)
            ffn_pe(pe, 0)
            mixb_pe(pe)
            ffn_pe(pe, 1)
            block2_pe(pe)

        @block.sync
        def _(sp):
            def const(dst, name, n, done):
                sp.dma_start(dst, consts[:, CO[name]:CO[name] + n]).then_inc(done, 16)
            for k in range(KD):
                sp.dma_start(h[:, k], x[:, k * T:(k + 1) * T]).then_inc(h_in[k], 16)
                if k == 0:
                    sp.dma_start(small[:, :], smalls[:, :]).then_inc(small_in, 16)
                    const(base[:, :], "base", 3 * P, small_in)
            for u in range(n_units):
                if u == RING:
                    const(cst[:, 0:2560], "mix_a", 2560, cst_in)
                for n in mod_due.get(u, ()):
                    mod_load(sp, n)
                if u == UNITS["up0_0"] + RING + 2:
                    sp.wait_ge(*after("a_ps", 1))
                    const(cst[:, 0:2560], "mix_b", 2560, cst_in)
                if u >= RING:
                    sp.wait_ge(part_ready, u - RING + 1)
                sp.dma_start(ring[:, u % RING], weights[u]).then_inc(ring_full[u % RING], 16)
            for k in range(KD):
                sp.wait_ge(*after("y", k + 1))
                sp.dma_start(out[:, k * T:(k + 1) * T], mix[:, k]).then_inc(sem("stored"), 16)
            sp.wait_ge(*after("stored", 16 * KD))

        @block.scalar
        def _(act):
            mixa_act(act)
            ffn_act(act, 0)
            mixb_act(act)
            ffn_act(act, 1)
            block2_act(act)

        @block.vector
        def _(dve):
            mixa_dve(dve)
            ffn_dve(dve, 0, "g03")
            mixb_dve(dve)
            ffn_dve(dve, 1, "g13")
            block2_dve(dve)

        @block.gpsimd
        def _(pool):
            split_units(pool, 0, UNITS["hy"])
            block2_pool(pool)
            split_units(pool, UNITS["gd_k"], UNITS["out2"])
            pool.wait_ge(*after("gd_gps", TB))
            pool.wait_ge(sem("h_out"), 16)
            pool.dma_start(h.rearrange("p k t -> p (k t)"), h_store[:, :]).then_inc(sem("h_back"), 16)
            recur_pool(pool)
            for d in range(2):
                pool.wait_ge(dl(f"S{d}"), NCH)
            split_units(pool, UNITS["out2"], n_units)


def kernel(**inputs):
    import concourse.bacc as bacc
    from concourse.bass_utils import run_bass_kernel_spmd

    i = {k: np.asarray(v) for k, v in inputs.items()}
    arrays = {
        "x": np.ascontiguousarray(i["x"][0].T.reshape(KD, P, T).transpose(1, 0, 2).reshape(P, KD * T)),
        "ctx_x": np.ascontiguousarray(i["ctx_2"][0].T.reshape(KD, P, CTX).transpose(1, 0, 2).reshape(P, KD * CTX)),
        "filt": filter_weights(i),
        "mod_w": mod_units(i["w_mod_2"][0]),
        "weights": np.concatenate([u for _, u in weight_list(i)]),
        "smalls": np.concatenate([a for _, a in small_list(i)], axis=1),
        "consts": np.concatenate([a for _, a in const_list()], axis=1),
    }
    nc = bacc.Bacc("TRN2", target_bir_lowering=False, num_devices=1)
    aps = {n: nc.dram_tensor(n, a.shape, F32, kind="ExternalInput").ap() for n, a in arrays.items()}
    out = nc.dram_tensor("out", (P, KD * T), F32, kind="ExternalOutput").ap()
    build(nc, out=out, **aps)
    r = run_bass_kernel_spmd(nc, [arrays], core_ids=[0])
    y = r.results[0]["out"]
    return y.reshape(P, KD, T).transpose(2, 1, 0).reshape(1, T, D)
```
